# Optimizing a Trainium2 kernel written in Bass

```python
import jax, jax.numpy as jnp
from jax import lax
import numpy as np
import math
import jax
import jax.numpy as jnp

D_MODEL = 1024
BATCH = 1
SEQ = 256
DEPTH = 2

N_A_LAYERS = DEPTH // 2
N_B_LAYERS = DEPTH - N_A_LAYERS
M_HEADS = 4
M_DV = D_MODEL // M_HEADS
M_DK = M_DV // 2
M_CHUNK = 64
GATE_CAP = 15.0
M_QK_W = M_HEADS * M_DK
M_V_W = M_HEADS * M_DV
M_IN_COLS = 2 * M_QK_W + 2 * M_V_W + 2 * M_HEADS
M_SPLITS = [M_QK_W, 2 * M_QK_W, 2 * M_QK_W + M_V_W, 2 * M_QK_W + 2 * M_V_W, 2 * M_QK_W + 2 * M_V_W + M_HEADS]
A_HEAD_DIM = 64
A_Q_HEADS = D_MODEL // A_HEAD_DIM
A_KV_HEADS = 4
A_GROUP = A_Q_HEADS // A_KV_HEADS
WINDOW = 128
ROPE_DIM = A_HEAD_DIM // 4
ROPE_THETA = 500000.0
D_FF = 4 * D_MODEL
PLE_DIM = 256
LN_EPS = 1e-5
DEEPNORM_ALPHA = (2 * DEPTH) ** 0.25
DEEPNORM_BETA = (8 * DEPTH) ** -0.25


def layer_norm(x, g, b):
    xf = x.astype(jnp.float32)
    mu = jnp.mean(xf, axis=-1, keepdims=True)
    var = jnp.mean(jnp.square(xf - mu), axis=-1, keepdims=True)
    return ((xf - mu) * lax.rsqrt(var + LN_EPS) * g + b).astype(x.dtype)

def partial_rope(t, pos):
    half = ROPE_DIM // 2
    inv_freq = jnp.power(ROPE_THETA, -jnp.arange(half, dtype=jnp.float32) * (2.0 / ROPE_DIM))
    ang = pos.astype(jnp.float32)[..., None] * inv_freq
    cos = jnp.cos(ang)[:, :, None, :]
    sin = jnp.sin(ang)[:, :, None, :]
    tr = t[..., :ROPE_DIM].astype(jnp.float32)
    t1, t2 = tr[..., :half], tr[..., half:]
    rot = jnp.concatenate([t1 * cos - t2 * sin, t2 * cos + t1 * sin], axis=-1).astype(t.dtype)
    return jnp.concatenate([rot, t[..., ROPE_DIM:]], axis=-1)

def soft_cap(g):
    return GATE_CAP * jnp.tanh(g / GATE_CAP)

def to_chunks(t, nc):
    t = t.reshape(t.shape[0], nc, M_CHUNK, *t.shape[2:])
    return jnp.moveaxis(t, (1, 3), (0, 2))

def mlstm_chunkwise(q, k, v, ig, lf):
    B, S, H, DK = q.shape
    DV = v.shape[-1]
    nc = S // M_CHUNK
    xs = tuple(to_chunks(t, nc) for t in (q, k, v, ig, lf))
    causal = jnp.tril(jnp.ones((M_CHUNK, M_CHUNK), dtype=bool))
    init = (jnp.zeros((B, H, DK, DV), jnp.float32),
            jnp.zeros((B, H, DK), jnp.float32),
            jnp.zeros((B, H), jnp.float32))

    def step(carry, chunk):
        C, n, m = carry
        qc, kc, vc, igc, lfc = chunk
        b = jnp.cumsum(lfc, axis=-1)
        log_d = b[..., :, None] - b[..., None, :] + igc[..., None, :]
        log_d = jnp.where(causal, log_d, -jnp.inf)
        log_inter = b + m[..., None]
        m_t = jnp.maximum(jnp.max(log_d, axis=-1), log_inter)
        d = jnp.exp(log_d - m_t[..., None])
        inter = jnp.exp(log_inter - m_t)
        s = jnp.einsum('bhtk,bhsk->bhts', qc, kc) * d
        num = jnp.einsum('bhts,bhsv->bhtv', s, vc) + inter[..., None] * jnp.einsum('bhtk,bhkv->bhtv', qc, C)
        den = jnp.sum(s, axis=-1) + inter * jnp.einsum('bhtk,bhk->bht', qc, n)
        h = num / jnp.maximum(jnp.abs(den), jnp.exp(-m_t))[..., None]
        b_last = b[..., -1]
        a = b_last[..., None] - b + igc
        m_new = jnp.maximum(b_last + m, jnp.max(a, axis=-1))
        w = jnp.exp(a - m_new[..., None])
        decay = jnp.exp(b_last + m - m_new)
        C_new = decay[..., None, None] * C + jnp.einsum('bhs,bhsk,bhsv->bhkv', w, kc, vc)
        n_new = decay[..., None] * n + jnp.einsum('bhs,bhsk->bhk', w, kc)
        return (C_new, n_new, m_new), h

    _, h = lax.scan(step, init, xs)
    return jnp.moveaxis(h, (0, 2), (1, 3)).reshape(B, S, H, DV)

def mlstm_mixer(x, w_in, b_ig, b_fg, head_g, w_out):
    B, S, _ = x.shape
    proj = x @ w_in
    q, k, v, o, ig, fg = jnp.split(proj, M_SPLITS, axis=-1)
    q = q.reshape(B, S, M_HEADS, M_DK).astype(jnp.float32) * (M_DK ** -0.5)
    k = k.reshape(B, S, M_HEADS, M_DK).astype(jnp.float32)
    v = v.reshape(B, S, M_HEADS, M_DV).astype(jnp.float32)
    log_i = soft_cap(ig.astype(jnp.float32) + b_ig)
    log_f = jax.nn.log_sigmoid(soft_cap(fg.astype(jnp.float32) + b_fg))
    h = mlstm_chunkwise(q, k, v, log_i, log_f)
    mu = jnp.mean(h, axis=-1, keepdims=True)
    var = jnp.mean(jnp.square(h - mu), axis=-1, keepdims=True)
    h = (h - mu) * lax.rsqrt(var + LN_EPS) * head_g.reshape(M_HEADS, M_DV)
    h = h.reshape(B, S, D_MODEL).astype(x.dtype)
    return (jax.nn.sigmoid(o) * h) @ w_out

def shared_kv(x, pos, kv_w, kv_b):
    B, S, _ = x.shape
    kv = x @ kv_w + kv_b
    k, v = jnp.split(kv, 2, axis=-1)
    k = partial_rope(k.reshape(B, S, A_KV_HEADS, A_HEAD_DIM), pos)
    v = v.reshape(B, S, A_KV_HEADS, A_HEAD_DIM)
    return k, v

def banded(t, nb):
    t = t.reshape(t.shape[0], nb, WINDOW, A_KV_HEADS, A_HEAD_DIM)
    prev = jnp.pad(t, ((0, 0), (1, 0), (0, 0), (0, 0), (0, 0)))[:, :-1]
    return jnp.concatenate([prev, t], axis=2)

def swa_sink_attention(x, pos, k_sh, v_sh, w_q, b_q, sinks, w_o, b_o):
    B, S, _ = x.shape
    nb = S // WINDOW
    q = partial_rope((x @ w_q + b_q).reshape(B, S, A_Q_HEADS, A_HEAD_DIM), pos)
    q = q.reshape(B, nb, WINDOW, A_KV_HEADS, A_GROUP, A_HEAD_DIM)
    kb, vb = banded(k_sh, nb), banded(v_sh, nb)
    scores = jnp.einsum('bnqkgd,bnskd->bnkgqs', q, kb).astype(jnp.float32) * (A_HEAD_DIM ** -0.5)
    qi = jnp.arange(WINDOW)[:, None]
    si = jnp.arange(2 * WINDOW)[None, :]
    diff = qi + WINDOW - si
    band = (diff >= 0) & (diff < WINDOW)
    blk = jnp.arange(nb)[:, None, None]
    valid = band[None] & (blk * WINDOW - WINDOW + si[None] >= 0)
    scores = jnp.where(valid[None, :, None, None], scores, -jnp.inf)
    sink = sinks.astype(jnp.float32).reshape(A_KV_HEADS, A_GROUP)[None, None, :, :, None]
    m = jnp.maximum(jnp.max(scores, axis=-1), sink)
    e = jnp.exp(scores - m[..., None])
    probs = e / (jnp.sum(e, axis=-1) + jnp.exp(sink - m))[..., None]
    out = jnp.einsum('bnkgqs,bnskd->bnqkgd', probs.astype(x.dtype), vb).reshape(B, S, D_MODEL)
    return out @ w_o + b_o

def squared_relu_mlp(x, w_up, w_down):
    return jnp.square(jax.nn.relu(x @ w_up)) @ w_down

def first_inputs(seed: int = 0) -> dict:
    key = jax.random.key(seed)
    ks = jax.random.split(key, 24)
    f32 = jnp.float32
    nrm = lambda k, shape, scale: jax.random.normal(k, shape, f32) * scale
    x = jax.random.normal(ks[0], (BATCH, SEQ, D_MODEL), f32)
    p = jax.random.normal(ks[1], (DEPTH, BATCH, SEQ, PLE_DIM), f32)
    start = jax.random.randint(ks[2], (BATCH, 1), 0, 1024, dtype=jnp.int32)
    positions = (start + jnp.arange(SEQ, dtype=jnp.int32)[None, :]).astype(jnp.int32)
    a_w_in = nrm(ks[3], (N_A_LAYERS, D_MODEL, M_IN_COLS), D_MODEL ** -0.5)
    a_b_igate = nrm(ks[4], (N_A_LAYERS, M_HEADS), 0.1)
    a_b_fgate = jnp.linspace(3.0, 6.0, M_HEADS, dtype=f32)[None, :] + nrm(ks[5], (N_A_LAYERS, M_HEADS), 0.1)
    a_head_norm_g = 1.0 + nrm(ks[6], (N_A_LAYERS, D_MODEL), 0.02)
    a_w_out = nrm(ks[7], (N_A_LAYERS, D_MODEL, D_MODEL), D_MODEL ** -0.5 * DEEPNORM_BETA)
    kv_w = nrm(ks[8], (D_MODEL, 2 * A_KV_HEADS * A_HEAD_DIM), D_MODEL ** -0.5)
    kv_b = nrm(ks[9], (2 * A_KV_HEADS * A_HEAD_DIM,), 0.02)
    b_w_q = nrm(ks[10], (N_B_LAYERS, D_MODEL, A_Q_HEADS * A_HEAD_DIM), D_MODEL ** -0.5)
    b_b_q = nrm(ks[11], (N_B_LAYERS, A_Q_HEADS * A_HEAD_DIM), 0.02)
    b_sinks = nrm(ks[12], (N_B_LAYERS, A_Q_HEADS), 0.5)
    b_w_o = nrm(ks[13], (N_B_LAYERS, A_Q_HEADS * A_HEAD_DIM, D_MODEL), D_MODEL ** -0.5 * DEEPNORM_BETA)
    b_b_o = nrm(ks[14], (N_B_LAYERS, D_MODEL), 0.02)
    mix_ln_g = 1.0 + nrm(ks[15], (DEPTH, D_MODEL), 0.02)
    mix_ln_b = nrm(ks[16], (DEPTH, D_MODEL), 0.02)
    mlp_w_up = nrm(ks[17], (DEPTH, D_MODEL, D_FF), D_MODEL ** -0.5)
    mlp_w_down = nrm(ks[18], (DEPTH, D_FF, D_MODEL), D_FF ** -0.5 * DEEPNORM_BETA)
    mlp_ln_g = 1.0 + nrm(ks[19], (DEPTH, D_MODEL), 0.02)
    mlp_ln_b = nrm(ks[20], (DEPTH, D_MODEL), 0.02)
    ple_w_gate = nrm(ks[21], (DEPTH, D_MODEL, D_MODEL), D_MODEL ** -0.5)
    ple_b_gate = nrm(ks[22], (DEPTH, D_MODEL), 0.02)
    ple_w_proj = nrm(ks[23], (DEPTH, PLE_DIM, D_MODEL), PLE_DIM ** -0.5 * DEEPNORM_BETA)
    return {"x": x, "p": p, "positions": positions,
            "a_w_in": a_w_in, "a_b_igate": a_b_igate, "a_b_fgate": a_b_fgate,
            "a_head_norm_g": a_head_norm_g, "a_w_out": a_w_out,
            "kv_w": kv_w, "kv_b": kv_b,
            "b_w_q": b_w_q, "b_b_q": b_b_q, "b_sinks": b_sinks, "b_w_o": b_w_o, "b_b_o": b_b_o,
            "mix_ln_g": mix_ln_g, "mix_ln_b": mix_ln_b,
            "mlp_w_up": mlp_w_up, "mlp_w_down": mlp_w_down, "mlp_ln_g": mlp_ln_g, "mlp_ln_b": mlp_ln_b,
            "ple_w_gate": ple_w_gate, "ple_b_gate": ple_b_gate, "ple_w_proj": ple_w_proj}

def first_block(x, p, positions, a_w_in, a_b_igate, a_b_fgate, a_head_norm_g, a_w_out,
              kv_w, kv_b, b_w_q, b_b_q, b_sinks, b_w_o, b_b_o,
              mix_ln_g, mix_ln_b, mlp_w_up, mlp_w_down, mlp_ln_g, mlp_ln_b,
              ple_w_gate, ple_b_gate, ple_w_proj):
    k_sh, v_sh = None, None
    for i in range(DEPTH):
        if i < N_A_LAYERS:
            mix = mlstm_mixer(x, a_w_in[i], a_b_igate[i], a_b_fgate[i], a_head_norm_g[i], a_w_out[i])
        else:
            if i == N_A_LAYERS:
                k_sh, v_sh = shared_kv(x, positions, kv_w, kv_b)
            j = i - N_A_LAYERS
            mix = swa_sink_attention(x, positions, k_sh, v_sh, b_w_q[j], b_b_q[j], b_sinks[j], b_w_o[j], b_b_o[j])
        x = layer_norm(DEEPNORM_ALPHA * x + mix, mix_ln_g[i], mix_ln_b[i])
        x = layer_norm(DEEPNORM_ALPHA * x + squared_relu_mlp(x, mlp_w_up[i], mlp_w_down[i]), mlp_ln_g[i], mlp_ln_b[i])
        x = x + jax.nn.sigmoid(x @ ple_w_gate[i] + ple_b_gate[i]) * (p[i] @ ple_w_proj[i])
    return x


DEPTH_2 = 1

HEAD_DIM = 64
N_HEADS_NSA = 8
N_KV_NSA = 2
GROUP_NSA = N_HEADS_NSA // N_KV_NSA
N_HEADS_FOX = 8
MIX_WIDTH = (N_HEADS_NSA + N_HEADS_FOX) * HEAD_DIM
NSA_Q_W = N_HEADS_NSA * HEAD_DIM
NSA_KV_W = N_KV_NSA * HEAD_DIM
FOX_W = N_HEADS_FOX * HEAD_DIM
PROJ_SIZES = (NSA_Q_W, NSA_KV_W, NSA_KV_W, NSA_KV_W, NSA_KV_W, NSA_KV_W, NSA_KV_W,
              3 * N_HEADS_NSA, FOX_W, FOX_W, FOX_W, N_HEADS_FOX)
IN_WIDTH = sum(PROJ_SIZES)
D_FF_2 = 2816
D_PLE = 256
ROT_DIM = HEAD_DIM // 4
CMP_BLOCK = 32
CMP_STRIDE = 16
CMP_HIDDEN = 256
SEL_BLOCK = 64
SEL_TOPK = 16
WINDOW_2 = 512
NSA_Q_BLOCK = 32
FOX_Q_BLOCK = 128
FORCED_SCORE = 1e6
EPS = 1e-6
NEG = -1e30


def rmsnorm(x, g):
    xf = x.astype(jnp.float32)
    y = xf * lax.rsqrt(jnp.mean(xf * xf, axis=-1, keepdims=True) + EPS)
    return (y * g.astype(jnp.float32)).astype(x.dtype)

def swiglu(x, wg, wu, wd):
    return (jax.nn.silu(x @ wg) * (x @ wu)) @ wd

def split_heads(t, n):
    b, s, _ = t.shape
    return t.reshape(b, s, n, HEAD_DIM).transpose(0, 2, 1, 3)

def merge_heads(t):
    b, n, s, d = t.shape
    return t.transpose(0, 2, 1, 3).reshape(b, s, n * d)

def rope_tables(seq):
    pos = jnp.arange(seq, dtype=jnp.float32)
    inv = ROPE_THETA ** (-jnp.arange(0, ROT_DIM, 2, dtype=jnp.float32) / ROT_DIM)
    ang = pos[:, None] * inv[None, :]
    return jnp.cos(ang), jnp.sin(ang)

def partial_rope_2(x, cos, sin):
    half = ROT_DIM // 2
    xf = x.astype(jnp.float32)
    x1, x2, rest = xf[..., :half], xf[..., half:ROT_DIM], xf[..., ROT_DIM:]
    out = jnp.concatenate([x1 * cos - x2 * sin, x2 * cos + x1 * sin, rest], axis=-1)
    return out.astype(x.dtype)

def masked_softmax(s, mask):
    return jax.nn.softmax(jnp.where(mask, s.astype(jnp.float32), NEG), axis=-1)

def compress_blocks(tok, pos_emb, w1, w2):
    s = tok.shape[2]
    n_cmp = (s - CMP_BLOCK) // CMP_STRIDE + 1
    idx = np.arange(n_cmp)[:, None] * CMP_STRIDE + np.arange(CMP_BLOCK)[None, :]
    blk = tok[:, :, idx, :] + pos_emb
    blk = blk.reshape(blk.shape[0], blk.shape[1], n_cmp, CMP_BLOCK * HEAD_DIM)
    return jax.nn.silu(blk @ w1) @ w2

def nsa_attention(q, k_cmp, v_cmp, k_slc, v_slc, k_win, v_win, gates):
    b, h, s, d = q.shape
    qg = q.reshape(b, N_KV_NSA, GROUP_NSA, s, d)
    gg_all = gates.reshape(b, N_KV_NSA, GROUP_NSA, s, 3)
    n_cmp = k_cmp.shape[2]
    n_sel = s // SEL_BLOCK
    top = min(SEL_TOPK, n_sel)
    cmp_start = np.arange(n_cmp) * CMP_STRIDE
    cmp_end = jnp.asarray(cmp_start + CMP_BLOCK - 1)
    sel_start = np.arange(n_sel) * SEL_BLOCK
    overlap = jnp.asarray(((cmp_start[:, None] <= sel_start[None, :] + SEL_BLOCK - 1)
                           & (cmp_start[:, None] + CMP_BLOCK - 1 >= sel_start[None, :])).astype(np.float32))
    ks_blocks = k_slc.reshape(b, N_KV_NSA, n_sel, SEL_BLOCK, d)
    vs_blocks = v_slc.reshape(b, N_KV_NSA, n_sel, SEL_BLOCK, d)
    pad = ((0, 0), (0, 0), (WINDOW_2, 0), (0, 0))
    kw_pad = jnp.pad(k_win, pad)
    vw_pad = jnp.pad(v_win, pad)
    bi = np.arange(b)[:, None, None, None]
    hi = np.arange(N_KV_NSA)[None, :, None, None]
    blk_j = jnp.arange(n_sel)
    scale = HEAD_DIM ** -0.5
    qn = NSA_Q_BLOCK

    def block(qb):
        t0 = qb * qn
        tpos = t0 + jnp.arange(qn)
        qq = lax.dynamic_slice_in_dim(qg, t0, qn, axis=3)
        gg = lax.dynamic_slice_in_dim(gg_all, t0, qn, axis=3)
        m_c = cmp_end[None, :] <= tpos[:, None]
        s_c = jnp.einsum('bkgqd,bknd->bkgqn', qq, k_cmp) * scale
        p_c = masked_softmax(s_c, m_c) * m_c
        o_c = jnp.einsum('bkgqn,bknd->bkgqd', p_c.astype(v_cmp.dtype), v_cmp)
        imp = jnp.einsum('bkgqn,nj->bkqj', p_c, overlap)
        cur = tpos // SEL_BLOCK
        valid = blk_j[None, :] <= cur[:, None]
        forced = (blk_j[None, :] == 0) | (blk_j[None, :] == cur[:, None]) | (blk_j[None, :] == cur[:, None] - 1)
        imp = jnp.where(valid, jnp.where(forced, FORCED_SCORE, imp), -1.0)
        vals, sel = lax.top_k(imp, top)
        kg = ks_blocks[bi, hi, sel].reshape(b, N_KV_NSA, qn, top * SEL_BLOCK, d)
        vg = vs_blocks[bi, hi, sel].reshape(b, N_KV_NSA, qn, top * SEL_BLOCK, d)
        kpos = (sel[..., None] * SEL_BLOCK + jnp.arange(SEL_BLOCK)).reshape(b, N_KV_NSA, qn, top * SEL_BLOCK)
        m_s = (kpos <= tpos[:, None]) & jnp.repeat(vals >= 0, SEL_BLOCK, axis=-1)
        s_s = jnp.einsum('bkgqd,bkqnd->bkgqn', qq, kg) * scale
        p_s = masked_softmax(s_s, m_s[:, :, None])
        o_s = jnp.einsum('bkgqn,bkqnd->bkgqd', p_s.astype(vg.dtype), vg)
        kw = lax.dynamic_slice_in_dim(kw_pad, t0, qn + WINDOW_2, axis=2)
        vw = lax.dynamic_slice_in_dim(vw_pad, t0, qn + WINDOW_2, axis=2)
        kpos_w = t0 - WINDOW_2 + jnp.arange(qn + WINDOW_2)
        diff = tpos[:, None] - kpos_w[None, :]
        m_w = (kpos_w[None, :] >= 0) & (diff >= 0) & (diff < WINDOW_2)
        s_w = jnp.einsum('bkgqd,bknd->bkgqn', qq, kw) * scale
        p_w = masked_softmax(s_w, m_w)
        o_w = jnp.einsum('bkgqn,bknd->bkgqd', p_w.astype(vw.dtype), vw)
        return gg[..., 0:1] * o_c + gg[..., 1:2] * o_s + gg[..., 2:3] * o_w

    out = lax.map(block, jnp.arange(s // qn))
    return jnp.moveaxis(out, 0, 3).reshape(b, h, s, d)

def forgetting_attention(q, k, v, log_f):
    b, h, s, d = q.shape
    c = jnp.cumsum(log_f, axis=-1)
    kpos = jnp.arange(s)
    scale = HEAD_DIM ** -0.5
    qn = FOX_Q_BLOCK

    def block(qb):
        t0 = qb * qn
        tpos = t0 + jnp.arange(qn)
        qq = lax.dynamic_slice_in_dim(q, t0, qn, axis=2)
        cq = lax.dynamic_slice_in_dim(c, t0, qn, axis=2)
        logits = (jnp.einsum('bhqd,bhsd->bhqs', qq, k).astype(jnp.float32) * scale
                  + cq[..., :, None] - c[:, :, None, :])
        p = masked_softmax(logits, kpos[None, :] <= tpos[:, None])
        return jnp.einsum('bhqs,bhsd->bhqd', p.astype(v.dtype), v)

    out = lax.map(block, jnp.arange(s // qn))
    return jnp.moveaxis(out, 0, 2).reshape(b, h, s, d)

def second_inputs(seed: int = 0) -> dict:
    key = jax.random.key(seed)
    ks = iter(jax.random.split(key, 40))
    nrm = lambda shape, sc: jax.random.normal(next(ks), shape, jnp.float32) * sc
    gain = lambda n: 1.0 + nrm((DEPTH_2, n), 0.05)
    L = DEPTH_2
    return {
        'x': nrm((BATCH, SEQ, D_MODEL), 1.0),
        'p': nrm((DEPTH_2, BATCH, SEQ, D_PLE), 1.0),
        'ffn1_norm': gain(D_MODEL),
        'ffn1_wg': nrm((L, D_MODEL, D_FF_2), D_MODEL ** -0.5),
        'ffn1_wu': nrm((L, D_MODEL, D_FF_2), D_MODEL ** -0.5),
        'ffn1_wd': nrm((L, D_FF_2, D_MODEL), D_FF_2 ** -0.5),
        'mix_norm': gain(D_MODEL),
        'w_in': nrm((L, D_MODEL, IN_WIDTH), D_MODEL ** -0.5),
        'b_forget': 4.0 + nrm((L, N_HEADS_FOX), 0.5),
        'q_norm_nsa': gain(HEAD_DIM),
        'k_norm_cmp': gain(HEAD_DIM),
        'k_norm_slc': gain(HEAD_DIM),
        'k_norm_win': gain(HEAD_DIM),
        'cmp_pos_k': nrm((L, CMP_BLOCK, HEAD_DIM), 0.02),
        'cmp_pos_v': nrm((L, CMP_BLOCK, HEAD_DIM), 0.02),
        'cmp_k_w1': nrm((L, CMP_BLOCK * HEAD_DIM, CMP_HIDDEN), (CMP_BLOCK * HEAD_DIM) ** -0.5),
        'cmp_k_w2': nrm((L, CMP_HIDDEN, HEAD_DIM), CMP_HIDDEN ** -0.5),
        'cmp_v_w1': nrm((L, CMP_BLOCK * HEAD_DIM, CMP_HIDDEN), (CMP_BLOCK * HEAD_DIM) ** -0.5),
        'cmp_v_w2': nrm((L, CMP_HIDDEN, HEAD_DIM), CMP_HIDDEN ** -0.5),
        'q_norm_fox': gain(HEAD_DIM),
        'k_norm_fox': gain(HEAD_DIM),
        'out_norm_nsa': gain(NSA_Q_W),
        'out_norm_fox': gain(FOX_W),
        'w_out': nrm((L, MIX_WIDTH, D_MODEL), MIX_WIDTH ** -0.5),
        'ffn2_norm': gain(D_MODEL),
        'ffn2_wg': nrm((L, D_MODEL, D_FF_2), D_MODEL ** -0.5),
        'ffn2_wu': nrm((L, D_MODEL, D_FF_2), D_MODEL ** -0.5),
        'ffn2_wd': nrm((L, D_FF_2, D_MODEL), D_FF_2 ** -0.5),
        'ple_gate_norm': gain(D_MODEL),
        'ple_w_gate': nrm((L, D_MODEL, D_MODEL), D_MODEL ** -0.5),
        'ple_w_proj': nrm((L, D_PLE, D_MODEL), D_PLE ** -0.5),
        'ple_norm': gain(D_MODEL),
    }

def second_block(x, p, ffn1_norm, ffn1_wg, ffn1_wu, ffn1_wd, mix_norm, w_in, b_forget,
              q_norm_nsa, k_norm_cmp, k_norm_slc, k_norm_win, cmp_pos_k, cmp_pos_v,
              cmp_k_w1, cmp_k_w2, cmp_v_w1, cmp_v_w2, q_norm_fox, k_norm_fox,
              out_norm_nsa, out_norm_fox, w_out, ffn2_norm, ffn2_wg, ffn2_wu, ffn2_wd,
              ple_gate_norm, ple_w_gate, ple_w_proj, ple_norm):
    b, s, _ = x.shape
    cos, sin = rope_tables(s)
    split_points = [int(v) for v in np.cumsum(PROJ_SIZES)[:-1]]
    h = x
    for i in range(DEPTH_2):
        h = h + 0.5 * swiglu(rmsnorm(h, ffn1_norm[i]), ffn1_wg[i], ffn1_wu[i], ffn1_wd[i])
        a = rmsnorm(h, mix_norm[i])
        u = a @ w_in[i]
        (qa, kc, vc, ksl, vsl, kwn, vwn, ga, qf, kf, vf, fl) = jnp.split(u, split_points, axis=-1)
        q_a = partial_rope_2(rmsnorm(split_heads(qa, N_HEADS_NSA), q_norm_nsa[i]), cos, sin)
        kc_tok = partial_rope_2(split_heads(kc, N_KV_NSA), cos, sin)
        k_cmp = rmsnorm(compress_blocks(kc_tok, cmp_pos_k[i], cmp_k_w1[i], cmp_k_w2[i]), k_norm_cmp[i])
        v_cmp = compress_blocks(split_heads(vc, N_KV_NSA), cmp_pos_v[i], cmp_v_w1[i], cmp_v_w2[i])
        k_slc = partial_rope_2(rmsnorm(split_heads(ksl, N_KV_NSA), k_norm_slc[i]), cos, sin)
        k_win = partial_rope_2(rmsnorm(split_heads(kwn, N_KV_NSA), k_norm_win[i]), cos, sin)
        gates = jax.nn.sigmoid(ga).reshape(b, s, N_HEADS_NSA, 3).transpose(0, 2, 1, 3)
        o_a = nsa_attention(q_a, k_cmp, v_cmp, k_slc, split_heads(vsl, N_KV_NSA),
                            k_win, split_heads(vwn, N_KV_NSA), gates)
        q_b = rmsnorm(split_heads(qf, N_HEADS_FOX), q_norm_fox[i])
        k_b = rmsnorm(split_heads(kf, N_HEADS_FOX), k_norm_fox[i])
        log_f = jax.nn.log_sigmoid((fl + b_forget[i]).astype(jnp.float32)).transpose(0, 2, 1)
        o_b = forgetting_attention(q_b, k_b, split_heads(vf, N_HEADS_FOX), log_f)
        mixed = jnp.concatenate([rmsnorm(merge_heads(o_a), out_norm_nsa[i]),
                                 rmsnorm(merge_heads(o_b), out_norm_fox[i])], axis=-1)
        h = h + mixed @ w_out[i]
        h = h + 0.5 * swiglu(rmsnorm(h, ffn2_norm[i]), ffn2_wg[i], ffn2_wu[i], ffn2_wd[i])
        gate = jax.nn.sigmoid(rmsnorm(h, ple_gate_norm[i]) @ ple_w_gate[i])
        e = rmsnorm(p[i] @ ple_w_proj[i], ple_norm[i])
        h = h + gate * e
    return h


def setup_inputs(seed=0):
    out = dict(first_inputs(seed))
    for name, value in second_inputs(seed + 1).items():
        if name != "x":
            out[name + "_2"] = value
    return out


def reference(
    x, p, positions, a_w_in, a_b_igate, a_b_fgate, a_head_norm_g, a_w_out, kv_w, kv_b, b_w_q,
    b_b_q, b_sinks, b_w_o, b_b_o, mix_ln_g, mix_ln_b, mlp_w_up, mlp_w_down, mlp_ln_g, mlp_ln_b,
    ple_w_gate, ple_b_gate, ple_w_proj, p_2, ffn1_norm_2, ffn1_wg_2, ffn1_wu_2, ffn1_wd_2,
    mix_norm_2, w_in_2, b_forget_2, q_norm_nsa_2, k_norm_cmp_2, k_norm_slc_2, k_norm_win_2,
    cmp_pos_k_2, cmp_pos_v_2, cmp_k_w1_2, cmp_k_w2_2, cmp_v_w1_2, cmp_v_w2_2, q_norm_fox_2,
    k_norm_fox_2, out_norm_nsa_2, out_norm_fox_2, w_out_2, ffn2_norm_2, ffn2_wg_2, ffn2_wu_2,
    ffn2_wd_2, ple_gate_norm_2, ple_w_gate_2, ple_w_proj_2, ple_norm_2,
):
    x = first_block(
        x, p, positions, a_w_in, a_b_igate, a_b_fgate, a_head_norm_g, a_w_out, kv_w, kv_b,
        b_w_q, b_b_q, b_sinks, b_w_o, b_b_o, mix_ln_g, mix_ln_b, mlp_w_up, mlp_w_down, mlp_ln_g,
        mlp_ln_b, ple_w_gate, ple_b_gate, ple_w_proj,
    )
    return second_block(
        x, p_2, ffn1_norm_2, ffn1_wg_2, ffn1_wu_2, ffn1_wd_2, mix_norm_2, w_in_2, b_forget_2,
        q_norm_nsa_2, k_norm_cmp_2, k_norm_slc_2, k_norm_win_2, cmp_pos_k_2, cmp_pos_v_2,
        cmp_k_w1_2, cmp_k_w2_2, cmp_v_w1_2, cmp_v_w2_2, q_norm_fox_2, k_norm_fox_2,
        out_norm_nsa_2, out_norm_fox_2, w_out_2, ffn2_norm_2, ffn2_wg_2, ffn2_wu_2, ffn2_wd_2,
        ple_gate_norm_2, ple_w_gate_2, ple_w_proj_2, ple_norm_2,
    )


_drawn_inputs = setup_inputs


def setup_inputs(seed=0):
    import zlib

    import numpy as np

    out = dict(_drawn_inputs(seed))
    spreads = {}
    factors = {'a_b_igate': 58.458,
     'a_head_norm_g': 8.0,
     'kv_b': 4.555,
     'b_b_q': 8.0,
     'b_sinks': 8.0,
     'ple_b_gate': 8.0,
     'ffn1_norm_2': 2.808,
     'q_norm_nsa_2': 4.938,
     'k_norm_cmp_2': 30.547,
     'k_norm_slc_2': 8.0,
     'k_norm_win_2': 8.0,
     'cmp_pos_k_2': 8.0,
     'cmp_pos_v_2': 25.809,
     'q_norm_fox_2': 4.44,
     'k_norm_fox_2': 3.766,
     'ffn2_norm_2': 4.224,
     'ple_gate_norm_2': 28.662,
     'ple_norm_2': 12.147,
     'out_norm_nsa_2': 3.624,
     'out_norm_fox_2': 3.8}
    for name, (base, spread) in spreads.items():
        noise = np.random.default_rng([zlib.crc32(name.encode()), seed]).standard_normal(out[name].shape)
        drawn = base * np.exp(spread * noise) if base else spread * noise
        out[name] = jnp.asarray(drawn.astype(out[name].dtype))
    for name, factor in factors.items():
        out[name] = (out[name] * factor).astype(out[name].dtype)
    return out
```

```python
import math
from contextlib import ExitStack

import numpy as np

import concourse.bass as bass
from concourse import mybir

F32 = mybir.dt.float32
I32 = mybir.dt.int32
ALU = mybir.AluOpType
ACT = mybir.ActivationFunctionType
AX = mybir.AxisListType

P = 128
SEQ = 256
TT = SEQ // P
D = 1024
KT = D // P
BANK = 512
NBANK = 8
DEPTH = 2
ALPHA = (2 * DEPTH) ** 0.25
LN_EPS = 1e-5
RMS_EPS = 1e-6
NEG = -1e30

M_HEADS, M_DK, M_DV, GATE_CAP = 4, 128, 256, 15.0
HD = 64
A_Q_HEADS, A_KV_HEADS = 16, 4
ROT, THETA = HD // 4, 500000.0
HALF = ROT // 2
PLE = 256
D_FF, D_FF_2 = 4096, 2816
N_Q, N_KV, FOX = 8, 2, 8
SIZES = (512, 128, 128, 128, 128, 128, 128, 24, 512, 512, 512, 8)
QA, KC, VC, KSL, VSL, KWN, VWN, GA, QF, KF, VF, FL = [sum(SIZES[:i]) for i in range(12)]
IN2 = sum(SIZES)
CMP_BLOCK, CMP_STRIDE, CMP_HID = 32, 16, 256
N_CMP = (SEQ - CMP_BLOCK) // CMP_STRIDE + 1

SLOTS = 4
SLOT = 4096


class Signal:

    def __init__(self, sem):
        self.sem, self.total = sem, 0


class Chain:

    def __init__(self, eng, steps):
        self.eng, self.steps = eng, steps

    def do(self, ins):
        self.steps.total += 1
        ins.then_inc(self.steps.sem, 1)
        self.eng.wait_ge(self.steps.sem, self.steps.total)


def shares(owners):
    seen, out = {}, []
    for o in owners:
        seen[o] = seen.get(o, 0) + 1
        out.append(seen[o])
    return out


class Kit:
    pass


def rows_of(w):
    return w.rearrange("(k p) n -> p k n", p=P)


def plan_weights(a):
    loads = []

    def cols(w, n0, n1):
        loads.append([rows_of(w)[:, :, n0:n1]])

    def mlp(up, down, hid, width):
        def piece_up(c):
            loads.append([rows_of(w)[:, :, c * width:(c + 1) * width] for w in up])

        def piece_down(c):
            loads.append([rows_of(down[c * width:(c + 1) * width, :])])
        n = hid // width
        piece_up(0)
        for c in range(n):
            if c + 1 < n:
                piece_up(c + 1)
            piece_down(c)

    def ple(gate, proj):
        for c in range(2):
            cols(gate, c * BANK, (c + 1) * BANK)
        loads.append([rows_of(proj)])

    for n0 in range(0, 3072, BANK):
        cols(a["a_w_in"][0], n0, n0 + BANK)
    cols(a["a_w_in"][0], 3072, 3080)
    for c in range(2):
        cols(a["a_w_out"][0], c * BANK, (c + 1) * BANK)
    mlp([a["mlp_w_up"][0]], a["mlp_w_down"][0], D_FF, 512)
    ple(a["ple_w_gate"][0], a["ple_w_proj"][0])
    cols(a["kv_w"], 0, BANK)
    for c in range(2):
        cols(a["b_w_q"][0], c * BANK, (c + 1) * BANK)
    for c in range(2):
        cols(a["b_w_o"][0], c * BANK, (c + 1) * BANK)
    mlp([a["mlp_w_up"][1]], a["mlp_w_down"][1], D_FF, 512)
    ple(a["ple_w_gate"][1], a["ple_w_proj"][1])
    mlp([a["ffn1_wg_2"][0], a["ffn1_wu_2"][0]], a["ffn1_wd_2"][0], D_FF_2, 256)
    for n0, n1 in IN2_CHUNKS:
        cols(a["w_in_2"][0], n0, n1)
    loads.append([rows_of(a["cmp_k_w1_2"][0])])
    loads.append([rows_of(a["cmp_v_w1_2"][0])])
    loads.append([rows_of(a["cmp_k_w2_2"][0]), rows_of(a["cmp_v_w2_2"][0])])
    for c in range(2):
        cols(a["w_out_2"][0], c * BANK, (c + 1) * BANK)
    mlp([a["ffn2_wg_2"][0], a["ffn2_wu_2"][0]], a["ffn2_wd_2"][0], D_FF_2, 256)
    ple(a["ple_w_gate_2"][0], a["ple_w_proj_2"][0])
    return loads


IN2_CHUNKS = [(0, 512), (512, 1024), (1024, 1304), (1304, 1816), (1816, 2328), (2328, 2840), (2840, 2848)]


def weight_views(K, n):
    out, at = [], 0
    for src in K.loads[n]:
        k, w = src.shape[1], src.shape[2]
        out.append(K.ring[:, n % SLOTS, at:at + k * w].rearrange("p (k n) -> p k n", k=k))
        at += k * w
    return out


def load_weights(K, sp, n):
    if n < len(K.loads):
        for dst, src in zip(weight_views(K, n), K.loads[n]):
            sp.dma_start(dst, src).then_inc(K.slot_loaded[n % SLOTS], 16)


def weights_here(K, pe, n):
    pe.wait_ge(K.slot_loaded[n % SLOTS], 16 * sum(len(K.loads[m]) for m in range(n % SLOTS, n + 1, SLOTS)))


def refill(K, sp, first, last_reads):
    for n, (sem, value) in enumerate(last_reads):
        sp.wait_ge(sem, value)
        load_weights(K, sp, first + n + SLOTS)


def bank(K, b, rows=P):
    return K.psum[0:rows, b, :]


def turn(K, items):
    nc = K.nc
    with nc.Block(no_gpsimd_drain=True) as block:
        turned, taken = K.turned.total, {"act": K.act_took.total, "dve": K.dve_took.total}
        who = ["act" if i % 2 == 0 else "dve" for i in range(len(items))]
        nth = shares(who)

        @block.tensor
        def _(pe):
            for i, (srcs, dst, scale) in enumerate(items):
                if i >= NBANK:
                    j = i - NBANK
                    pe.wait_ge((K.act_took if who[j] == "act" else K.dve_took).sem, taken[who[j]] + nth[j])
                for t, src in enumerate(srcs):
                    p, w = src.shape
                    last = nc.tensor.transpose(K.psum[0:w, i % NBANK, t * p:(t + 1) * p], src, K.ident[0:p, 0:p])
                last.then_inc(K.turned.sem, 1)

        def copy(eng, i):
            srcs, dst, scale = items[i]
            w = srcs[0].shape[1]
            ps = K.psum[0:w, i % NBANK, 0:len(srcs) * srcs[0].shape[0]]
            eng.wait_ge(K.turned.sem, turned + i + 1)
            if who[i] == "act":
                if scale is None:
                    nc.scalar.activation(dst, ps, ACT.Copy).then_inc(K.act_took.sem, 1)
                else:
                    nc.scalar.activation(dst, ps, ACT.Copy, scale=scale).then_inc(K.act_took.sem, 1)
            elif scale is None:
                nc.vector.tensor_copy(dst, ps).then_inc(K.dve_took.sem, 1)
            else:
                nc.vector.tensor_scalar(dst, ps, scale, None, ALU.mult).then_inc(K.dve_took.sem, 1)

        @block.scalar
        def _(act):
            for i in range(0, len(items), 2):
                copy(act, i)

        @block.vector
        def _(dve):
            for i in range(1, len(items), 2):
                copy(dve, i)

    K.turned.total += len(items)
    K.act_took.total += who.count("act")
    K.dve_took.total += who.count("dve")


def turn_model(K, src, scale_col=None):
    turn(K, [([src[:, t, k * P:(k + 1) * P] for t in range(TT)], K.xT[:, k, :],
              None if scale_col is None else K.cols[:, scale_col + k:scale_col + k + 1]) for k in range(KT)])


def project(K, groups, who, take):
    nc = K.nc
    first = K.next_load
    items = []
    for g, parts in enumerate(groups):
        for part in parts:
            for t in range(TT):
                items.append((g, part, t))
    owners = [who(n // TT, t) for n, (_, _, t) in enumerate(items)]
    nth = shares(owners)
    filled, took = K.filled.total, {"act": K.act_took.total, "dve": K.dve_took.total}
    with nc.Block(no_gpsimd_drain=True) as block:

        @block.sync
        def _(sp):
            refill(K, sp, first, [(K.filled.sem, filled + 1 + max(i for i, it in enumerate(items) if it[0] == g))
                                  for g in range(len(groups))])

        @block.tensor
        def _(pe):
            for i, (g, (stat, piece, lo, hi), t) in enumerate(items):
                if i == 0 or items[i - 1][0] != g:
                    weights_here(K, pe, first + g)
                if i >= NBANK:
                    j = i - NBANK
                    pe.wait_ge((K.act_took if owners[j] == "act" else K.dve_took).sem, took[owners[j]] + nth[j])
                w = weight_views(K, first + g)[piece]
                kt = w.shape[1]
                for k in range(kt):
                    mm = nc.tensor.matmul(K.psum[:, i % NBANK, 0:hi - lo], stat(k, t), w[:, k, lo:hi],
                                          start=(k == 0), stop=(k == kt - 1))
                mm.then_inc(K.filled.sem, 1)

        def engine(eng, name):
            for i, (g, (stat, piece, lo, hi), t) in enumerate(items):
                if owners[i] == name:
                    eng.wait_ge(K.filled.sem, filled + i + 1)
                    last = take(eng, i // TT, t, K.psum[:, i % NBANK, 0:hi - lo])
                    last.then_inc((K.act_took if name == "act" else K.dve_took).sem, 1)

        @block.scalar
        def _(act):
            engine(act, "act")

        @block.vector
        def _(dve):
            engine(dve, "dve")

    K.filled.total += len(items)
    K.act_took.total += owners.count("act")
    K.dve_took.total += owners.count("dve")
    K.next_load += len(groups)


def feed_forward(K, count, width, gated):
    nc = K.nc
    jt = width // P
    npair = jt // 2
    first = K.next_load
    up0, act0, hid0 = K.filled.total, K.act_took.total, K.hidden_ready.total
    turned0, down0 = K.turned.total, K.down_done.total
    acopy0, vcopy0 = K.act_turned.total, K.dve_turned.total
    up_load = lambda c: first + (0 if c == 0 else 2 * c - 1)
    down_load = lambda c: first + (2 * c + 2 if c + 1 < count else 2 * c + 1)
    xT, hid, rel, hidT = K.xT, K.hid, K.rel, K.hidT
    bank_of = lambda c, q: 6 + (q if npair == 2 else c % 2)

    with nc.Block(no_gpsimd_drain=True) as block:

        @block.sync
        def _(sp):
            reads = [(K.filled.sem, up0 + TT)]
            for c in range(count):
                if c + 1 < count:
                    reads.append((K.filled.sem, up0 + TT * (c + 2)))
                reads.append((K.down_done.sem, down0 + c + 1))
            refill(K, sp, first, reads)

        @block.tensor
        def _(pe):
            def up(c, t):
                if t == 0:
                    weights_here(K, pe, up_load(c))
                if c >= 1:
                    if gated:
                        pe.wait_ge(K.hidden_ready.sem, hid0 + TT * (c - 1) + t + 1)
                    else:
                        pe.wait_ge(K.act_took.sem, act0 + TT * (c - 1) + t + 1)
                pieces = weight_views(K, up_load(c))
                n = len(pieces) * width
                w = K.ring[:, up_load(c) % SLOTS, :].rearrange("p (g k n) -> p k g n", g=len(pieces), k=KT)
                for k in range(KT):
                    mm = nc.tensor.matmul(K.psum[:, 4 + t, 0:n].rearrange("p (g n) -> p g n", g=len(pieces)),
                                          xT[:, k, t * P:(t + 1) * P], w[:, k, :, :],
                                          start=(k == 0), stop=(k == KT - 1))
                mm.then_inc(K.filled.sem, 1)

            def turn_hidden(c):
                pe.wait_ge(K.hidden_ready.sem, hid0 + TT * (c + 1))
                for q in range(npair):
                    b = bank_of(c, q)
                    if npair == 2 and c >= 1:
                        pe.wait_ge((K.act_turned if q == 0 else K.dve_turned).sem, (acopy0 if q == 0 else vcopy0) + c)
                    if npair == 1 and c >= 2:
                        pe.wait_ge(K.act_turned.sem, acopy0 + c - 1)
                    for j in range(2):
                        for t in range(TT):
                            tr = nc.tensor.transpose(K.psum[:, b, (2 * j + t) * P:(2 * j + t + 1) * P],
                                                     hid[:, c % 2, t, (2 * q + j) * P:(2 * q + j + 1) * P],
                                                     K.ident[:, :])
                    tr.then_inc(K.turned.sem, 1)

            def down(c):
                weights_here(K, pe, down_load(c))
                w = weight_views(K, down_load(c))[0]
                for j in range(jt):
                    if j % 2 == 0:
                        if npair == 2 and j == 2:
                            pe.wait_ge(K.dve_turned.sem, vcopy0 + c + 1)
                        else:
                            pe.wait_ge(K.act_turned.sem, acopy0 + c + 1)
                    for t in range(TT):
                        for h in range(2):
                            mm = nc.tensor.matmul(K.psum[:, 2 * t + h, :], hidT[:, c % 2, j, t * P:(t + 1) * P],
                                                  w[:, j, h * BANK:(h + 1) * BANK],
                                                  start=(c == 0 and j == 0), stop=(c == count - 1 and j == jt - 1))
                mm.then_inc(K.down_done.sem, 1)

            for t in range(TT):
                up(0, t)
            for c in range(count):
                if c + 1 < count:
                    up(c + 1, 0)
                turn_hidden(c)
                if c + 1 < count:
                    up(c + 1, 1)
                down(c)

        @block.scalar
        def _(act):
            def first_half(c):
                for t in range(TT):
                    act.wait_ge(K.filled.sem, up0 + TT * c + t + 1)
                    if c >= 1:
                        act.wait_ge(K.hidden_ready.sem, hid0 + TT * (c - 1) + t + 1)
                    nc.scalar.activation(rel[:, t, 0:width], K.psum[:, 4 + t, 0:width],
                                         ACT.Silu if gated else ACT.Relu).then_inc(K.act_took.sem, 1)

            def copy(c):
                act.wait_ge(K.turned.sem, turned0 + npair * c + 1)
                if c >= 2:
                    act.wait_ge(K.down_done.sem, down0 + c - 1)
                nc.scalar.activation(hidT[:, c % 2, 0:2, :], K.psum[:, bank_of(c, 0), :].rearrange(
                    "p (j n) -> p j n", j=2), ACT.Copy).then_inc(K.act_turned.sem, 1)

            first_half(0)
            for c in range(count):
                if c + 1 < count:
                    act.wait_ge(K.filled.sem, up0 + TT * (c + 1) + 1)
                    act.wait_ge(K.hidden_ready.sem, hid0 + TT * c + 1)
                    nc.scalar.activation(rel[:, 0, 0:width], K.psum[:, 4, 0:width],
                                         ACT.Silu if gated else ACT.Relu).then_inc(K.act_took.sem, 1)
                copy(c)
                if c + 1 < count:
                    act.wait_ge(K.filled.sem, up0 + TT * (c + 1) + 2)
                    act.wait_ge(K.hidden_ready.sem, hid0 + TT * c + 2)
                    nc.scalar.activation(rel[:, 1, 0:width], K.psum[:, 5, 0:width],
                                         ACT.Silu if gated else ACT.Relu).then_inc(K.act_took.sem, 1)

        @block.vector
        def _(dve):
            def second_half(c, t):
                dve.wait_ge(K.act_took.sem, act0 + TT * c + t + 1)
                if c >= 2:
                    dve.wait_ge(K.turned.sem, turned0 + npair * (c - 1))
                other = K.psum[:, 4 + t, width:2 * width] if gated else rel[:, t, 0:width]
                nc.vector.tensor_tensor(hid[:, c % 2, t, 0:width], rel[:, t, 0:width], other,
                                        ALU.mult).then_inc(K.hidden_ready.sem, 1)

            def copy(c):
                if npair == 2:
                    dve.wait_ge(K.turned.sem, turned0 + npair * c + 2)
                    if c >= 2:
                        dve.wait_ge(K.down_done.sem, down0 + c - 1)
                    nc.vector.tensor_copy(hidT[:, c % 2, 2:4, :], K.psum[:, 7, :].rearrange(
                        "p (j n) -> p j n", j=2)).then_inc(K.dve_turned.sem, 1)

            for t in range(TT):
                second_half(0, t)
            for c in range(count):
                if c + 1 < count:
                    second_half(c + 1, 0)
                copy(c)
                if c + 1 < count:
                    second_half(c + 1, 1)

    K.filled.total += TT * count
    K.act_took.total += TT * count
    K.hidden_ready.total += TT * count
    K.turned.total += npair * count
    K.down_done.total += count
    K.act_turned.total += count
    K.dve_turned.total += count if npair == 2 else 0
    K.next_load += 2 * count


def residual_norm(K, gain, shift, bias=None):
    nc = K.nc
    with nc.Block(no_gpsimd_drain=True) as block:
        stat0, rstd0, hat0 = K.stat_ready.total, K.rstd_ready.total, K.hat_ready.total

        @block.vector
        def _(dve):
            ch = Chain(dve, K.dve_step)
            for r in (gain, shift, bias):
                if r is not None:
                    row_here(K, dve, r)
            for t in range(TT):
                z = K.z[:, t, :]
                for h in range(2):
                    s = slice(h * BANK, (h + 1) * BANK)
                    ch.do(nc.vector.scalar_tensor_tensor(z[:, s], K.x[:, t, s], ALPHA, K.psum[:, 2 * t + h, :],
                                                         ALU.mult, ALU.add))
                    if bias is not None:
                        ch.do(nc.vector.tensor_tensor(z[:, s], z[:, s], K.rows[:, bias, s], ALU.add))
                    ch.do(nc.vector.bn_stats(K.bn[:, t, h, :], z[:, s]))
                ch.do(nc.vector.bn_aggr(K.stat[:, t, 0:2], K.bn[:, t, :, :]))
                nc.vector.tensor_scalar(K.stat[:, t, 1:2], K.stat[:, t, 1:2], LN_EPS, None,
                                        ALU.add).then_inc(K.stat_ready.sem, 1)
            for t in range(TT):
                dve.wait_ge(K.rstd_ready.sem, rstd0 + t + 1)
                nc.vector.scalar_tensor_tensor(K.stat[:, t, 3:4], K.stat[:, t, 0:1], -1.0, K.stat[:, t, 2:3],
                                               ALU.mult, ALU.mult).then_inc(K.stat_ready.sem, 1)
            for t in range(TT):
                dve.wait_ge(K.hat_ready.sem, hat0 + t + 1)
                ch.do(nc.vector.tensor_tensor(K.z[:, t, :], K.z[:, t, :], K.rows[:, gain, :], ALU.mult))
                ch.do(nc.vector.tensor_tensor(K.x[:, t, :], K.z[:, t, :], K.rows[:, shift, :], ALU.add))

        @block.gpsimd
        def _(pool):
            for t in range(TT):
                pool.wait_ge(K.stat_ready.sem, stat0 + t + 1)
                nc.gpsimd.tensor_tensor(K.stat[:, t, 2:3], K.stat[:, t, 1:2], K.minus_half[:, 0:1],
                                        ALU.pow).then_inc(K.rstd_ready.sem, 1)
            pool.wait_ge(K.rstd_ready.sem, rstd0 + TT)

        @block.scalar
        def _(act):
            for t in range(TT):
                act.wait_ge(K.stat_ready.sem, stat0 + TT + t + 1)
                nc.scalar.activation(K.z[:, t, :], K.z[:, t, :], ACT.Identity, bias=K.stat[:, t, 3:4],
                                     scale=K.stat[:, t, 2:3]).then_inc(K.hat_ready.sem, 1)

    K.stat_ready.total += 2 * TT
    K.rstd_ready.total += TT
    K.hat_ready.total += TT


def root_norm(K, src, widths, dst):
    nc = K.nc
    n = len(widths)
    with nc.Block(no_gpsimd_drain=True) as block:
        sq0, stat0, rstd0 = K.square_ready.total, K.stat_ready.total, K.rstd_ready.total

        @block.scalar
        def _(act):
            for t in range(TT):
                for i, (lo, hi) in enumerate(widths):
                    nc.scalar.activation(K.scratch[:, t, lo:hi], src[:, t, lo:hi], ACT.Square,
                                         accum_out=K.stat[:, t, i:i + 1]).then_inc(K.square_ready.sem, 1)

        @block.vector
        def _(dve):
            for t in range(TT):
                dve.wait_ge(K.square_ready.sem, sq0 + n * (t + 1))
                for i, (lo, hi) in enumerate(widths):
                    last = nc.vector.tensor_scalar(K.stat[:, t, 2 + i:3 + i], K.stat[:, t, i:i + 1], 1.0 / (hi - lo),
                                                   RMS_EPS, ALU.mult, ALU.add)
                last.then_inc(K.stat_ready.sem, 1)
            for t in range(TT):
                dve.wait_ge(K.rstd_ready.sem, rstd0 + t + 1)
                for i, (lo, hi) in enumerate(widths):
                    nc.vector.tensor_scalar(dst[:, t, lo:hi], src[:, t, lo:hi], K.stat[:, t, 4 + i:5 + i], None,
                                            ALU.mult)

        @block.gpsimd
        def _(pool):
            for t in range(TT):
                pool.wait_ge(K.stat_ready.sem, stat0 + t + 1)
                nc.gpsimd.tensor_tensor(K.stat[:, t, 4:4 + n], K.stat[:, t, 2:2 + n], K.minus_half[:, 0:n],
                                        ALU.pow).then_inc(K.rstd_ready.sem, 1)
            pool.wait_ge(K.rstd_ready.sem, rstd0 + TT)

    K.square_ready.total += n * TT
    K.stat_ready.total += TT
    K.rstd_ready.total += TT


def half_step(K):
    nc = K.nc
    with nc.Block(no_gpsimd_drain=True) as block:

        @block.vector
        def _(dve):
            for t in range(TT):
                for h in range(2):
                    s = slice(h * BANK, (h + 1) * BANK)
                    nc.vector.scalar_tensor_tensor(K.x[:, t, s], K.psum[:, 2 * t + h, :], 0.5, K.x[:, t, s],
                                                   ALU.mult, ALU.add)


def row_here(K, eng, r):
    eng.wait_ge(K.row_loaded[r], 16 * K.row_loads[r])


def load_rows(K, sp, which):
    for r, vec in which.items():
        w = vec.shape[0]
        sp.dma_start(K.rows[:, r, 0:w], vec.partition_broadcast(P)).then_inc(K.row_loaded[r], 16)
        K.row_loads[r] += 1


def rows_stage(K, which):
    with K.nc.Block(no_gpsimd_drain=True) as block:

        @block.sync
        def _(sp):
            load_rows(K, sp, which)


def setup(K, a):
    nc = K.nc
    lists = [("head_g", a["a_head_norm_g"][0]), ("ffn1", a["ffn1_norm_2"][0]), ("mix", a["mix_norm_2"][0]),
             ("out_nsa", a["out_norm_nsa_2"][0]), ("out_fox", a["out_norm_fox_2"][0]), ("ffn2", a["ffn2_norm_2"][0]),
             ("ple", a["ple_gate_norm_2"][0]), ("pos_k", a["cmp_pos_k_2"][0].rearrange("j d -> (j d)")),
             ("pos_v", a["cmp_pos_v_2"][0].rearrange("j d -> (j d)"))]
    K.col_of, n = {}, 0
    for name, vec in lists:
        K.col_of[name] = n
        n += vec.shape[0] // P
    K.n_cols = n
    with nc.Block(no_gpsimd_drain=True) as block:

        @block.sync
        def _(sp):
            sp.dma_start(K.x[:, :, :], a["x"][0].rearrange("(t p) d -> p t d", p=P)).then_inc(K.input_loaded, 16)
            for n in range(SLOTS):
                load_weights(K, sp, n)

        @block.scalar
        def _(act):
            for name, vec in lists:
                c, m = K.col_of[name], vec.shape[0] // P
                act.dma_start(K.z[c:c + m, 0, 0:P], vec.rearrange("(k p) -> k p", p=P)).then_inc(K.small_loaded, 16)
            act.dma_start(K.positions[:, :], a["positions"][0].rearrange("(t p) -> p t", p=P),
                          allow_slow_non_contiguous=True).then_inc(K.small_loaded, 16)
            act.dma_start(K.gate_bias[0:M_HEADS, 0:1], a["a_b_igate"][0].unsqueeze(1)).then_inc(K.small_loaded, 16)
            act.dma_start(K.gate_bias[0:M_HEADS, 1:2], a["a_b_fgate"][0].unsqueeze(1)).then_inc(K.small_loaded, 16)
            act.dma_start(K.gate_bias[0:FOX, 2:3], a["b_forget_2"][0].unsqueeze(1)).then_inc(K.small_loaded, 16)
            act.dma_start(K.sinks[:, :], a["b_sinks"][0].partition_broadcast(P)).then_inc(K.small_loaded, 16)
            for i, name in enumerate(["q_norm_nsa_2", "k_norm_slc_2", "k_norm_win_2", "q_norm_fox_2", "k_norm_fox_2",
                                      "k_norm_cmp_2"]):
                act.dma_start(K.head_gain[:, i, :], a[name][0].partition_broadcast(P)).then_inc(K.small_loaded, 16)
            act.wait_ge(K.small_loaded, 16 * (len(lists) + 11))

        @block.vector
        def _(dve):
            for ap, value in [(K.ident[:, :], 0.0), (K.sel[:, :, :], 0.0), (K.ones[:, :], 1.0),
                              (K.minus_half[:, :], -0.5), (K.causal[:, :], 0.0), (K.window[:, :], 0.0),
                              (K.causal_t[:, :], 0.0), (K.cmp_mask[:, :, :], 0.0), (K.cmp_keep[:, :, :], 1.0),
                              (K.v_ext[:, :, :, :], 1.0)]:
                last = nc.vector.memset(ap, value)
            for i in range(HALF):
                last = nc.vector.memset(K.inv_freq[:, i:i + 1], float(np.float32(THETA) ** np.float32(-i * 2.0 / ROT)))
            last.then_inc(K.zeroed, 1)

        @block.gpsimd
        def _(pool):
            pool.wait_ge(K.zeroed, 1)

            def select(out, src, pattern, base, mult, fill, op=ALU.is_ge):
                K.masked_total += 1
                nc.gpsimd.affine_select(out=out, in_=src, compare_op=op, fill=fill, base=base, pattern=pattern,
                                        channel_multiplier=mult).then_inc(K.masked, 1)
                pool.wait_ge(K.masked, K.masked_total)

            select(K.ident[:, :], K.ident[:, :], [[-1, P]], 0, 1, 1.0, ALU.not_equal)
            select(K.sel[:, :, :], K.sel[:, :, :], [[-1, FOX], [0, P]], 0, 1, 1.0, ALU.not_equal)
            select(K.causal[:, :], K.causal[:, :], [[-1, SEQ]], P, 1, NEG)
            select(K.window[:, :], K.causal[:, :], [[1, SEQ]], 0, -1, NEG, ALU.is_gt)
            select(K.causal_t[:, 0:P], K.causal_t[:, 0:P], [[1, P]], 0, -1, NEG)
            select(K.causal_t[:, 2 * P:3 * P], K.causal_t[:, 2 * P:3 * P], [[1, P]], 0, -1, NEG)
            for t in range(TT):
                pat = [[-CMP_STRIDE, N_CMP]]
                select(K.cmp_mask[:, t, :], K.cmp_mask[:, t, :], pat, t * P - CMP_BLOCK + 1, 1, NEG)
                select(K.cmp_keep[:, t, :], K.cmp_keep[:, t, :], pat, t * P - CMP_BLOCK + 1, 1, 0.0)
            nc.gpsimd.iota(K.index[:, :], [[P, TT]], base=0, channel_multiplier=1).then_inc(K.masked, 1)
            K.masked_total += 1
            pool.wait_ge(K.masked, K.masked_total)

        @block.tensor
        def _(pe):
            pe.wait_ge(K.input_loaded, 16)

    turn(K, [([K.z[0:n, 0, 0:P]], K.cols[:, 0:n], None)])
    turn_model(K, K.x)
    rotary_tables(K)


def rotary_tables(K):
    nc = K.nc
    n = 2 * TT * HALF
    with nc.Block(no_gpsimd_drain=True) as block:
        ready0 = K.angle_ready.total

        @block.vector
        def _(dve):
            ch = Chain(dve, K.dve_step)
            A = K.angle
            ch.do(nc.vector.tensor_copy(K.pos_f[:, 0:TT], K.positions[:, :]))
            ch.do(nc.vector.tensor_copy(K.pos_f[:, TT:2 * TT], K.index[:, :]))
            for i in range(2 * TT):
                ch.do(nc.vector.tensor_scalar(A[:, 0, i * HALF:(i + 1) * HALF], K.inv_freq[:, :],
                                              K.pos_f[:, i:i + 1], None, ALU.mult))
            for which, shift in ((1, 0.25), (2, 0.0)):
                ch.do(nc.vector.tensor_scalar(A[:, 3, :], A[:, 0, :], 1.0 / (2 * math.pi), shift, ALU.mult, ALU.add))
                ch.do(nc.vector.tensor_scalar(A[:, 3, :], A[:, 3, :], ROUND, None, ALU.add))
                ch.do(nc.vector.tensor_scalar(A[:, 3, :], A[:, 3, :], ROUND, None, ALU.subtract))
                ch.do(nc.vector.scalar_tensor_tensor(A[:, which, :], A[:, 3, :], -TWO_PI[0], A[:, 0, :],
                                                     ALU.mult, ALU.add))
                ch.do(nc.vector.scalar_tensor_tensor(A[:, which, :], A[:, 3, :], -TWO_PI[1], A[:, which, :],
                                                     ALU.mult, ALU.add))
                ch.do(nc.vector.scalar_tensor_tensor(A[:, which, :], A[:, 3, :], -TWO_PI[2], A[:, which, :],
                                                     ALU.mult, ALU.add))
                if which == 1:
                    ch.do(nc.vector.tensor_scalar(A[:, which, :], A[:, which, :], math.pi / 2, None, ALU.add))
                ch.do(nc.vector.tensor_scalar(A[:, which, :], A[:, which, :], PI_BELOW, -PI_BELOW, ALU.min, ALU.max))
            nc.vector.tensor_copy(A[:, 4, :], A[:, 1, :]).then_inc(K.angle_ready.sem, 1)

        @block.scalar
        def _(act):
            act.wait_ge(K.angle_ready.sem, ready0 + 1)
            nc.scalar.activation(K.cos_sin[:, 0, :], K.angle[:, 1, :], ACT.Sin)
            nc.scalar.activation(K.cos_sin[:, 1, :], K.angle[:, 2, :], ACT.Sin)
    K.angle_ready.total += 1


ROUND = 1.5 * 2.0 ** 23
TWO_PI = [6.28125, float(np.float32(2 * math.pi - 6.28125)),
          float(2 * math.pi - 6.28125 - float(np.float32(2 * math.pi - 6.28125)))]
PI_BELOW = 3.1415925


def rotate(K, ch, heads, table, t):
    nc = K.nc
    n = heads.shape[1]
    at = (table * TT + t) * HALF
    cos, sin = [K.cos_sin[:, i, at:at + HALF].unsqueeze(1).broadcast_to([P, n, HALF]) for i in range(2)]
    a, b = heads[:, :, 0:HALF], heads[:, :, HALF:ROT]
    w = [K.rot[:, i, 0:n, :] for i in range(4)]
    nc.vector.tensor_tensor(w[0], a, cos, ALU.mult)
    nc.vector.tensor_tensor(w[1], b, sin, ALU.mult)
    nc.vector.tensor_tensor(w[2], b, cos, ALU.mult)
    ch.do(nc.vector.tensor_tensor(w[3], a, sin, ALU.mult))
    nc.vector.tensor_tensor(a, w[0], w[1], ALU.subtract)
    ch.do(nc.vector.tensor_tensor(b, w[2], w[3], ALU.add))


def gate_columns(K):
    nc = K.nc
    H = M_HEADS
    with nc.Block(no_gpsimd_drain=True) as block:
        turned, step0, act0 = K.turned.total, K.gates_v.total, K.gates_a.total

        @block.tensor
        def _(pe):
            for i in range(2):
                for t in range(TT):
                    tr = nc.tensor.transpose(K.psum[0:H, 0, (i * TT + t) * P:(i * TT + t + 1) * P],
                                             K.u[:, t, 3072 + i * H:3072 + (i + 1) * H], K.ident[:, :])
            tr.then_inc(K.turned.sem, 1)
            pe.wait_ge(K.gates_v.sem, step0 + 3)
            for i, r in enumerate((1, 3)):
                for t in range(TT):
                    at = (i * TT + t) * H
                    tr = nc.tensor.transpose(K.psum[:, 1, at:at + H], K.gates[0:H, r, t * P:(t + 1) * P],
                                             K.ident[0:H, 0:H])
            tr.then_inc(K.turned.sem, 1)

        @block.vector
        def _(dve):
            ch = Chain(dve, K.dve_step)
            G = K.gates
            nc.vector.tensor_scalar(K.gate_bias[0:H, 0:2], K.gate_bias[0:H, 0:2], 1.0 / GATE_CAP, None,
                                    ALU.mult).then_inc(K.gates_v.sem, 1)
            dve.wait_ge(K.gates_a.sem, act0 + 3)
            ch.do(nc.vector.tensor_tensor_scan(G[0:H, 5, :], K.ones[0:H, :], G[0:H, 6, :], 0.0, ALU.mult,
                                               ALU.subtract))
            ch.do(nc.vector.scalar_tensor_tensor(G[0:H, 1, :], G[0:H, 0, 0:SEQ], GATE_CAP, G[0:H, 5, :], ALU.mult,
                                                 ALU.subtract))
            ch.do(nc.vector.tensor_tensor_scan(G[0:H, 4, :], G[0:H, 1, :], G[0:H, 1, :], 0.0, ALU.max, ALU.max))
            nc.vector.tensor_scalar(G[0:H, 2, :], G[0:H, 4, :], -1.0, None, ALU.mult).then_inc(K.gates_v.sem, 1)
            nc.vector.scalar_tensor_tensor(G[0:H, 3, :], G[0:H, 4, :], -1.0, G[0:H, 5, :], ALU.mult,
                                           ALU.subtract).then_inc(K.gates_v.sem, 1)
            dve.wait_ge(K.turned.sem, turned + 2)
            nc.vector.tensor_copy(K.u_col[:, :], K.psum[:, 1, 0:TT * H]).then_inc(K.gates_v.sem, 1)

        @block.scalar
        def _(act):
            G = K.gates
            act.wait_ge(K.turned.sem, turned + 1)
            act.wait_ge(K.gates_v.sem, step0 + 1)
            nc.scalar.activation(G[0:H, 0, :], K.psum[0:H, 0, 0:SEQ], ACT.Tanh, bias=K.gate_bias[0:H, 0:1],
                                 scale=1.0 / GATE_CAP)
            nc.scalar.activation(G[0:H, 7, :], K.psum[0:H, 0, SEQ:2 * SEQ], ACT.Tanh, bias=K.gate_bias[0:H, 1:2],
                                 scale=1.0 / GATE_CAP).then_inc(K.gates_a.sem, 1)
            act.wait_ge(K.gates_a.sem, act0 + 1)
            nc.scalar.activation(G[0:H, 7, :], G[0:H, 7, :], ACT.Exp, scale=-GATE_CAP).then_inc(K.gates_a.sem, 1)
            act.wait_ge(K.gates_a.sem, act0 + 2)
            nc.scalar.activation(G[0:H, 6, :], G[0:H, 7, :], ACT.Ln, bias=1.0).then_inc(K.gates_a.sem, 1)
            act.wait_ge(K.gates_v.sem, step0 + 4)
            nc.scalar.activation(K.exp_m[:, :], K.psum[:, 1, TT * H:2 * TT * H], ACT.Exp)

    K.turned.total += 2
    K.gates_v.total += 4
    K.gates_a.total += 3


def mlstm(K):
    nc = K.nc
    H, W = M_HEADS, 3 * P
    pieces = ((0, 0, SEQ, 0), (1, P, SEQ, SEQ))
    with nc.Block(no_gpsimd_drain=True) as block:
        scores0, arg0, expd0, weight0 = K.scores_ready.total, K.masked_scores.total, K.probs_ready.total, \
            K.weights_ready.total
        out0, took0 = K.values_ready.total, K.act_took.total

        @block.tensor
        def _(pe):
            def scores(h):
                if h >= 2:
                    pe.wait_ge(K.weights_ready.sem, weight0 + h - 1)
                for s, q0, q1, at in pieces:
                    nc.tensor.matmul(K.psum[:, h % 2, at:at + q1 - q0], K.qkT[:, H + h, s * P:(s + 1) * P],
                                     K.qkT[:, h, q0:q1], start=True, stop=True)
                    mm = nc.tensor.matmul(K.psum[:, 2 + h % 2, at:at + q1 - q0], K.sel[0:H, h, :],
                                          K.gates[0:H, 2, q0:q1], start=True, stop=True)
                mm.then_inc(K.scores_ready.sem, 1)

            def values(h):
                pe.wait_ge(K.weights_ready.sem, weight0 + h + 1)
                if h >= 2:
                    pe.wait_ge(K.act_took.sem, took0 + TT * (h - 1))
                w = K.decayed[:, h % 2, :]
                b = 4 + 2 * (h % 2)
                nc.tensor.matmul(K.psum[:, b, 0:M_DV + 1], w[:, 0:P], K.v_ext[:, 0, h, :], start=True, stop=True)
                nc.tensor.matmul(K.psum[:, b + 1, 0:M_DV + 1], w[:, P:2 * P], K.v_ext[:, 0, h, :],
                                 start=True, stop=False)
                nc.tensor.matmul(K.psum[:, b + 1, 0:M_DV + 1], w[:, 2 * P:3 * P], K.v_ext[:, 1, h, :],
                                 start=False, stop=True).then_inc(K.values_ready.sem, 1)

            scores(0)
            for h in range(H):
                if h + 1 < H:
                    scores(h + 1)
                values(h)

        @block.vector
        def _(dve):
            def exponent(h):
                dve.wait_ge(K.scores_ready.sem, scores0 + h + 1)
                if h >= 2:
                    dve.wait_ge(K.probs_ready.sem, expd0 + h - 1)
                nc.vector.scalar_tensor_tensor(K.exponent[:, h % 2, 0:SEQ], K.psum[:, 2 + h % 2, 0:SEQ],
                                               K.u_col[:, h:h + 1], K.causal_t[:, 0:SEQ], ALU.add, ALU.add)
                nc.vector.scalar_tensor_tensor(K.exponent[:, h % 2, SEQ:W], K.psum[:, 2 + h % 2, SEQ:W],
                                               K.u_col[:, H + h:H + h + 1], K.causal_t[:, SEQ:W], ALU.add,
                                               ALU.add).then_inc(K.masked_scores.sem, 1)

            def weigh(h):
                dve.wait_ge(K.probs_ready.sem, expd0 + h + 1)
                if h >= 2:
                    dve.wait_ge(K.values_ready.sem, out0 + h - 1)
                nc.vector.scalar_tensor_tensor(K.decayed[:, h % 2, :], K.psum[:, h % 2, 0:W], M_DK ** -0.5,
                                               K.decay[:, h % 2, :], ALU.mult,
                                               ALU.mult).then_inc(K.weights_ready.sem, 1)

            exponent(0)
            for h in range(H):
                if h + 1 < H:
                    exponent(h + 1)
                weigh(h)

        @block.scalar
        def _(act):
            def decay(h):
                act.wait_ge(K.masked_scores.sem, arg0 + h + 1)
                if h >= 2:
                    act.wait_ge(K.weights_ready.sem, weight0 + h - 1)
                nc.scalar.activation(K.decay[:, h % 2, :], K.exponent[:, h % 2, :],
                                     ACT.Exp).then_inc(K.probs_ready.sem, 1)

            def copy_out(h):
                act.wait_ge(K.values_ready.sem, out0 + h + 1)
                for t in range(TT):
                    nc.scalar.activation(K.h_raw[:, t, h, :], K.psum[:, 4 + 2 * (h % 2) + t, 0:M_DV + 1],
                                         ACT.Copy).then_inc(K.act_took.sem, 1)

            decay(0)
            for h in range(H):
                if h + 1 < H:
                    decay(h + 1)
                copy_out(h)

    K.scores_ready.total += H
    K.masked_scores.total += H
    K.probs_ready.total += H
    K.weights_ready.total += H
    K.values_ready.total += H
    K.act_took.total += TT * H


def mlstm_norm(K):
    nc = K.nc
    H, n = M_HEADS, TT * M_HEADS
    with nc.Block(no_gpsimd_drain=True) as block:
        stat0, rstd0 = K.stat_ready.total, K.rstd_ready.total
        S = K.mstat

        @block.vector
        def _(dve):
            ch = Chain(dve, K.dve_step)
            for t in range(TT):
                for h in range(H):
                    ch.do(nc.vector.bn_stats(K.bn8[:, t * H + h, :], K.h_raw[:, t, h, 0:M_DV]))
            for i in range(n):
                ch.do(nc.vector.bn_aggr(K.mean_var[:, i, :], K.bn8[:, i, :]))
            mean, var = K.mean_var[:, :, 0], K.mean_var[:, :, 1]
            for t in range(TT):
                den = K.h_raw[:, t, :, M_DV]
                ch.do(nc.vector.scalar_tensor_tensor(S[:, 0, t * H:(t + 1) * H], den, -1.0, den, ALU.mult, ALU.max))
            ch.do(nc.vector.tensor_tensor(S[:, 0, :], S[:, 0, :], K.exp_m[:, :], ALU.max))
            ch.do(nc.vector.reciprocal(S[:, 1, :], S[:, 0, :]))
            ch.do(nc.vector.tensor_tensor(S[:, 2, :], S[:, 1, :], S[:, 1, :], ALU.mult))
            ch.do(nc.vector.tensor_tensor(S[:, 2, :], S[:, 2, :], var, ALU.mult))
            nc.vector.tensor_scalar(S[:, 2, :], S[:, 2, :], LN_EPS, None, ALU.add).then_inc(K.stat_ready.sem, 1)
            dve.wait_ge(K.rstd_ready.sem, rstd0 + 1)
            ch.do(nc.vector.tensor_tensor(S[:, 4, :], S[:, 3, :], S[:, 1, :], ALU.mult))
            for t in range(TT):
                for h in range(H):
                    i = t * H + h
                    ch.do(nc.vector.tensor_scalar(K.z[:, t, h * M_DV:(h + 1) * M_DV], K.h_raw[:, t, h, 0:M_DV],
                                                  mean[:, i:i + 1], S[:, 4, i:i + 1], ALU.subtract, ALU.mult))
                nc.vector.tensor_tensor(K.z[:, t, :], K.z[:, t, :], K.u[:, t, 2048:3072], ALU.mult)

        @block.gpsimd
        def _(pool):
            pool.wait_ge(K.stat_ready.sem, stat0 + 1)
            nc.gpsimd.tensor_tensor(S[:, 3, :], S[:, 2, :], K.minus_half[:, 0:n], ALU.pow).then_inc(K.rstd_ready.sem, 1)
            pool.wait_ge(K.rstd_ready.sem, rstd0 + 1)

    K.stat_ready.total += 1
    K.rstd_ready.total += 1


def attend(K, units, groups):
    nc = K.nc
    n = len(units)
    with nc.Block(no_gpsimd_drain=True) as block:
        sc0, ms0, pr0, kp0 = K.scores_ready.total, K.masked_scores.total, K.probs_ready.total, K.probs_kept.total
        tu0, ac0, vc0 = K.turned.total, K.act_turned.total, K.dve_turned.total
        va0, og0 = K.values_ready.total, K.group_out.total
        kept = lambda i: sum(1 for u in units[:i] if u["keep"] is not None)
        columns = lambda u: u["size"] + (u["sink"] is not None)
        tiles = lambda u: [(s, min(P, u["size"] - s)) for s in range(0, u["size"], P)]

        def copied(eng, i):
            if i % 2 == 0:
                eng.wait_ge(K.act_turned.sem, ac0 + i // 2 + 1)
            else:
                eng.wait_ge(K.dve_turned.sem, vc0 + i // 2 + 1)

        @block.tensor
        def _(pe):
            def scores(i):
                u = units[i]
                if i >= 3:
                    pe.wait_ge(K.masked_scores.sem, ms0 + i - 2)
                for a in range(2):
                    out = K.psum[:, i % 3, a * SEQ:a * SEQ + u["size"]]
                    mm = nc.tensor.matmul(out, u["q"][a], u["k"][a], start=True, stop=u["bias"] is None)
                    if u["bias"] is not None:
                        mm = nc.tensor.matmul(out, *u["bias"][a], start=False, stop=True)
                mm.then_inc(K.scores_ready.sem, 1)

            def turn_probs(i):
                u = units[i]
                pe.wait_ge(K.probs_ready.sem, pr0 + i + 1)
                if u["keep"] is not None:
                    pe.wait_ge(K.probs_kept.sem, kp0 + kept(i) + 1)
                if i >= 2:
                    copied(pe, i - 2)
                for a in range(2):
                    for j, (s, w) in enumerate(tiles(u)):
                        tr = nc.tensor.transpose(K.psum[0:w, 3 + i % 2, (2 * a + j) * P:(2 * a + j + 1) * P],
                                                 K.probs[:, i % 3, a, s:s + w], K.ident[:, :])
                tr.then_inc(K.turned.sem, 1)

            def values(i):
                u = units[i]
                copied(pe, i)
                g = i // 4
                if i % 4 == 0 and g >= 3:
                    pe.wait_ge(K.group_out.sem, og0 + g - 2)
                for a in range(2):
                    for j, (s, w) in enumerate(tiles(u)):
                        at = (2 * (i % 4) + a) * HD
                        mm = nc.tensor.matmul(K.psum[:, 5 + g % 3, at:at + HD],
                                              K.probsT[0:w, i % 2, (2 * a + j) * P:(2 * a + j + 1) * P],
                                              u["v"][a][j], start=(j == 0), stop=(j == len(tiles(u)) - 1))
                mm.then_inc(K.values_ready.sem, 1)

            for i in range(n + 3):
                if i < n:
                    scores(i)
                if 0 <= i - 2 < n:
                    turn_probs(i - 2)
                if 0 <= i - 3 < n:
                    values(i - 3)

        def copy(eng, i):
            u = units[i]
            eng.wait_ge(K.turned.sem, tu0 + i + 1)
            if i >= 2:
                eng.wait_ge(K.values_ready.sem, va0 + i - 1)
            w = min(P, u["size"])
            if u["size"] > P:
                src, dst = K.psum[:, 3 + i % 2, :], K.probsT[:, i % 2, :]
            else:
                src, dst = [z.rearrange("p (a j q) -> p a j q", a=2, j=2)[:, :, 0, :]
                            for z in (K.psum[0:w, 3 + i % 2, :], K.probsT[0:w, i % 2, :])]
            if i % 2 == 0:
                nc.scalar.activation(dst, src, ACT.Copy).then_inc(K.act_turned.sem, 1)
            else:
                nc.vector.tensor_copy(dst, src).then_inc(K.dve_turned.sem, 1)

        @block.scalar
        def _(act):
            for i in range(n + 2):
                if i < n:
                    u = units[i]
                    act.wait_ge(K.masked_scores.sem, ms0 + i + 1)
                    if i >= 3:
                        act.wait_ge(K.turned.sem, tu0 + i - 2)
                    for a in range(2):
                        at = slice(0, columns(u))
                        e = nc.scalar.activation(K.probs[:, i % 3, a, at], K.s_sb[:, i % 3, a, at], ACT.Exp,
                                                 bias=K.neg_max[:, 2 * i + a:2 * i + a + 1],
                                                 accum_out=K.sums[:, 2 * i + a:2 * i + a + 1])
                    e.then_inc(K.probs_ready.sem, 1)
                if 0 <= i - 2 < n and i % 2 == 0:
                    copy(act, i - 2)

        @block.vector
        def _(dve):
            ch = Chain(dve, K.dve_step)
            for i in range(n + 5):
                if i < n:
                    u = units[i]
                    w = u["size"]
                    dve.wait_ge(K.scores_ready.sem, sc0 + i + 1)
                    if i >= 3:
                        dve.wait_ge(K.probs_ready.sem, pr0 + i - 2)
                    s_sb = K.s_sb[:, i % 3, :, :]
                    if u["sink"] is not None:
                        nc.vector.tensor_copy(s_sb[:, :, w:w + 1],
                                              K.sinks[:, u["sink"]:u["sink"] + 2].unsqueeze(2))
                    ps = K.psum[:, i % 3, :].rearrange("p (a k) -> p a k", a=2)[:, :, 0:w]
                    ch.do(nc.vector.scalar_tensor_tensor(s_sb[:, :, 0:w], ps, HD ** -0.5,
                                                         u["mask"].unsqueeze(1).broadcast_to([P, 2, w]), ALU.mult,
                                                         ALU.add))
                    nc.vector.tensor_reduce(K.neg_max[:, 2 * i:2 * i + 2], s_sb[:, :, 0:columns(u)], AX.X, ALU.max,
                                            negate=True).then_inc(K.masked_scores.sem, 1)
                if 0 <= i - 1 < n and units[i - 1]["keep"] is not None:
                    dve.wait_ge(K.probs_ready.sem, pr0 + i)
                    w = units[i - 1]["size"]
                    p = K.probs[:, (i - 1) % 3, :, 0:w]
                    nc.vector.tensor_tensor(p, p, units[i - 1]["keep"].unsqueeze(1).broadcast_to([P, 2, w]),
                                            ALU.mult).then_inc(K.probs_kept.sem, 1)
                if 0 <= i - 2 < n and i % 2 == 1:
                    copy(dve, i - 2)
                if 0 <= i - 4 < n and (i - 4) % 4 == 3:
                    g = (i - 4) // 4
                    dve.wait_ge(K.values_ready.sem, va0 + i - 3)
                    at = slice(8 * g, 8 * g + 8)
                    groups[g](ch, K.psum[:, 5 + g % 3, :].rearrange("p (h d) -> p h d", d=HD),
                              K.sums[:, at]).then_inc(K.group_out.sem, 1)

    K.scores_ready.total += n
    K.masked_scores.total += n
    K.probs_ready.total += n
    K.probs_kept.total += kept(n)
    K.turned.total += n
    K.act_turned.total += (n + 1) // 2
    K.dve_turned.total += n // 2
    K.values_ready.total += n
    K.group_out.total += n // 4


def fox_gates(K):
    nc = K.nc
    H, G = FOX, K.gates
    with nc.Block(no_gpsimd_drain=True) as block:
        turned, v0, a0 = K.turned.total, K.gates_v.total, K.gates_a.total

        @block.tensor
        def _(pe):
            for t in range(TT):
                tr = nc.tensor.transpose(K.psum[0:H, 0, t * P:(t + 1) * P], K.u[:, t, FL:FL + H], K.ident[:, :])
            tr.then_inc(K.turned.sem, 1)

        @block.vector
        def _(dve):
            ch = Chain(dve, K.dve_step)
            dve.wait_ge(K.turned.sem, turned + 1)
            ch.do(nc.vector.tensor_scalar(G[:, 0, :], K.psum[0:H, 0, 0:SEQ], K.gate_bias[0:H, 2:3], None, ALU.add))
            nc.vector.scalar_tensor_tensor(G[:, 1, :], G[:, 0, :], -1.0, G[:, 0, :], ALU.mult,
                                           ALU.max).then_inc(K.gates_v.sem, 1)
            ch.do(nc.vector.tensor_scalar(G[:, 3, :], G[:, 0, :], 0.0, None, ALU.min))
            dve.wait_ge(K.gates_a.sem, a0 + 2)
            ch.do(nc.vector.tensor_tensor(G[:, 4, :], G[:, 3, :], G[:, 2, :], ALU.subtract))
            ch.do(nc.vector.tensor_tensor_scan(G[:, 5, :], K.ones[0:H, :], G[:, 4, :], 0.0, ALU.mult, ALU.add))
            nc.vector.tensor_scalar(G[:, 6, :], G[:, 5, :], -HD ** 0.5, None, ALU.mult)

        @block.scalar
        def _(act):
            act.wait_ge(K.gates_v.sem, v0 + 1)
            nc.scalar.activation(G[:, 7, :], G[:, 1, :], ACT.Exp, scale=-1.0).then_inc(K.gates_a.sem, 1)
            act.wait_ge(K.gates_a.sem, a0 + 1)
            nc.scalar.activation(G[:, 2, :], G[:, 7, :], ACT.Ln, bias=1.0).then_inc(K.gates_a.sem, 1)
    K.turned.total += 1
    K.gates_v.total += 1
    K.gates_a.total += 2


def normed_heads(K):
    nc = K.nc
    groups = [(QA, N_Q, 0), (KSL, N_KV, 1), (KWN, N_KV, 2), (QF, FOX, 3), (KF, FOX, 4)]
    total = sum(h for _, h, _ in groups)
    with nc.Block(no_gpsimd_drain=True) as block:
        sq0, st0, rs0 = K.square_ready.total, K.stat_ready.total, K.rstd_ready.total

        @block.scalar
        def _(act):
            for t in range(TT):
                nc.scalar.activation(K.squares[:, t, :], K.u[:, t, 0:VF], ACT.Square).then_inc(K.square_ready.sem, 1)

        @block.vector
        def _(dve):
            ch = Chain(dve, K.dve_step)

            def heads(buf, t, c, h):
                return buf[:, t, c:c + h * HD].rearrange("p (h d) -> p h d", d=HD)
            for t in range(TT):
                dve.wait_ge(K.square_ready.sem, sq0 + t + 1)
                at = 0
                for c, h, _ in groups:
                    ch.do(nc.vector.tensor_reduce(K.head_ms[:, t, 0, at:at + h], heads(K.squares, t, c, h), AX.X,
                                                  ALU.add))
                    at += h
                nc.vector.tensor_scalar(K.head_ms[:, t, 1, :], K.head_ms[:, t, 0, :], 1.0 / HD, RMS_EPS, ALU.mult,
                                        ALU.add).then_inc(K.stat_ready.sem, 1)
            for t in range(TT):
                rotate(K, ch, heads(K.u, t, KC, N_KV), 1, t)
                dve.wait_ge(K.rstd_ready.sem, rs0 + t + 1)
                at = 0
                for c, h, g in groups:
                    x = heads(K.u, t, c, h)
                    ch.do(nc.vector.tensor_tensor(x, x, K.head_ms[:, t, 2, at:at + h].unsqueeze(2).broadcast_to(
                        [P, h, HD]), ALU.mult))
                    ch.do(nc.vector.tensor_tensor(x, x, K.head_gain[:, g, :].unsqueeze(1).broadcast_to([P, h, HD]),
                                                  ALU.mult))
                    at += h
                    if g < 3:
                        rotate(K, ch, x, 1, t)

        @block.gpsimd
        def _(pool):
            for t in range(TT):
                pool.wait_ge(K.stat_ready.sem, st0 + t + 1)
                nc.gpsimd.tensor_tensor(K.head_ms[:, t, 2, :], K.head_ms[:, t, 1, :], K.minus_half[:, 0:total],
                                        ALU.pow).then_inc(K.rstd_ready.sem, 1)
            pool.wait_ge(K.rstd_ready.sem, rs0 + TT)

    K.square_ready.total += TT
    K.stat_ready.total += TT
    K.rstd_ready.total += TT


def compress(K):
    nc = K.nc
    first = K.next_load
    nb = N_KV * N_CMP
    JJ = CMP_BLOCK // 2
    with nc.Block(no_gpsimd_drain=True) as block:

        @block.sync
        def _(sp):
            for w in range(2):
                sp.dma_start(K.kc2[HD:P, w, :, 0:SEQ - 1], K.kc2[0:HD, w, :, 1:SEQ]).then_inc(K.shifted, 16)

        @block.vector
        def _(dve):
            dve.wait_ge(K.shifted, 32)
            for which, pos in ((0, K.col_of["pos_k"]), (1, K.col_of["pos_v"])):
                for h in range(N_KV):
                    tok = K.kc2[:, which, h, :].rearrange("p (n s) -> p s n", s=CMP_STRIDE)
                    for half in range(2):
                        js = slice(half * JJ // 2, (half + 1) * JJ // 2)
                        nc.vector.tensor_tensor(
                            K.blocks[:, which, js, h * N_CMP:(h + 1) * N_CMP],
                            tok[:, 0:CMP_STRIDE:2, half:half + N_CMP],
                            K.cols[:, pos + half * JJ // 2:pos + (half + 1) * JJ // 2].unsqueeze(2).broadcast_to(
                                [P, JJ // 2, N_CMP]), ALU.add)

    with nc.Block(no_gpsimd_drain=True) as block:
        f0, a0, t0, v0 = K.filled.total, K.act_took.total, K.turned.total, K.dve_took.total
        st0, rs0 = K.stat_ready.total, K.rstd_ready.total

        @block.sync
        def _(sp):
            refill(K, sp, first, [(K.filled.sem, f0 + 1), (K.filled.sem, f0 + 2), (K.filled.sem, f0 + 3)])

        @block.tensor
        def _(pe):
            for which in range(2):
                weights_here(K, pe, first + which)
                w1 = weight_views(K, first + which)[0]
                for j in range(JJ):
                    mm = nc.tensor.matmul(K.psum[0:nb, which, 0:CMP_HID], K.blocks[:, which, j, :], w1[:, j, :],
                                          start=(j == 0), stop=(j == JJ - 1))
                mm.then_inc(K.filled.sem, 1)
            for which in range(2):
                pe.wait_ge(K.act_took.sem, a0 + which + 1)
                for k in range(2):
                    tr = nc.tensor.transpose(K.psum[:, 2 + which, k * P:k * P + nb],
                                             K.cmp_hid[0:nb, which, k * P:(k + 1) * P], K.ident[0:nb, 0:nb])
                tr.then_inc(K.turned.sem, 1)
            weights_here(K, pe, first + 2)
            for which in range(2):
                pe.wait_ge(K.dve_took.sem, v0 + which + 1)
                w2 = weight_views(K, first + 2)[which]
                for h in range(N_KV):
                    for k in range(2):
                        mm = nc.tensor.matmul(K.psum[0:N_CMP, 4 + which, h * HD:(h + 1) * HD],
                                              K.cmp_hidT[:, which, k, h * N_CMP:(h + 1) * N_CMP], w2[:, k, :],
                                              start=(k == 0), stop=(k == 1))
            mm.then_inc(K.filled.sem, 1)
            pe.wait_ge(K.dve_took.sem, v0 + 3)
            for h in range(N_KV):
                tr = nc.tensor.transpose(K.psum[0:HD, 6, h * P:h * P + N_CMP], K.cmp_k[:, h, :],
                                         K.ident[0:N_CMP, 0:N_CMP])
            tr.then_inc(K.turned.sem, 1)

        @block.scalar
        def _(act):
            for which in range(2):
                act.wait_ge(K.filled.sem, f0 + which + 1)
                nc.scalar.activation(K.cmp_hid[0:nb, which, :], K.psum[0:nb, which, 0:CMP_HID],
                                     ACT.Silu).then_inc(K.act_took.sem, 1)
            act.wait_ge(K.filled.sem, f0 + 3)
            nc.scalar.activation(K.cmp_v[:, :, :], K.psum[0:N_CMP, 5, 0:N_KV * HD].rearrange(
                "p (h d) -> p h d", d=HD), ACT.Copy)

        @block.vector
        def _(dve):
            ch = Chain(dve, K.dve_step)
            for which in range(2):
                dve.wait_ge(K.turned.sem, t0 + which + 1)
                nc.vector.tensor_copy(K.cmp_hidT[:, which, :, :], K.psum[:, 2 + which, 0:2 * P].rearrange(
                    "p (k n) -> p k n", k=2)[:, :, 0:nb]).then_inc(K.dve_took.sem, 1)
            dve.wait_ge(K.filled.sem, f0 + 3)
            k = K.cmp_k
            ch.do(nc.vector.tensor_copy(k[:, :, :], K.psum[0:N_CMP, 4, 0:N_KV * HD].rearrange(
                "p (h d) -> p h d", d=HD)))
            ch.do(nc.vector.tensor_tensor(K.cmp_sq[:, :, :], k[:, :, :], k[:, :, :], ALU.mult))
            ch.do(nc.vector.tensor_reduce(K.stat[0:N_CMP, 0, 0:N_KV], K.cmp_sq[:, :, :], AX.X, ALU.add))
            nc.vector.tensor_scalar(K.stat[0:N_CMP, 0, 2:4], K.stat[0:N_CMP, 0, 0:N_KV], 1.0 / HD, RMS_EPS, ALU.mult,
                                    ALU.add).then_inc(K.stat_ready.sem, 1)
            dve.wait_ge(K.rstd_ready.sem, rs0 + 1)
            ch.do(nc.vector.tensor_tensor(k[:, :, :], k[:, :, :], K.stat[0:N_CMP, 0, 4:6].unsqueeze(2).broadcast_to(
                [N_CMP, N_KV, HD]), ALU.mult))
            nc.vector.tensor_tensor(k[:, :, :], k[:, :, :], K.head_gain[0:N_CMP, 5, :].unsqueeze(1).broadcast_to(
                [N_CMP, N_KV, HD]), ALU.mult).then_inc(K.dve_took.sem, 1)
            dve.wait_ge(K.turned.sem, t0 + 3)
            nc.vector.tensor_copy(K.cmp_kT[:, :, :], K.psum[0:HD, 6, 0:2 * P].rearrange(
                "p (h n) -> p h n", h=2)[:, :, 0:N_CMP])

        @block.gpsimd
        def _(pool):
            pool.wait_ge(K.stat_ready.sem, st0 + 1)
            nc.gpsimd.tensor_tensor(K.stat[0:N_CMP, 0, 4:6], K.stat[0:N_CMP, 0, 2:4], K.minus_half[0:N_CMP, 0:2],
                                    ALU.pow).then_inc(K.rstd_ready.sem, 1)
            pool.wait_ge(K.rstd_ready.sem, rs0 + 1)

    K.filled.total += 3
    K.act_took.total += 2
    K.turned.total += 3
    K.dve_took.total += 3
    K.stat_ready.total += 1
    K.rstd_ready.total += 1
    K.next_load += 3


def stationary(xT):
    return lambda k, t: xT[:, k, t * P:(t + 1) * P]


def embed(K, p, gate_bias_row, normed_row):
    nc = K.nc
    with nc.Block(no_gpsimd_drain=True) as block:

        @block.sync
        def _(sp):
            K.p_loads += 1
            sp.dma_start(K.p[:, :, :], p.rearrange("(t p) d -> p t d", p=P)).then_inc(K.p_loaded, 16)
            sp.wait_ge(K.p_loaded, 16 * K.p_loads)
    turn(K, [([K.p[:, t, k * P:(k + 1) * P] for t in range(TT)], K.pT[:, k, :], None) for k in range(PLE // P)])
    gate = K.scratch
    halves = [(stationary(K.xT), 0, 0, BANK)]

    def take_gate(eng, item, t, ps):
        s = slice(item * BANK, (item + 1) * BANK)
        if gate_bias_row is None:
            return nc.scalar.activation(gate[:, t, s], ps, ACT.Sigmoid)
        return nc.vector.tensor_tensor(gate[:, t, s], ps, K.rows[:, gate_bias_row, s], ALU.add)

    if gate_bias_row is not None:
        with nc.Block(no_gpsimd_drain=True) as block:
            @block.vector
            def _(dve):
                row_here(K, dve, gate_bias_row)
    project(K, [halves, halves], lambda n, t: "act" if gate_bias_row is None else "dve", take_gate)
    if gate_bias_row is not None:
        with nc.Block(no_gpsimd_drain=True) as block:
            @block.scalar
            def _(act):
                for t in range(TT):
                    nc.scalar.activation(gate[:, t, :], gate[:, t, :], ACT.Sigmoid)
    proj = [(stationary(K.pT), 0, h * BANK, (h + 1) * BANK) for h in range(2)]

    def take_proj(eng, item, t, ps):
        s = slice(item * BANK, (item + 1) * BANK)
        if normed_row is None:
            return nc.vector.tensor_tensor(K.z[:, t, s], ps, gate[:, t, s], ALU.mult)
        return nc.scalar.activation(K.z[:, t, s], ps, ACT.Copy)
    project(K, [proj], lambda n, t: "dve" if normed_row is None else "act", take_proj)
    if normed_row is not None:
        keep = K.scratch
        K.scratch = K.hid_flat
        root_norm(K, K.z, [(0, D)], K.z)
        K.scratch = keep
    with nc.Block(no_gpsimd_drain=True) as block:

        @block.vector
        def _(dve):
            ch = Chain(dve, K.dve_step)
            if normed_row is not None:
                row_here(K, dve, normed_row)
            for t in range(TT):
                if normed_row is not None:
                    ch.do(nc.vector.tensor_tensor(K.z[:, t, :], K.z[:, t, :], K.rows[:, normed_row, :], ALU.mult))
                    ch.do(nc.vector.tensor_tensor(K.z[:, t, :], K.z[:, t, :], gate[:, t, :], ALU.mult))
                nc.vector.tensor_tensor(K.x[:, t, :], K.x[:, t, :], K.z[:, t, :], ALU.add)


def build(nc, a, out, stop=99):
    K = Kit()
    K.nc = nc
    with ExitStack() as ctx:
        def sb(name, shape, dt=F32):
            return ctx.enter_context(nc.sbuf_tensor(name, shape, dt))

        def sem(name):
            return ctx.enter_context(nc.semaphore(name))

        K.ring = sb("ring", [P, SLOTS, SLOT])
        K.x = sb("x", [P, TT, D])
        K.xT = sb("xT", [P, KT, SEQ])
        K.z = sb("z", [P, TT, D])
        K.rows = sb("rows", [P, 6, D])
        K.psum = ctx.enter_context(nc.psum_tensor("psum", [P, NBANK, BANK], F32))
        K.ident = sb("ident", [P, P])
        K.sel = sb("sel", [FOX, FOX, P])
        K.ones = sb("ones", [P, SEQ])
        K.minus_half = sb("minus_half", [P, 32])
        K.causal = sb("causal", [P, SEQ])
        K.window = sb("window", [P, SEQ])
        K.causal_t = sb("causal_t", [P, 3 * P])
        K.cmp_mask = sb("cmp_mask", [P, TT, N_CMP])
        K.cmp_keep = sb("cmp_keep", [P, TT, N_CMP])
        K.inv_freq = sb("inv_freq", [P, HALF])
        K.cols = sb("cols", [P, 80])
        K.positions = sb("positions", [P, TT], I32)
        K.index = sb("index", [P, TT], I32)
        K.pos_f = sb("pos_f", [P, 2 * TT])
        K.angle = sb("angle", [P, 5, 2 * TT * HALF])
        K.cos_sin = sb("cos_sin", [P, 2, 2 * TT * HALF])
        K.rot = sb("rot", [P, 4, A_Q_HEADS, HALF])
        K.gate_bias = sb("gate_bias", [P, 3])
        K.sinks = sb("sinks", [P, A_Q_HEADS])
        K.head_gain = sb("head_gain", [P, 6, HD])
        K.stat = sb("stat", [P, TT, 6])
        K.bn = sb("bn", [P, TT, 2, 6])
        K.bn8 = sb("bn8", [P, TT * M_HEADS, 6])
        K.mean_var = sb("mean_var", [P, TT * M_HEADS, 2])
        K.mstat = sb("mstat", [P, 5, TT * M_HEADS])
        K.u_col = sb("u_col", [P, TT * M_HEADS])
        K.exp_m = sb("exp_m", [P, TT * M_HEADS])
        K.neg_max = sb("neg_max", [P, 64])
        K.sums = sb("sums", [P, 64])
        K.recip = sb("recip", [P, 8])
        K.head_ms = sb("head_ms", [P, TT, 3, 28])
        arena = sb("arena", [P, ARENA])

        def cut(at, rows, *shape):
            n = int(np.prod(shape))
            assert at + n <= ARENA, (at, n)
            view = arena[0:rows, at:at + n]
            names = "abcd"[:len(shape)]
            return view.rearrange(f"p ({' '.join(names)}) -> p {' '.join(names)}",
                                  **dict(zip(names, shape))) if len(shape) > 1 else view

        K.hid = cut(0, P, 2, TT, 512)
        K.hid_flat = cut(0, P, TT, D)
        K.rel = cut(2048, P, TT, 512)
        K.hidT = cut(3072, P, 2, 4, SEQ)
        K.scratch = cut(5120, P, TT, D)
        K.p = cut(7168, P, TT, PLE)
        K.pT = cut(7680, P, PLE // P, SEQ)
        U = 3080 * TT
        K.u = cut(0, P, TT, 3080)
        K.qkT = cut(U, P, 2 * M_HEADS, SEQ)
        K.v_ext = cut(U + 2048, P, TT, M_HEADS, M_DV + 1)
        K.h_raw = cut(U + 2048 + 2056, P, TT, M_HEADS, M_DV + 1)
        at = U + 2048 + 2 * 2056
        K.exponent = cut(at, P, 2, 3 * P)
        K.decay = cut(at + 768, P, 2, 3 * P)
        K.decayed = cut(at + 1536, P, 2, 3 * P)
        K.gates = sb("gates", [FOX, 8, SEQ])
        SK = SEQ + 8
        K.s_sb = cut(U, P, 3, 2, SK)
        K.probs = cut(U + 1584, P, 3, 2, SK)
        K.probsT = cut(U + 3168, P, 2, 512)
        K.attT = cut(U + 4192, HD, 28, SEQ)
        K.kc2 = K.z[:, :, :].rearrange("p t (h n) -> p t h n", n=SEQ)[:, :, 0:N_KV, :]
        K.group_tmp = K.rows[:, 3, 0:512]
        K.squares = cut(U, P, TT, VF)
        K.blocks = K.xT[:, :, :].rearrange("p k n -> p (k n)")[:, 0:2 * 16 * N_KV * N_CMP].rearrange(
            "p (w j n) -> p w j n", w=2, j=16)
        small = K.rows[:, 5, :]
        nb = N_KV * N_CMP
        K.cmp_hid = small[:, 0:512].rearrange("p (w n) -> p w n", w=2)
        K.cmp_hidT = small[:, 512:512 + 4 * nb].rearrange("p (w k n) -> p w k n", w=2, k=2)
        K.cmp_k = small[0:N_CMP, 640:768].rearrange("p (h d) -> p h d", d=HD)
        K.cmp_sq = small[0:N_CMP, 768:896].rearrange("p (h d) -> p h d", d=HD)
        K.cmp_v = K.rows[0:N_CMP, 4, 0:128].rearrange("p (h d) -> p h d", d=HD)
        K.cmp_kT = K.rows[0:HD, 4, 128:128 + nb].rearrange("p (h n) -> p h n", h=N_KV)

        K.turned = Signal(sem("turned"))
        K.act_took = Signal(sem("act_took"))
        K.dve_took = Signal(sem("dve_took"))
        K.filled = Signal(sem("filled"))
        K.hidden_ready = Signal(sem("hidden_ready"))
        K.down_done = Signal(sem("down_done"))
        K.act_turned = Signal(sem("act_turned"))
        K.dve_turned = Signal(sem("dve_turned"))
        K.stat_ready = Signal(sem("stat_ready"))
        K.rstd_ready = Signal(sem("rstd_ready"))
        K.hat_ready = Signal(sem("hat_ready"))
        K.square_ready = Signal(sem("square_ready"))
        K.dve_step = Signal(sem("dve_step"))
        K.angle_ready = Signal(sem("angle_ready"))
        K.gates_v = Signal(sem("gates_v"))
        K.gates_a = Signal(sem("gates_a"))
        K.scores_ready = Signal(sem("scores_ready"))
        K.masked_scores = Signal(sem("masked_scores"))
        K.probs_ready = Signal(sem("probs_ready"))
        K.probs_kept = Signal(sem("probs_kept"))
        K.weights_ready = Signal(sem("weights_ready"))
        K.values_ready = Signal(sem("values_ready"))
        K.group_out = Signal(sem("group_out"))
        K.slot_loaded = [sem(f"slot_loaded{i}") for i in range(SLOTS)]
        K.row_loaded = [sem(f"row_loaded{i}") for i in range(6)]
        K.row_loads = [0] * 6
        K.input_loaded = sem("input_loaded")
        K.small_loaded = sem("small_loaded")
        K.zeroed = sem("zeroed")
        K.masked = sem("masked")
        K.shifted = sem("shifted")
        K.p_loaded = sem("p_loaded")
        K.stored = sem("stored")
        K.masked_total, K.p_loads, K.next_load = 0, 0, 0
        K.loads = plan_weights(a)

        def done(level):
            if stop <= level:
                store(K, out)
                return True
            return False

        setup(K, a)
        rows_stage(K, {0: a["mix_ln_g"][0], 1: a["mix_ln_b"][0], 2: a["mlp_ln_g"][0], 3: a["mlp_ln_b"][0],
                       4: a["ple_b_gate"][0]})
        full = [(stationary(K.xT), 0, 0, BANK)]

        def take_mlstm(eng, item, t, ps):
            if item in (2, 3):
                dst = K.v_ext[:, t, 2 * (item - 2):2 * (item - 1), 0:M_DV]
                ps = ps.rearrange("p (h d) -> p h d", d=M_DV)
            else:
                dst = K.u[:, t, item * BANK:item * BANK + ps.shape[1]]
            if item in (4, 5):
                return nc.scalar.activation(dst, ps, ACT.Sigmoid)
            return nc.scalar.activation(dst, ps, ACT.Copy) if t == 0 else nc.vector.tensor_copy(dst, ps)
        project(K, [full] * 6 + [[(stationary(K.xT), 0, 0, 8)]], lambda n, t: "act" if t == 0 or n in (4, 5) else "dve",
                take_mlstm)
        turn(K, [([K.u[:, t, k * P:(k + 1) * P] for t in range(TT)], K.qkT[:, k, :], None) for k in range(8)])
        gate_columns(K)
        mlstm(K)
        mlstm_norm(K)
        turn_model(K, K.z, K.col_of["head_g"])
        if done(0):
            return
        model_product(K)
        residual_norm(K, 0, 1)
        if done(1):
            return
        turn_model(K, K.x)
        feed_forward(K, D_FF // 512, 512, False)
        residual_norm(K, 2, 3)
        if done(2):
            return
        turn_model(K, K.x)
        embed(K, a["p"][0, 0], 4, None)
        if done(3):
            return
        turn_model(K, K.x)
        rows_stage(K, {0: a["kv_b"], 1: a["b_b_q"][0], 2: a["b_b_o"][0], 3: a["mix_ln_g"][1], 4: a["mix_ln_b"][1]})

        def take_qkv(eng, item, t, ps):
            at = (A_Q_HEADS * HD, 0, BANK)[item]
            row, r0 = ((0, 0), (1, 0), (1, BANK))[item]
            return nc.vector.tensor_tensor(K.u[:, t, at:at + BANK], ps, K.rows[:, row, r0:r0 + BANK], ALU.add)
        with nc.Block(no_gpsimd_drain=True) as block:
            @block.vector
            def _(dve):
                row_here(K, dve, 0)
                row_here(K, dve, 1)
        project(K, [full] * 3, lambda n, t: "dve", take_qkv)
        nqk = A_Q_HEADS + A_KV_HEADS
        with nc.Block(no_gpsimd_drain=True) as block:
            @block.vector
            def _(dve):
                ch = Chain(dve, K.dve_step)
                for t in range(TT):
                    for h0, h in ((0, A_Q_HEADS), (A_Q_HEADS, A_KV_HEADS)):
                        rotate(K, ch, K.u[:, t, h0 * HD:(h0 + h) * HD].rearrange("p (h d) -> p h d", d=HD), 0, t)
        turn(K, [([K.u[:, t, h * HD:(h + 1) * HD] for t in range(TT)], K.attT[:, h, :], None) for h in range(nqk)])
        units, groups = [], []
        for t in range(TT):
            size = (t + 1) * P
            for g in range(A_Q_HEADS // 8):
                for pair in range(4):
                    h = 8 * g + 2 * pair
                    kv = h // (A_Q_HEADS // A_KV_HEADS)
                    vals = [K.u[:, s, (nqk + kv) * HD:(nqk + kv + 1) * HD] for s in range(t + 1)]
                    units.append(dict(q=[K.attT[:, h + i, t * P:(t + 1) * P] for i in range(2)],
                                      k=[K.attT[:, A_Q_HEADS + kv, 0:size]] * 2, size=size, bias=None, keep=None,
                                      mask=K.causal[:, P:SEQ] if t == 0 else K.window[:, :], sink=h, v=[vals] * 2))
                groups.append(divided(K, K.z[:, t, g * 512:(g + 1) * 512]))
        attend(K, units, groups)
        turn_model(K, K.z)
        model_product(K)
        residual_norm(K, 3, 4, bias=2)
        if done(4):
            return
        turn_model(K, K.x)
        rows_stage(K, {0: a["mlp_ln_g"][1], 1: a["mlp_ln_b"][1], 2: a["ple_b_gate"][1]})
        feed_forward(K, D_FF // 512, 512, False)
        residual_norm(K, 0, 1)
        if done(5):
            return
        turn_model(K, K.x)
        embed(K, a["p"][1, 0], 2, None)
        if done(6):
            return
        root_norm(K, K.x, [(0, D)], K.z)
        turn_model(K, K.z, K.col_of["ffn1"])
        feed_forward(K, D_FF_2 // 256, 256, True)
        half_step(K)
        if done(7):
            return
        root_norm(K, K.x, [(0, D)], K.z)
        turn_model(K, K.z, K.col_of["mix"])

        def take_in2(eng, item, t, ps):
            n0, n1 = IN2_CHUNKS[item]
            dst = K.u[:, t, n0:n1]
            return nc.scalar.activation(dst, ps, ACT.Copy) if t == 0 else nc.vector.tensor_copy(dst, ps)
        project(K, [[(stationary(K.xT), 0, 0, n1 - n0)] for n0, n1 in IN2_CHUNKS],
                lambda n, t: "act" if t == 0 else "dve", take_in2)
        fox_gates(K)
        normed_heads(K)
        order = [(QA, N_Q), (KSL, N_KV), (KWN, N_KV), (QF, FOX), (KF, FOX)]
        base, items, at = {}, [], 0
        for c, n in order:
            base[c] = at
            items += [([K.u[:, t, c + h * HD:c + (h + 1) * HD] for t in range(TT)], K.attT[:, at + h, :], None)
                      for h in range(n)]
            at += n
        for w, c in enumerate((KC, VC)):
            items += [([K.u[:, t, c + h * HD:c + (h + 1) * HD] for t in range(TT)], K.kc2[0:HD, w, h, :], None)
                      for h in range(N_KV)]
        turn(K, items)
        compress(K)
        with nc.Block(no_gpsimd_drain=True) as block:
            @block.scalar
            def _(act):
                for t in range(TT):
                    nc.scalar.activation(K.u[:, t, GA:QF], K.u[:, t, GA:QF], ACT.Sigmoid)
        units, groups = [], []
        for t in range(TT):
            tok = slice(t * P, (t + 1) * P)
            size = (t + 1) * P
            causal = K.causal[:, P:SEQ] if t == 0 else K.causal[:, :]
            for kind in ("cmp", "slc", "win", "fox"):
                for pair in range(4):
                    h = 2 * pair
                    kv = h // (N_Q // N_KV)
                    if kind == "fox":
                        u = dict(q=[K.attT[:, base[QF] + h + i, tok] for i in range(2)],
                                 k=[K.attT[:, base[KF] + h + i, 0:size] for i in range(2)], size=size,
                                 bias=[(K.sel[:, h + i, :], K.gates[:, 6, 0:size]) for i in range(2)], keep=None,
                                 v=[[K.u[:, s, VF + (h + i) * HD:VF + (h + i + 1) * HD] for s in range(t + 1)]
                                    for i in range(2)], mask=causal)
                    elif kind == "cmp":
                        u = dict(k=[K.cmp_kT[:, kv, :]] * 2, size=N_CMP, bias=None, keep=K.cmp_keep[:, t, :],
                                 v=[[K.cmp_v[:, kv, :]]] * 2, mask=K.cmp_mask[:, t, :])
                    else:
                        kc, vc = (KSL, VSL) if kind == "slc" else (KWN, VWN)
                        u = dict(k=[K.attT[:, base[kc] + kv, 0:size]] * 2, size=size, bias=None, keep=None,
                                 v=[[K.u[:, s, vc + kv * HD:vc + (kv + 1) * HD] for s in range(t + 1)]] * 2,
                                 mask=causal)
                    if kind != "fox":
                        u["q"] = [K.attT[:, base[QA] + h + i, tok] for i in range(2)]
                    u["sink"] = None
                    units.append(u)
        groups = []
        for t in range(TT):
            gate = K.u[:, t, GA:QF].rearrange("p (h c) -> p h c", c=3)
            for c in range(3):
                groups.append(divided(K, K.z[:, t, 0:512], gate=gate[:, :, c], add=c > 0))
            groups.append(divided(K, K.z[:, t, 512:1024]))
        attend(K, units, groups)
        root_norm(K, K.z, [(0, 512), (512, 1024)], K.z)
        turn_model(K, K.z, K.col_of["out_nsa"])
        model_product(K)
        with nc.Block(no_gpsimd_drain=True) as block:
            @block.vector
            def _(dve):
                for t in range(TT):
                    for h in range(2):
                        s = slice(h * BANK, (h + 1) * BANK)
                        nc.vector.tensor_tensor(K.x[:, t, s], K.psum[:, 2 * t + h, :], K.x[:, t, s], ALU.add)
        if done(8):
            return
        root_norm(K, K.x, [(0, D)], K.z)
        turn_model(K, K.z, K.col_of["ffn2"])
        rows_stage(K, {0: a["ple_norm_2"][0]})
        feed_forward(K, D_FF_2 // 256, 256, True)
        half_step(K)
        if done(9):
            return
        root_norm(K, K.x, [(0, D)], K.z)
        turn_model(K, K.z, K.col_of["ple"])
        embed(K, a["p_2"][0, 0], None, 0)
        store(K, out)


ARENA = 17520


def divided(K, dst, gate=None, add=False):
    nc = K.nc
    d = dst.rearrange("p (h d) -> p h d", d=HD)

    def run(ch, outputs, sums):
        ch.do(nc.vector.reciprocal(K.recip[:, :], sums))
        if gate is not None:
            ch.do(nc.vector.tensor_tensor(K.recip[:, :], K.recip[:, :], gate, ALU.mult))
        r = K.recip[:, :].unsqueeze(2).broadcast_to([P, 8, HD])
        if not add:
            return nc.vector.tensor_tensor(d, outputs, r, ALU.mult)
        tmp = K.group_tmp[:, :].rearrange("p (h d) -> p h d", d=HD)
        ch.do(nc.vector.tensor_tensor(tmp, outputs, r, ALU.mult))
        return nc.vector.tensor_tensor(d, d, tmp, ALU.add)
    return run


def model_product(K):
    nc = K.nc
    first = K.next_load
    with nc.Block(no_gpsimd_drain=True) as block:
        f0 = K.filled.total

        @block.sync
        def _(sp):
            refill(K, sp, first, [(K.filled.sem, f0 + 1), (K.filled.sem, f0 + 2)])

        @block.tensor
        def _(pe):
            for h in range(2):
                weights_here(K, pe, first + h)
                w = weight_views(K, first + h)[0]
                for t in range(TT):
                    for k in range(KT):
                        mm = nc.tensor.matmul(K.psum[:, 2 * t + h, :], K.xT[:, k, t * P:(t + 1) * P], w[:, k, :],
                                              start=(k == 0), stop=(k == KT - 1))
                mm.then_inc(K.filled.sem, 1)
    K.filled.total += 2
    K.next_load += 2


def store(K, out):
    with K.nc.Block(no_gpsimd_drain=True) as block:

        @block.sync
        def _(sp):
            sp.dma_start(out[0].rearrange("(t p) d -> p t d", p=P), K.x[:, :, :]).then_inc(K.stored, 16)
            sp.wait_ge(K.stored, 16)


STOP = 99


def kernel(**inputs):
    import concourse.bacc as bacc
    from concourse.bass_utils import run_bass_kernel_spmd

    nc = bacc.Bacc("TRN2", target_bir_lowering=False, num_devices=1)
    arrays, aps = {}, {}
    for name, value in inputs.items():
        v = np.ascontiguousarray(value)
        arrays[f"in_{name}"] = v
        aps[name] = nc.dram_tensor(f"in_{name}", v.shape, mybir.dt.from_np(v.dtype), kind="ExternalInput").ap()
    out = nc.dram_tensor("out", (1, SEQ, D), F32, kind="ExternalOutput").ap()
    build(nc, aps, out, STOP)
    return run_bass_kernel_spmd(nc, [arrays], core_ids=[0]).results[0]["out"]
```

```python
import math
from contextlib import ExitStack

import numpy as np

import concourse.bass as bass
from concourse import mybir

F32 = mybir.dt.float32
F32R = mybir.dt.float32r
I32 = mybir.dt.int32
ALU = mybir.AluOpType
ACT = mybir.ActivationFunctionType
AX = mybir.AxisListType

P = 128
SEQ = 256
TT = SEQ // P
D = 1024
KT = D // P
BANK = 512
NBANK = 8
DEPTH = 2
ALPHA = (2 * DEPTH) ** 0.25
LN_EPS = 1e-5
RMS_EPS = 1e-6
NEG = -1e30

M_HEADS, M_DK, M_DV, GATE_CAP = 4, 128, 256, 15.0
HD = 64
A_Q_HEADS, A_KV_HEADS = 16, 4
ROT, THETA = HD // 4, 500000.0
HALF = ROT // 2
PLE = 256
D_FF, D_FF_2 = 4096, 2816
N_Q, N_KV, FOX = 8, 2, 8
QA, KC, VC, KSL, KWN, QF, KF, QW = 0, 512, 640, 768, 896, 1024, 1536, 2048
VSL, VWN, GA, VF, FL, VW = 0, 128, 256, 280, 792, 800
IN2_CHUNKS = [
    (0, 512, [("q", QA, KC, 0)]),
    (512, 1024, [("q", KC, KWN, 0), ("v", VSL, VWN, 384)]),
    (1024, 1304, [("q", KWN, QF, 0), ("v", VWN, VF, 128)]),
    (1304, 1816, [("q", QF, KF, 0)]),
    (1816, 2328, [("q", KF, QW, 0)]),
    (2328, 2840, [("v", VF, FL, 0)]),
    (2840, 2848, [("v", FL, VW, 0)]),
]
CMP_BLOCK, CMP_STRIDE, CMP_HID = 32, 16, 256
N_CMP = (SEQ - CMP_BLOCK) // CMP_STRIDE + 1

SLOT = 2048
SLOTS = 4
PARTS = 3
AHEAD = PARTS - 1


class Signal:

    def __init__(self, sem):
        self.sem, self.total = sem, 0


class Chain:

    def __init__(self, eng, steps):
        self.eng, self.steps = eng, steps

    def do(self, ins):
        self.steps.total += 1
        ins.then_inc(self.steps.sem, 1)
        self.eng.wait_ge(self.steps.sem, self.steps.total)


def shares(owners):
    seen, out = {}, []
    for o in owners:
        seen[o] = seen.get(o, 0) + 1
        out.append(seen[o])
    return out


class Kit:
    pass


def rows_of(w):
    return w.rearrange("(k p) n -> p k n", p=P)


def plan_weights(a):
    loads = []

    def load(*pieces):
        assert sum(p.shape[1] * p.shape[2] for p in pieces) <= SLOT
        loads.append(list(pieces))

    def cols(w, n0, n1):
        v = rows_of(w)[:, :, n0:n1]
        n = loads_of(v.shape[1], n1 - n0)
        for i in range(n):
            load(v[:, i * v.shape[1] // n:(i + 1) * v.shape[1] // n, :])

    def mlp(up, down, hid, width):
        def piece_up(c):
            for i in range(2):
                load(*[rows_of(w)[:, i * KT // 2:(i + 1) * KT // 2, c * width:(c + 1) * width] for w in up])

        def piece_down(c):
            cols(down[c * width:(c + 1) * width, :], 0, D)
        n = hid // width
        piece_up(0)
        for c in range(n):
            if c + 1 < n:
                piece_up(c + 1)
            piece_down(c)

    def ple(gate, proj):
        for c in range(2):
            cols(gate, c * BANK, (c + 1) * BANK)
        cols(proj, 0, D)

    for n0 in range(0, 3072, BANK):
        cols(a["a_w_in"][0], n0, n0 + BANK)
    cols(a["a_w_in"][0], 3072, 3080)
    for c in range(2):
        cols(a["a_w_out"][0], c * BANK, (c + 1) * BANK)
    mlp([a["mlp_w_up"][0]], a["mlp_w_down"][0], D_FF, 512)
    ple(a["ple_w_gate"][0], a["ple_w_proj"][0])
    cols(a["kv_w"], 0, BANK)
    for c in range(2):
        cols(a["b_w_q"][0], c * BANK, (c + 1) * BANK)
    for c in range(2):
        cols(a["b_w_o"][0], c * BANK, (c + 1) * BANK)
    mlp([a["mlp_w_up"][1]], a["mlp_w_down"][1], D_FF, 512)
    ple(a["ple_w_gate"][1], a["ple_w_proj"][1])
    mlp([a["ffn1_wg_2"][0], a["ffn1_wu_2"][0]], a["ffn1_wd_2"][0], D_FF_2, 256)
    for n0, n1, _ in IN2_CHUNKS:
        cols(a["w_in_2"][0], n0, n1)
    cols(a["cmp_k_w1_2"][0], 0, CMP_HID)
    cols(a["cmp_v_w1_2"][0], 0, CMP_HID)
    load(rows_of(a["cmp_k_w2_2"][0]), rows_of(a["cmp_v_w2_2"][0]))
    for c in range(2):
        cols(a["w_out_2"][0], c * BANK, (c + 1) * BANK)
    mlp([a["ffn2_wg_2"][0], a["ffn2_wu_2"][0]], a["ffn2_wd_2"][0], D_FF_2, 256)
    ple(a["ple_w_gate_2"][0], a["ple_w_proj_2"][0])
    return loads


def loads_of(k, n):
    return 1 if k * n <= SLOT else 2


def pieces_in(K, n, slot):
    out, at = [], 0
    for src in K.loads[n]:
        k, w = src.shape[1], src.shape[2]
        out.append(slot[:, at:at + k * w].rearrange("p (k n) -> p k n", k=k))
        at += k * w
    return out


def weight_parts(K, n):
    return list(zip(pieces_in(K, n, K.wh[:, n % PARTS, :]), pieces_in(K, n, K.wl[:, n % PARTS, :])))


def load_weights(K, sp, n):
    if n < len(K.loads):
        for dst, src in zip(pieces_in(K, n, K.ring[:, n % SLOTS, :]), K.loads[n]):
            sp.dma_start(dst, src).then_inc(K.slot_loaded[n % SLOTS], 16)


def load_size(K, n):
    return sum(p.shape[1] * p.shape[2] for p in K.loads[n])


def split_high(K, act, n):
    if n < len(K.loads):
        act.wait_ge(K.slot_loaded[n % SLOTS], 16 * sum(len(K.loads[m]) for m in range(n % SLOTS, n + 1, SLOTS)))
        if n >= PARTS:
            act.wait_ge(K.load_used, n - PARTS + 1)
        w = load_size(K, n)
        K.nc.scalar.activation(K.wh[:, n % PARTS, 0:w], K.ring[:, n % SLOTS, 0:w], ACT.Copy).then_inc(K.high_ready, 1)


def split_low(K, dve, n):
    if n < len(K.loads):
        dve.wait_ge(K.high_ready, n + 1)
        w = load_size(K, n)
        K.nc.vector.tensor_tensor(K.wl[:, n % PARTS, 0:w], K.ring[:, n % SLOTS, 0:w],
                                  K.wh[:, n % PARTS, 0:w].bitcast(F32), ALU.subtract).then_inc(K.low_ready, 1)


def split_ahead(K, eng, name, n):
    (split_high if name == "act" else split_low)(K, eng, n + AHEAD)


def weights_here(K, pe, n):
    pe.wait_ge(K.low_ready, n + 1)


def product(K, out, x, w, start, stop):
    nc = K.nc
    nc.tensor.matmul(out, x[0], w[0], start=start, stop=False)
    nc.tensor.matmul(out, x[0], w[1], start=False, stop=False)
    return nc.tensor.matmul(out, x[1], w[0], start=False, stop=stop)


def refill(K, sp, first, count):
    for n in range(first + AHEAD, first + AHEAD + count):
        if n < len(K.loads):
            sp.wait_ge(K.low_ready, n + 1)
            load_weights(K, sp, n + SLOTS)


def bank(K, b, rows=P):
    return K.psum[0:rows, b, :]


def turn(K, items):
    nc = K.nc
    with nc.Block(no_gpsimd_drain=True) as block:
        turned, taken = K.turned.total, {"act": K.act_took.total, "dve": K.dve_took.total}
        who = ["act" if i % 2 == 0 else "dve" for i in range(len(items))]
        nth = shares(who)

        @block.tensor
        def _(pe):
            for i, (srcs, dst, scale) in enumerate(items):
                if i >= NBANK:
                    j = i - NBANK
                    pe.wait_ge((K.act_took if who[j] == "act" else K.dve_took).sem, taken[who[j]] + nth[j])
                for t, src in enumerate(srcs):
                    last = nc.tensor.transpose(K.psum[0:dst.shape[0], i % NBANK, t * src.shape[0]:(t + 1) * src.shape[0]],
                                               src, K.ident[0:src.shape[0], 0:src.shape[0]])
                last.then_inc(K.turned.sem, 1)

        def copy(eng, i):
            srcs, dst, scale = items[i]
            ps = K.psum[0:dst.shape[0], i % NBANK, 0:len(srcs) * srcs[0].shape[0]]
            eng.wait_ge(K.turned.sem, turned + i + 1)
            if who[i] == "act":
                if scale is None:
                    nc.scalar.activation(dst, ps, ACT.Copy).then_inc(K.act_took.sem, 1)
                else:
                    nc.scalar.activation(dst, ps, ACT.Copy, scale=scale).then_inc(K.act_took.sem, 1)
            elif scale is None:
                nc.vector.tensor_copy(dst, ps).then_inc(K.dve_took.sem, 1)
            else:
                nc.vector.tensor_scalar(dst, ps, scale, None, ALU.mult).then_inc(K.dve_took.sem, 1)

        @block.scalar
        def _(act):
            for i in range(0, len(items), 2):
                copy(act, i)

        @block.vector
        def _(dve):
            for i in range(1, len(items), 2):
                copy(dve, i)

    K.turned.total += len(items)
    K.act_took.total += who.count("act")
    K.dve_took.total += who.count("dve")


def turn_parts(K, items):
    nc = K.nc
    with nc.Block(no_gpsimd_drain=True) as block:
        turned, high0, low0 = K.turned.total, K.high_turned.total, K.low_turned.total

        @block.tensor
        def _(pe):
            for i, (srcs, dst, scale) in enumerate(items):
                if i >= NBANK:
                    pe.wait_ge(K.low_turned.sem, low0 + i - NBANK + 1)
                for t, src in enumerate(srcs):
                    p, w = src.shape
                    last = nc.tensor.transpose(K.psum[0:w, i % NBANK, t * p:(t + 1) * p], src, K.ident[0:p, 0:p])
                last.then_inc(K.turned.sem, 1)

        def bank_of(i):
            srcs = items[i][0]
            return K.psum[0:srcs[0].shape[1], i % NBANK, 0:len(srcs) * srcs[0].shape[0]]

        @block.scalar
        def _(act):
            for i, (srcs, dst, scale) in enumerate(items):
                act.wait_ge(K.turned.sem, turned + i + 1)
                nc.scalar.activation(dst[0], bank_of(i), ACT.Copy,
                                     scale=1.0 if scale is None else scale).then_inc(K.high_turned.sem, 1)

        @block.vector
        def _(dve):
            for i, (srcs, dst, scale) in enumerate(items):
                dve.wait_ge(K.high_turned.sem, high0 + i + 1)
                nc.vector.scalar_tensor_tensor(dst[1], bank_of(i), 1.0 if scale is None else scale,
                                               dst[0].bitcast(F32), ALU.mult,
                                               ALU.subtract).then_inc(K.low_turned.sem, 1)

    K.turned.total += len(items)
    K.high_turned.total += len(items)
    K.low_turned.total += len(items)


def turn_model(K, src, scale_col=None):
    turn_parts(K, [([src[:, t, k * P:(k + 1) * P] for t in range(TT)], (K.xT[0][:, k, :], K.xT[1][:, k, :]),
                    None if scale_col is None else K.cols[:, scale_col + k:scale_col + k + 1]) for k in range(KT)])


def project(K, groups, who, take):
    nc = K.nc
    first = K.next_load
    items, group_loads, n = [], [], first
    for g, (stat, kt, spans) in enumerate(groups):
        m = loads_of(kt, spans[-1][1])
        group_loads.append(range(n, n + m))
        n += m
        items += [(g, span, t) for span in spans for t in range(TT)]
    count = n - first
    owners = [who(i // TT, t) for i, (_, _, t) in enumerate(items)]
    nth = shares(owners)
    closes = [i + 1 == len(items) or items[i + 1][0] != items[i][0] for i in range(len(items))]
    filled0, took = K.filled.total, {"act": K.act_took.total, "dve": K.dve_took.total}
    with nc.Block(no_gpsimd_drain=True) as block:

        @block.sync
        def _(sp):
            refill(K, sp, first, count)

        @block.tensor
        def _(pe):
            for g, (stat, kt, spans) in enumerate(groups):
                mine = [i for i, it in enumerate(items) if it[0] == g]
                ks = kt // len(group_loads[g])
                for half, n in enumerate(group_loads[g]):
                    weights_here(K, pe, n)
                    w = weight_parts(K, n)[0]
                    for i in mine:
                        _, (lo, hi), t = items[i]
                        if half == 0 and i >= NBANK:
                            j = i - NBANK
                            pe.wait_ge((K.act_took if owners[j] == "act" else K.dve_took).sem,
                                       took[owners[j]] + nth[j])
                        for k in range(ks):
                            kk = half * ks + k
                            mm = product(K, K.psum[:, i % NBANK, 0:hi - lo], stat(kk, t),
                                         [part[:, k, lo:hi] for part in w], kk == 0, kk == kt - 1)
                        if i == mine[-1]:
                            mm.then_inc(K.load_used, 1)
                        elif half == len(group_loads[g]) - 1:
                            mm.then_inc(K.filled.sem, 1)

        def engine(eng, name):
            for g in range(len(groups)):
                for n in group_loads[g]:
                    split_ahead(K, eng, name, n)
                for i, (gi, (lo, hi), t) in enumerate(items):
                    if gi == g and owners[i] == name:
                        if closes[i]:
                            eng.wait_ge(K.load_used, group_loads[g][-1] + 1)
                        else:
                            eng.wait_ge(K.filled.sem, filled0 + sum(not c for c in closes[:i + 1]))
                        take(i // TT, t, K.psum[:, i % NBANK, 0:hi - lo]).then_inc(
                            (K.act_took if name == "act" else K.dve_took).sem, 1)

        @block.scalar
        def _(act):
            engine(act, "act")

        @block.vector
        def _(dve):
            engine(dve, "dve")

    K.filled.total += sum(not c for c in closes)
    K.act_took.total += owners.count("act")
    K.dve_took.total += owners.count("dve")
    K.next_load += count


def feed_forward(K, count, width, gated):
    nc = K.nc
    jt = width // P
    npair = jt // 2
    nd = loads_of(jt, D)
    first = K.next_load
    up_load = lambda c: first + (0 if c == 0 else 2 + (c - 1) * (2 + nd))
    down_load = lambda c: first + 2 + c * (2 + nd) + (2 if c + 1 < count else 0)
    total = count * (2 + nd)
    fill0, act0, hid0 = K.filled.total, K.act_took.total, K.hidden_ready.total
    turned0, high0, low0 = K.turned.total, K.high_turned.total, K.low_turned.total
    hid, rel, hidT = K.hid, K.rel, K.hidT
    bank_of = lambda c, q: 6 + (npair * c + q) % 2

    def up_ready(eng, c, t):
        if t == 0:
            eng.wait_ge(K.filled.sem, fill0 + c + 1)
        else:
            eng.wait_ge(K.load_used, up_load(c) + 2)

    def steps():
        yield from [("split", up_load(0)), ("hidden", 0, 0), ("split", up_load(0) + 1), ("hidden", 0, 1)]
        for c in range(count):
            if c + 1 < count:
                yield from [("split", up_load(c + 1)), ("hidden", c + 1, 0)]
            yield ("parts", c)
            if c + 1 < count:
                yield from [("split", up_load(c + 1) + 1), ("hidden", c + 1, 1)]
            for i in range(nd):
                yield ("split", down_load(c) + i)

    with nc.Block(no_gpsimd_drain=True) as block:

        @block.sync
        def _(sp):
            refill(K, sp, first, total)

        @block.tensor
        def _(pe):
            def up(c, t):
                if c >= 1:
                    if gated:
                        pe.wait_ge(K.hidden_ready.sem, hid0 + TT * (c - 1) + t + 1)
                    else:
                        pe.wait_ge(K.act_took.sem, act0 + TT * (c - 1) + t + 1)
                g = 2 if gated else 1
                out = K.psum[:, 4 + t, :].rearrange("p (g n) -> p g n", g=g)
                for half in range(2):
                    n = up_load(c) + half
                    if t == 0:
                        weights_here(K, pe, n)
                    w = [part[:, n % PARTS, :].rearrange("p (g k n) -> p k g n", g=g, k=KT // 2)
                         for part in (K.wh, K.wl)]
                    for k in range(KT // 2):
                        kk = half * KT // 2 + k
                        mm = product(K, out, [x[:, kk, t * P:(t + 1) * P] for x in K.xT],
                                     [part[:, k, :, :] for part in w], kk == 0, kk == KT - 1)
                    if t == 1:
                        mm.then_inc(K.load_used, 1)
                    elif half == 1:
                        mm.then_inc(K.filled.sem, 1)

            def turn_hidden(c):
                pe.wait_ge(K.hidden_ready.sem, hid0 + TT * (c + 1))
                for q in range(npair):
                    i = npair * c + q
                    if i >= 2:
                        pe.wait_ge(K.low_turned.sem, low0 + i - 1)
                    for j in range(2):
                        for t in range(TT):
                            tr = nc.tensor.transpose(K.psum[:, bank_of(c, q), (2 * j + t) * P:(2 * j + t + 1) * P],
                                                     hid[:, c % 2, t, (2 * q + j) * P:(2 * q + j + 1) * P],
                                                     K.ident[:, :])
                    tr.then_inc(K.turned.sem, 1)

            def down(c):
                for j in range(jt):
                    n = down_load(c) + j * nd // jt
                    if j % (jt // nd) == 0:
                        weights_here(K, pe, n)
                    if j % 2 == 0:
                        pe.wait_ge(K.low_turned.sem, low0 + npair * c + j // 2 + 1)
                    w = weight_parts(K, n)[0]
                    for t in range(TT):
                        for h in range(2):
                            mm = product(K, K.psum[:, 2 * t + h, :],
                                         [x[:, c % 2, j, t * P:(t + 1) * P] for x in hidT],
                                         [part[:, j % (jt // nd), h * BANK:(h + 1) * BANK] for part in w],
                                         c == 0 and j == 0, c == count - 1 and j == jt - 1)
                    if (j + 1) % (jt // nd) == 0:
                        mm.then_inc(K.load_used, 1)

            for t in range(TT):
                up(0, t)
            for c in range(count):
                if c + 1 < count:
                    up(c + 1, 0)
                turn_hidden(c)
                if c + 1 < count:
                    up(c + 1, 1)
                down(c)

        @block.scalar
        def _(act):
            for step, *args in steps():
                if step == "split":
                    split_ahead(K, act, "act", *args)
                elif step == "hidden":
                    c, t = args
                    up_ready(act, c, t)
                    if c >= 1:
                        act.wait_ge(K.hidden_ready.sem, hid0 + TT * (c - 1) + t + 1)
                    nc.scalar.activation(rel[:, t, 0:width], K.psum[:, 4 + t, 0:width],
                                         ACT.Silu if gated else ACT.Relu).then_inc(K.act_took.sem, 1)
                else:
                    c, = args
                    for q in range(npair):
                        act.wait_ge(K.turned.sem, turned0 + npair * c + q + 1)
                        if c >= 2:
                            act.wait_ge(K.load_used, down_load(c - 2) + nd)
                        nc.scalar.activation(hidT[0][:, c % 2, 2 * q:2 * q + 2, :],
                                             K.psum[:, bank_of(c, q), :].rearrange("p (j n) -> p j n", j=2),
                                             ACT.Copy).then_inc(K.high_turned.sem, 1)

        @block.vector
        def _(dve):
            for step, *args in steps():
                if step == "split":
                    split_ahead(K, dve, "dve", *args)
                elif step == "hidden":
                    c, t = args
                    dve.wait_ge(K.act_took.sem, act0 + TT * c + t + 1)
                    if c >= 2:
                        dve.wait_ge(K.turned.sem, turned0 + npair * (c - 1))
                    other = K.psum[:, 4 + t, width:2 * width] if gated else rel[:, t, 0:width]
                    nc.vector.tensor_tensor(hid[:, c % 2, t, 0:width], rel[:, t, 0:width], other,
                                            ALU.mult).then_inc(K.hidden_ready.sem, 1)
                else:
                    c, = args
                    for q in range(npair):
                        dve.wait_ge(K.high_turned.sem, high0 + npair * c + q + 1)
                        at = (slice(None), c % 2, slice(2 * q, 2 * q + 2), slice(None))
                        nc.vector.tensor_tensor(hidT[1][at],
                                                K.psum[:, bank_of(c, q), :].rearrange("p (j n) -> p j n", j=2),
                                                hidT[0][at].bitcast(F32), ALU.subtract).then_inc(K.low_turned.sem, 1)

    K.filled.total += count
    K.act_took.total += TT * count
    K.hidden_ready.total += TT * count
    K.turned.total += npair * count
    K.high_turned.total += npair * count
    K.low_turned.total += npair * count
    K.next_load += total


def residual_norm(K, gain, shift, bias=None):
    nc = K.nc
    with nc.Block(no_gpsimd_drain=True) as block:
        stat0, rstd0, hat0 = K.stat_ready.total, K.rstd_ready.total, K.hat_ready.total

        @block.vector
        def _(dve):
            ch = Chain(dve, K.dve_step)
            for r in (gain, shift, bias):
                if r is not None:
                    row_here(K, dve, r)
            for t in range(TT):
                z = K.z[:, t, :]
                for h in range(2):
                    s = slice(h * BANK, (h + 1) * BANK)
                    ch.do(nc.vector.scalar_tensor_tensor(z[:, s], K.x[:, t, s], ALPHA, K.psum[:, 2 * t + h, :],
                                                         ALU.mult, ALU.add))
                    if bias is not None:
                        ch.do(nc.vector.tensor_tensor(z[:, s], z[:, s], K.rows[:, bias, s], ALU.add))
                    ch.do(nc.vector.bn_stats(K.bn[:, t, h, :], z[:, s]))
                ch.do(nc.vector.bn_aggr(K.stat[:, t, 0:2], K.bn[:, t, :, :]))
                nc.vector.tensor_scalar(K.stat[:, t, 1:2], K.stat[:, t, 1:2], LN_EPS, None,
                                        ALU.add).then_inc(K.stat_ready.sem, 1)
            for t in range(TT):
                dve.wait_ge(K.rstd_ready.sem, rstd0 + t + 1)
                nc.vector.scalar_tensor_tensor(K.stat[:, t, 3:4], K.stat[:, t, 0:1], -1.0, K.stat[:, t, 2:3],
                                               ALU.mult, ALU.mult).then_inc(K.stat_ready.sem, 1)
            for t in range(TT):
                dve.wait_ge(K.hat_ready.sem, hat0 + t + 1)
                ch.do(nc.vector.tensor_tensor(K.z[:, t, :], K.z[:, t, :], K.rows[:, gain, :], ALU.mult))
                ch.do(nc.vector.tensor_tensor(K.x[:, t, :], K.z[:, t, :], K.rows[:, shift, :], ALU.add))

        @block.gpsimd
        def _(pool):
            for t in range(TT):
                pool.wait_ge(K.stat_ready.sem, stat0 + t + 1)
                nc.gpsimd.tensor_tensor(K.stat[:, t, 2:3], K.stat[:, t, 1:2], K.minus_half[:, 0:1],
                                        ALU.pow).then_inc(K.rstd_ready.sem, 1)
            pool.wait_ge(K.rstd_ready.sem, rstd0 + TT)

        @block.scalar
        def _(act):
            for t in range(TT):
                act.wait_ge(K.stat_ready.sem, stat0 + TT + t + 1)
                nc.scalar.activation(K.z[:, t, :], K.z[:, t, :], ACT.Identity, bias=K.stat[:, t, 3:4],
                                     scale=K.stat[:, t, 2:3]).then_inc(K.hat_ready.sem, 1)

    K.stat_ready.total += 2 * TT
    K.rstd_ready.total += TT
    K.hat_ready.total += TT


def root_norm(K, src, widths, dst):
    nc = K.nc
    n = len(widths)
    with nc.Block(no_gpsimd_drain=True) as block:
        sq0, stat0, rstd0 = K.square_ready.total, K.stat_ready.total, K.rstd_ready.total

        @block.scalar
        def _(act):
            for t in range(TT):
                for i, (lo, hi) in enumerate(widths):
                    nc.scalar.activation(K.scratch[:, t, lo:hi], src[:, t, lo:hi], ACT.Square,
                                         accum_out=K.stat[:, t, i:i + 1]).then_inc(K.square_ready.sem, 1)

        @block.vector
        def _(dve):
            for t in range(TT):
                dve.wait_ge(K.square_ready.sem, sq0 + n * (t + 1))
                for i, (lo, hi) in enumerate(widths):
                    last = nc.vector.tensor_scalar(K.stat[:, t, 2 + i:3 + i], K.stat[:, t, i:i + 1], 1.0 / (hi - lo),
                                                   RMS_EPS, ALU.mult, ALU.add)
                last.then_inc(K.stat_ready.sem, 1)
            for t in range(TT):
                dve.wait_ge(K.rstd_ready.sem, rstd0 + t + 1)
                for i, (lo, hi) in enumerate(widths):
                    nc.vector.tensor_scalar(dst[:, t, lo:hi], src[:, t, lo:hi], K.stat[:, t, 4 + i:5 + i], None,
                                            ALU.mult)

        @block.gpsimd
        def _(pool):
            for t in range(TT):
                pool.wait_ge(K.stat_ready.sem, stat0 + t + 1)
                nc.gpsimd.tensor_tensor(K.stat[:, t, 4:4 + n], K.stat[:, t, 2:2 + n], K.minus_half[:, 0:n],
                                        ALU.pow).then_inc(K.rstd_ready.sem, 1)
            pool.wait_ge(K.rstd_ready.sem, rstd0 + TT)

    K.square_ready.total += n * TT
    K.stat_ready.total += TT
    K.rstd_ready.total += TT


def half_step(K):
    nc = K.nc
    with nc.Block(no_gpsimd_drain=True) as block:

        @block.vector
        def _(dve):
            for t in range(TT):
                for h in range(2):
                    s = slice(h * BANK, (h + 1) * BANK)
                    nc.vector.scalar_tensor_tensor(K.x[:, t, s], K.psum[:, 2 * t + h, :], 0.5, K.x[:, t, s],
                                                   ALU.mult, ALU.add)


def row_here(K, eng, r):
    eng.wait_ge(K.row_loaded[r], 16 * K.row_loads[r])


def load_rows(K, sp, which):
    for r, vec in which.items():
        w = vec.shape[0]
        sp.dma_start(K.rows[:, r, 0:w], vec.partition_broadcast(P)).then_inc(K.row_loaded[r], 16)
        K.row_loads[r] += 1


def rows_stage(K, which):
    with K.nc.Block(no_gpsimd_drain=True) as block:

        @block.sync
        def _(sp):
            load_rows(K, sp, which)


def setup(K, a):
    nc = K.nc
    lists = [("head_g", a["a_head_norm_g"][0]), ("ffn1", a["ffn1_norm_2"][0]), ("mix", a["mix_norm_2"][0]),
             ("out_nsa", a["out_norm_nsa_2"][0]), ("out_fox", a["out_norm_fox_2"][0]), ("ffn2", a["ffn2_norm_2"][0]),
             ("ple", a["ple_gate_norm_2"][0]), ("pos_k", a["cmp_pos_k_2"][0].rearrange("j d -> (j d)")),
             ("pos_v", a["cmp_pos_v_2"][0].rearrange("j d -> (j d)"))]
    K.col_of, n = {}, 0
    for name, vec in lists:
        K.col_of[name] = n
        n += vec.shape[0] // P
    K.n_cols = n
    with nc.Block(no_gpsimd_drain=True) as block:

        @block.sync
        def _(sp):
            sp.dma_start(K.x[:, :, :], a["x"][0].rearrange("(t p) d -> p t d", p=P)).then_inc(K.input_loaded, 16)
            for n in range(SLOTS):
                load_weights(K, sp, n)
            refill(K, sp, -AHEAD, AHEAD)

        @block.scalar
        def _(act):
            for name, vec in lists:
                c, m = K.col_of[name], vec.shape[0] // P
                act.dma_start(K.z[c:c + m, 0, 0:P], vec.rearrange("(k p) -> k p", p=P)).then_inc(K.small_loaded, 16)
            act.dma_start(K.positions[:, :], a["positions"][0].rearrange("(t p) -> p t", p=P),
                          allow_slow_non_contiguous=True).then_inc(K.small_loaded, 16)
            act.dma_start(K.gate_bias[0:M_HEADS, 0:1], a["a_b_igate"][0].unsqueeze(1)).then_inc(K.small_loaded, 16)
            act.dma_start(K.gate_bias[0:M_HEADS, 1:2], a["a_b_fgate"][0].unsqueeze(1)).then_inc(K.small_loaded, 16)
            act.dma_start(K.gate_bias[0:FOX, 2:3], a["b_forget_2"][0].unsqueeze(1)).then_inc(K.small_loaded, 16)
            act.dma_start(K.sinks[:, :], a["b_sinks"][0].partition_broadcast(P)).then_inc(K.small_loaded, 16)
            for i, name in enumerate(["q_norm_nsa_2", "k_norm_slc_2", "k_norm_win_2", "q_norm_fox_2", "k_norm_fox_2",
                                      "k_norm_cmp_2"]):
                act.dma_start(K.head_gain[:, i, :], a[name][0].partition_broadcast(P)).then_inc(K.small_loaded, 16)
            act.wait_ge(K.small_loaded, 16 * (len(lists) + 11))
            for n in range(AHEAD):
                split_high(K, act, n)

        @block.vector
        def _(dve):
            for ap, value in [(K.ident[:, :], 0.0), (K.sel[:, :, :], 0.0), (K.ones[:, :], 1.0), (K.fox_bias[:, :], 0.0),
                              (K.minus_half[:, :], -0.5), (K.causal[:, :], 0.0), (K.window[:, :], 0.0),
                              (K.causal_t[:, :], 0.0), (K.cmp_mask[:, :, :], 0.0), (K.cmp_keep[:, :, :], 1.0),
                              (K.v_ext[:, :, :, :], 1.0)]:
                last = nc.vector.memset(ap, value)
            for i in range(HALF):
                last = nc.vector.memset(K.inv_freq[:, i:i + 1], float(np.float32(THETA) ** np.float32(-i * 2.0 / ROT)))
            last.then_inc(K.zeroed, 1)
            for n in range(AHEAD):
                split_low(K, dve, n)

        @block.gpsimd
        def _(pool):
            pool.wait_ge(K.zeroed, 1)

            def select(out, src, pattern, base, mult, fill, op=ALU.is_ge):
                K.masked_total += 1
                nc.gpsimd.affine_select(out=out, in_=src, compare_op=op, fill=fill, base=base, pattern=pattern,
                                        channel_multiplier=mult).then_inc(K.masked, 1)
                pool.wait_ge(K.masked, K.masked_total)

            select(K.ident[:, :], K.ident[:, :], [[-1, P]], 0, 1, 1.0, ALU.not_equal)
            select(K.sel[:, :, :], K.sel[:, :, :], [[-1, FOX], [0, P]], 0, 1, 1.0, ALU.not_equal)
            select(K.causal[:, :], K.causal[:, :], [[-1, SEQ]], P, 1, NEG)
            select(K.window[:, :], K.causal[:, :], [[1, SEQ]], 0, -1, NEG, ALU.is_gt)
            select(K.causal_t[:, 0:P], K.causal_t[:, 0:P], [[1, P]], 0, -1, NEG)
            select(K.causal_t[:, 2 * P:3 * P], K.causal_t[:, 2 * P:3 * P], [[1, P]], 0, -1, NEG)
            for t in range(TT):
                pat = [[-CMP_STRIDE, N_CMP]]
                select(K.cmp_mask[:, t, :], K.cmp_mask[:, t, :], pat, t * P - CMP_BLOCK + 1, 1, NEG)
                select(K.cmp_keep[:, t, :], K.cmp_keep[:, t, :], pat, t * P - CMP_BLOCK + 1, 1, 0.0)
            nc.gpsimd.iota(K.index[:, :], [[P, TT]], base=0, channel_multiplier=1).then_inc(K.masked, 1)
            K.masked_total += 1
            pool.wait_ge(K.masked, K.masked_total)

        @block.tensor
        def _(pe):
            pe.wait_ge(K.input_loaded, 16)

    turn(K, [([K.z[0:n, 0, 0:P]], K.cols[:, 0:n], None)])
    turn_model(K, K.x)
    rotary_tables(K)


def rotary_tables(K):
    nc = K.nc
    n = 2 * TT * HALF
    with nc.Block(no_gpsimd_drain=True) as block:
        ready0 = K.angle_ready.total

        @block.vector
        def _(dve):
            ch = Chain(dve, K.dve_step)
            A = K.angle
            ch.do(nc.vector.tensor_copy(K.pos_f[:, 0:TT], K.positions[:, :]))
            ch.do(nc.vector.tensor_copy(K.pos_f[:, TT:2 * TT], K.index[:, :]))
            for i in range(2 * TT):
                ch.do(nc.vector.tensor_scalar(A[:, 0, i * HALF:(i + 1) * HALF], K.inv_freq[:, :],
                                              K.pos_f[:, i:i + 1], None, ALU.mult))
            for which, shift in ((1, 0.25), (2, 0.0)):
                ch.do(nc.vector.tensor_scalar(A[:, 3, :], A[:, 0, :], 1.0 / (2 * math.pi), shift, ALU.mult, ALU.add))
                ch.do(nc.vector.tensor_scalar(A[:, 3, :], A[:, 3, :], ROUND, None, ALU.add))
                ch.do(nc.vector.tensor_scalar(A[:, 3, :], A[:, 3, :], ROUND, None, ALU.subtract))
                ch.do(nc.vector.scalar_tensor_tensor(A[:, which, :], A[:, 3, :], -TWO_PI[0], A[:, 0, :],
                                                     ALU.mult, ALU.add))
                ch.do(nc.vector.scalar_tensor_tensor(A[:, which, :], A[:, 3, :], -TWO_PI[1], A[:, which, :],
                                                     ALU.mult, ALU.add))
                ch.do(nc.vector.scalar_tensor_tensor(A[:, which, :], A[:, 3, :], -TWO_PI[2], A[:, which, :],
                                                     ALU.mult, ALU.add))
                if which == 1:
                    ch.do(nc.vector.tensor_scalar(A[:, which, :], A[:, which, :], math.pi / 2, None, ALU.add))
                ch.do(nc.vector.tensor_scalar(A[:, which, :], A[:, which, :], PI_BELOW, -PI_BELOW, ALU.min, ALU.max))
            nc.vector.tensor_copy(A[:, 4, :], A[:, 1, :]).then_inc(K.angle_ready.sem, 1)

        @block.scalar
        def _(act):
            act.wait_ge(K.angle_ready.sem, ready0 + 1)
            nc.scalar.activation(K.cos_sin[:, 0, :], K.angle[:, 1, :], ACT.Sin)
            nc.scalar.activation(K.cos_sin[:, 1, :], K.angle[:, 2, :], ACT.Sin)
    K.angle_ready.total += 1


ROUND = 1.5 * 2.0 ** 23
TWO_PI = [6.28125, float(np.float32(2 * math.pi - 6.28125)),
          float(2 * math.pi - 6.28125 - float(np.float32(2 * math.pi - 6.28125)))]
PI_BELOW = 3.1415925


def rotate(K, ch, heads, table, t):
    nc = K.nc
    n = heads.shape[1]
    at = (table * TT + t) * HALF
    cos, sin = [K.cos_sin[:, i, at:at + HALF].unsqueeze(1).broadcast_to([P, n, HALF]) for i in range(2)]
    a, b = heads[:, :, 0:HALF], heads[:, :, HALF:ROT]
    w = [K.rot[:, i, 0:n, :] for i in range(4)]
    nc.vector.tensor_tensor(w[0], a, cos, ALU.mult)
    nc.vector.tensor_tensor(w[1], b, sin, ALU.mult)
    nc.vector.tensor_tensor(w[2], b, cos, ALU.mult)
    ch.do(nc.vector.tensor_tensor(w[3], a, sin, ALU.mult))
    nc.vector.tensor_tensor(a, w[0], w[1], ALU.subtract)
    ch.do(nc.vector.tensor_tensor(b, w[2], w[3], ALU.add))


def gate_columns(K):
    nc = K.nc
    H = M_HEADS
    with nc.Block(no_gpsimd_drain=True) as block:
        turned, step0, act0 = K.turned.total, K.gates_v.total, K.gates_a.total

        @block.tensor
        def _(pe):
            for i in range(2):
                for t in range(TT):
                    tr = nc.tensor.transpose(K.psum[0:H, 0, (i * TT + t) * P:(i * TT + t + 1) * P],
                                             K.o[:, t, D + i * H:D + (i + 1) * H], K.ident[:, :])
            tr.then_inc(K.turned.sem, 1)
            pe.wait_ge(K.gates_v.sem, step0 + 3)
            for i, r in enumerate((1, 3)):
                for t in range(TT):
                    at = (i * TT + t) * H
                    tr = nc.tensor.transpose(K.psum[:, 1, at:at + H], K.gates[0:H, r, t * P:(t + 1) * P],
                                             K.ident[0:H, 0:H])
            tr.then_inc(K.turned.sem, 1)

        @block.vector
        def _(dve):
            ch = Chain(dve, K.dve_step)
            G = K.gates
            nc.vector.tensor_scalar(K.gate_bias[0:H, 0:2], K.gate_bias[0:H, 0:2], 1.0 / GATE_CAP, None,
                                    ALU.mult).then_inc(K.gates_v.sem, 1)
            dve.wait_ge(K.gates_a.sem, act0 + 3)
            ch.do(nc.vector.tensor_tensor_scan(G[0:H, 5, :], K.ones[0:H, :], G[0:H, 6, :], 0.0, ALU.mult,
                                               ALU.subtract))
            ch.do(nc.vector.scalar_tensor_tensor(G[0:H, 1, :], G[0:H, 0, 0:SEQ], GATE_CAP, G[0:H, 5, :], ALU.mult,
                                                 ALU.subtract))
            ch.do(nc.vector.tensor_tensor_scan(G[0:H, 4, :], G[0:H, 1, :], G[0:H, 1, :], 0.0, ALU.max, ALU.max))
            nc.vector.tensor_scalar(G[0:H, 2, :], G[0:H, 4, :], -1.0, None, ALU.mult).then_inc(K.gates_v.sem, 1)
            nc.vector.scalar_tensor_tensor(G[0:H, 3, :], G[0:H, 4, :], -1.0, G[0:H, 5, :], ALU.mult,
                                           ALU.subtract).then_inc(K.gates_v.sem, 1)
            dve.wait_ge(K.turned.sem, turned + 2)
            nc.vector.tensor_copy(K.u_col[:, :], K.psum[:, 1, 0:TT * H]).then_inc(K.gates_v.sem, 1)

        @block.scalar
        def _(act):
            G = K.gates
            act.wait_ge(K.turned.sem, turned + 1)
            act.wait_ge(K.gates_v.sem, step0 + 1)
            nc.scalar.activation(G[0:H, 0, :], K.psum[0:H, 0, 0:SEQ], ACT.Tanh, bias=K.gate_bias[0:H, 0:1],
                                 scale=1.0 / GATE_CAP)
            nc.scalar.activation(G[0:H, 7, :], K.psum[0:H, 0, SEQ:2 * SEQ], ACT.Tanh, bias=K.gate_bias[0:H, 1:2],
                                 scale=1.0 / GATE_CAP).then_inc(K.gates_a.sem, 1)
            act.wait_ge(K.gates_a.sem, act0 + 1)
            nc.scalar.activation(G[0:H, 7, :], G[0:H, 7, :], ACT.Exp, scale=-GATE_CAP).then_inc(K.gates_a.sem, 1)
            act.wait_ge(K.gates_a.sem, act0 + 2)
            nc.scalar.activation(G[0:H, 6, :], G[0:H, 7, :], ACT.Ln, bias=1.0).then_inc(K.gates_a.sem, 1)
            act.wait_ge(K.gates_v.sem, step0 + 4)
            nc.scalar.activation(K.exp_m[:, :], K.psum[:, 1, TT * H:2 * TT * H], ACT.Exp)

    K.turned.total += 2
    K.gates_v.total += 4
    K.gates_a.total += 3


def mlstm(K):
    nc = K.nc
    H, W = M_HEADS, 3 * P
    pieces = ((0, 0, SEQ, 0), (1, P, SEQ, SEQ))
    with nc.Block(no_gpsimd_drain=True) as block:
        scores0, arg0, expd0, weight0 = K.scores_ready.total, K.masked_scores.total, K.probs_ready.total, \
            K.weights_ready.total
        out0, took0 = K.values_ready.total, K.act_took.total

        @block.tensor
        def _(pe):
            def scores(h):
                if h >= 2:
                    pe.wait_ge(K.weights_ready.sem, weight0 + h - 1)
                for s, q0, q1, at in pieces:
                    nc.tensor.matmul(K.psum[:, h % 2, at:at + q1 - q0], K.qkT[:, H + h, s * P:(s + 1) * P],
                                     K.qkT[:, h, q0:q1], start=True, stop=True)
                    mm = nc.tensor.matmul(K.psum[:, 2 + h % 2, at:at + q1 - q0], K.sel[0:H, h, :],
                                          K.gates[0:H, 2, q0:q1], start=True, stop=True)
                mm.then_inc(K.scores_ready.sem, 1)

            def values(h):
                pe.wait_ge(K.weights_ready.sem, weight0 + h + 1)
                if h >= 2:
                    pe.wait_ge(K.act_took.sem, took0 + TT * (h - 1))
                w = K.decayed[:, h % 2, :]
                b = 4 + 2 * (h % 2)
                nc.tensor.matmul(K.psum[:, b, 0:M_DV + 1], w[:, 0:P], K.v_ext[:, 0, h, :], start=True, stop=True)
                nc.tensor.matmul(K.psum[:, b + 1, 0:M_DV + 1], w[:, P:2 * P], K.v_ext[:, 0, h, :],
                                 start=True, stop=False)
                nc.tensor.matmul(K.psum[:, b + 1, 0:M_DV + 1], w[:, 2 * P:3 * P], K.v_ext[:, 1, h, :],
                                 start=False, stop=True).then_inc(K.values_ready.sem, 1)

            scores(0)
            for h in range(H):
                if h + 1 < H:
                    scores(h + 1)
                values(h)

        @block.vector
        def _(dve):
            def exponent(h):
                dve.wait_ge(K.scores_ready.sem, scores0 + h + 1)
                if h >= 2:
                    dve.wait_ge(K.probs_ready.sem, expd0 + h - 1)
                nc.vector.scalar_tensor_tensor(K.exponent[:, h % 2, 0:SEQ], K.psum[:, 2 + h % 2, 0:SEQ],
                                               K.u_col[:, h:h + 1], K.causal_t[:, 0:SEQ], ALU.add, ALU.add)
                nc.vector.scalar_tensor_tensor(K.exponent[:, h % 2, SEQ:W], K.psum[:, 2 + h % 2, SEQ:W],
                                               K.u_col[:, H + h:H + h + 1], K.causal_t[:, SEQ:W], ALU.add,
                                               ALU.add).then_inc(K.masked_scores.sem, 1)

            def weigh(h):
                dve.wait_ge(K.probs_ready.sem, expd0 + h + 1)
                if h >= 2:
                    dve.wait_ge(K.values_ready.sem, out0 + h - 1)
                nc.vector.scalar_tensor_tensor(K.decayed[:, h % 2, :], K.psum[:, h % 2, 0:W], M_DK ** -0.5,
                                               K.decay[:, h % 2, :], ALU.mult,
                                               ALU.mult).then_inc(K.weights_ready.sem, 1)

            exponent(0)
            for h in range(H):
                if h + 1 < H:
                    exponent(h + 1)
                weigh(h)

        @block.scalar
        def _(act):
            def decay(h):
                act.wait_ge(K.masked_scores.sem, arg0 + h + 1)
                if h >= 2:
                    act.wait_ge(K.weights_ready.sem, weight0 + h - 1)
                nc.scalar.activation(K.decay[:, h % 2, :], K.exponent[:, h % 2, :],
                                     ACT.Exp).then_inc(K.probs_ready.sem, 1)

            def copy_out(h):
                act.wait_ge(K.values_ready.sem, out0 + h + 1)
                for t in range(TT):
                    nc.scalar.activation(K.h_raw[:, t, h, :], K.psum[:, 4 + 2 * (h % 2) + t, 0:M_DV + 1],
                                         ACT.Copy).then_inc(K.act_took.sem, 1)

            decay(0)
            for h in range(H):
                if h + 1 < H:
                    decay(h + 1)
                copy_out(h)

    K.scores_ready.total += H
    K.masked_scores.total += H
    K.probs_ready.total += H
    K.weights_ready.total += H
    K.values_ready.total += H
    K.act_took.total += TT * H


def mlstm_norm(K):
    nc = K.nc
    H, n = M_HEADS, TT * M_HEADS
    with nc.Block(no_gpsimd_drain=True) as block:
        stat0, rstd0 = K.stat_ready.total, K.rstd_ready.total
        S = K.mstat

        @block.vector
        def _(dve):
            ch = Chain(dve, K.dve_step)
            for t in range(TT):
                for h in range(H):
                    ch.do(nc.vector.bn_stats(K.bn8[:, t * H + h, :], K.h_raw[:, t, h, 0:M_DV]))
            for i in range(n):
                ch.do(nc.vector.bn_aggr(K.mean_var[:, i, :], K.bn8[:, i, :]))
            mean, var = K.mean_var[:, :, 0], K.mean_var[:, :, 1]
            for t in range(TT):
                den = K.h_raw[:, t, :, M_DV]
                ch.do(nc.vector.scalar_tensor_tensor(S[:, 0, t * H:(t + 1) * H], den, -1.0, den, ALU.mult, ALU.max))
            ch.do(nc.vector.tensor_tensor(S[:, 0, :], S[:, 0, :], K.exp_m[:, :], ALU.max))
            ch.do(nc.vector.reciprocal(S[:, 1, :], S[:, 0, :]))
            ch.do(nc.vector.tensor_tensor(S[:, 2, :], S[:, 1, :], S[:, 1, :], ALU.mult))
            ch.do(nc.vector.tensor_tensor(S[:, 2, :], S[:, 2, :], var, ALU.mult))
            nc.vector.tensor_scalar(S[:, 2, :], S[:, 2, :], LN_EPS, None, ALU.add).then_inc(K.stat_ready.sem, 1)
            dve.wait_ge(K.rstd_ready.sem, rstd0 + 1)
            ch.do(nc.vector.tensor_tensor(S[:, 4, :], S[:, 3, :], S[:, 1, :], ALU.mult))
            for t in range(TT):
                for h in range(H):
                    i = t * H + h
                    ch.do(nc.vector.tensor_scalar(K.z[:, t, h * M_DV:(h + 1) * M_DV], K.h_raw[:, t, h, 0:M_DV],
                                                  mean[:, i:i + 1], S[:, 4, i:i + 1], ALU.subtract, ALU.mult))
                nc.vector.tensor_tensor(K.z[:, t, :], K.z[:, t, :], K.o[:, t, 0:D], ALU.mult)

        @block.gpsimd
        def _(pool):
            pool.wait_ge(K.stat_ready.sem, stat0 + 1)
            nc.gpsimd.tensor_tensor(S[:, 3, :], S[:, 2, :], K.minus_half[:, 0:n], ALU.pow).then_inc(K.rstd_ready.sem, 1)
            pool.wait_ge(K.rstd_ready.sem, rstd0 + 1)

    K.stat_ready.total += 1
    K.rstd_ready.total += 1


def attend(K, units, groups):
    nc = K.nc
    n = len(units)
    with nc.Block(no_gpsimd_drain=True) as block:
        sc0, ms0, pr0, kp0 = K.scores_ready.total, K.masked_scores.total, K.probs_ready.total, K.probs_kept.total
        tu0, ac0, vc0 = K.turned.total, K.act_turned.total, K.dve_turned.total
        va0, og0 = K.values_ready.total, K.group_out.total
        kept = lambda i: sum(1 for u in units[:i] if u["keep"] is not None)
        columns = lambda u: u["size"] + (u["sink"] is not None)
        tiles = lambda u: [(s, min(P, u["size"] - s)) for s in range(0, u["size"], P)]

        def copied(eng, i):
            if i % 2 == 0:
                eng.wait_ge(K.act_turned.sem, ac0 + i // 2 + 1)
            else:
                eng.wait_ge(K.dve_turned.sem, vc0 + i // 2 + 1)

        @block.tensor
        def _(pe):
            def scores(i):
                u = units[i]
                if i >= 2:
                    pe.wait_ge(K.masked_scores.sem, ms0 + i - 1)
                out = [K.psum[:, 2 * (i % 2) + a, 0:u["size"]] for a in range(2)]
                if u["bias"] is not None:
                    for a in range(2):
                        nc.tensor.matmul(out[a], *u["bias"][a], start=True, stop=False)
                for a in range(2):
                    mm = nc.tensor.matmul(out[a], u["q"][a], u["k"][a], start=u["bias"] is None, stop=True)
                mm.then_inc(K.scores_ready.sem, 1)

            def turn_probs(i):
                u = units[i]
                pe.wait_ge(K.probs_ready.sem, pr0 + i + 1)
                if u["keep"] is not None:
                    pe.wait_ge(K.probs_kept.sem, kp0 + kept(i) + 1)
                if i >= 2:
                    copied(pe, i - 2)
                for a in range(2):
                    for j, (s, w) in enumerate(tiles(u)):
                        tr = nc.tensor.transpose(K.psum[0:w, 4 + i % 2, (2 * a + j) * P:(2 * a + j + 1) * P],
                                                 K.probs[:, i % 3, a, s:s + w], K.ident[:, :])
                tr.then_inc(K.turned.sem, 1)

            def values(i):
                u = units[i]
                copied(pe, i)
                g = i // 4
                if i % 4 == 0 and g >= 2:
                    pe.wait_ge(K.group_out.sem, og0 + g - 1)
                for a in range(2):
                    for j, (s, w) in enumerate(tiles(u)):
                        at = (2 * (i % 4) + a) * HD
                        mm = nc.tensor.matmul(K.psum[:, 6 + g % 2, at:at + HD],
                                              K.probsT[0:w, i % 2, (2 * a + j) * P:(2 * a + j + 1) * P],
                                              u["v"][a][j], start=(j == 0), stop=(j == len(tiles(u)) - 1))
                mm.then_inc(K.values_ready.sem, 1)

            for i in range(n + 3):
                if i < n:
                    scores(i)
                if 0 <= i - 2 < n:
                    turn_probs(i - 2)
                if 0 <= i - 3 < n:
                    values(i - 3)

        def copy(eng, i):
            u = units[i]
            eng.wait_ge(K.turned.sem, tu0 + i + 1)
            if i >= 2:
                eng.wait_ge(K.values_ready.sem, va0 + i - 1)
            w = min(P, u["size"])
            if u["size"] > P:
                src, dst = K.psum[:, 4 + i % 2, :], K.probsT[:, i % 2, :]
            else:
                src, dst = [z.rearrange("p (a j q) -> p a j q", a=2, j=2)[:, :, 0, :]
                            for z in (K.psum[0:w, 4 + i % 2, :], K.probsT[0:w, i % 2, :])]
            if i % 2 == 0:
                nc.scalar.activation(dst, src, ACT.Copy).then_inc(K.act_turned.sem, 1)
            else:
                nc.vector.tensor_copy(dst, src).then_inc(K.dve_turned.sem, 1)

        @block.scalar
        def _(act):
            for i in range(n + 2):
                if i < n:
                    u = units[i]
                    act.wait_ge(K.masked_scores.sem, ms0 + i + 1)
                    if i >= 3:
                        act.wait_ge(K.turned.sem, tu0 + i - 2)
                    for a in range(2):
                        at = slice(0, columns(u))
                        e = nc.scalar.activation(K.probs[:, i % 3, a, at], K.s_sb[:, i % 3, a, at], ACT.Exp,
                                                 bias=K.neg_max[:, 2 * i + a:2 * i + a + 1],
                                                 accum_out=K.sums[:, 2 * i + a:2 * i + a + 1])
                    e.then_inc(K.probs_ready.sem, 1)
                if 0 <= i - 2 < n and i % 2 == 0:
                    copy(act, i - 2)

        @block.vector
        def _(dve):
            ch = Chain(dve, K.dve_step)
            for i in range(n + 5):
                if i < n:
                    u = units[i]
                    w = u["size"]
                    dve.wait_ge(K.scores_ready.sem, sc0 + i + 1)
                    if i >= 3:
                        dve.wait_ge(K.probs_ready.sem, pr0 + i - 2)
                    s_sb = K.s_sb[:, i % 3, :, :]
                    if u["sink"] is not None:
                        nc.vector.tensor_copy(s_sb[:, :, w:w + 1],
                                              K.sinks[:, u["sink"]:u["sink"] + 2].unsqueeze(2))
                    ps = K.psum[:, 2 * (i % 2):2 * (i % 2) + 2, 0:w]
                    ch.do(nc.vector.scalar_tensor_tensor(s_sb[:, :, 0:w], ps, HD ** -0.5,
                                                         u["mask"].unsqueeze(1).broadcast_to([P, 2, w]), ALU.mult,
                                                         ALU.add))
                    nc.vector.tensor_reduce(K.neg_max[:, 2 * i:2 * i + 2], s_sb[:, :, 0:columns(u)], AX.X, ALU.max,
                                            negate=True).then_inc(K.masked_scores.sem, 1)
                if 0 <= i - 1 < n and units[i - 1]["keep"] is not None:
                    dve.wait_ge(K.probs_ready.sem, pr0 + i)
                    w = units[i - 1]["size"]
                    p = K.probs[:, (i - 1) % 3, :, 0:w]
                    nc.vector.tensor_tensor(p, p, units[i - 1]["keep"].unsqueeze(1).broadcast_to([P, 2, w]),
                                            ALU.mult).then_inc(K.probs_kept.sem, 1)
                if 0 <= i - 2 < n and i % 2 == 1:
                    copy(dve, i - 2)
                if 0 <= i - 4 < n and (i - 4) % 4 == 3:
                    g = (i - 4) // 4
                    dve.wait_ge(K.values_ready.sem, va0 + i - 3)
                    at = slice(8 * g, 8 * g + 8)
                    groups[g](ch, K.psum[:, 6 + g % 2, :].rearrange("p (h d) -> p h d", d=HD),
                              K.sums[:, at]).then_inc(K.group_out.sem, 1)

    K.scores_ready.total += n
    K.masked_scores.total += n
    K.probs_ready.total += n
    K.probs_kept.total += kept(n)
    K.turned.total += n
    K.act_turned.total += (n + 1) // 2
    K.dve_turned.total += n // 2
    K.values_ready.total += n
    K.group_out.total += n // 4


def fox_gates(K):
    nc = K.nc
    H, G = FOX, K.gates
    with nc.Block(no_gpsimd_drain=True) as block:
        turned, v0, a0 = K.turned.total, K.gates_v.total, K.gates_a.total

        @block.tensor
        def _(pe):
            for t in range(TT):
                tr = nc.tensor.transpose(K.psum[0:H, 0, t * P:(t + 1) * P], K.uv[:, t, FL:FL + H], K.ident[:, :])
            tr.then_inc(K.turned.sem, 1)

        @block.vector
        def _(dve):
            ch = Chain(dve, K.dve_step)
            dve.wait_ge(K.turned.sem, turned + 1)
            ch.do(nc.vector.tensor_scalar(G[:, 0, :], K.psum[0:H, 0, 0:SEQ], K.gate_bias[0:H, 2:3], None, ALU.add))
            nc.vector.scalar_tensor_tensor(G[:, 1, :], G[:, 0, :], -1.0, G[:, 0, :], ALU.mult,
                                           ALU.max).then_inc(K.gates_v.sem, 1)
            ch.do(nc.vector.tensor_scalar(G[:, 3, :], G[:, 0, :], 0.0, None, ALU.min))
            dve.wait_ge(K.gates_a.sem, a0 + 2)
            ch.do(nc.vector.tensor_tensor(G[:, 4, :], G[:, 3, :], G[:, 2, :], ALU.subtract))
            ch.do(nc.vector.tensor_tensor_scan(G[:, 5, :], K.ones[0:H, :], G[:, 4, :], 0.0, ALU.mult, ALU.add))
            nc.vector.tensor_scalar(K.fox_bias[0:H, :], G[:, 5, :], -HD ** 0.5, None, ALU.mult)

        @block.scalar
        def _(act):
            act.wait_ge(K.gates_v.sem, v0 + 1)
            nc.scalar.activation(G[:, 7, :], G[:, 1, :], ACT.Exp, scale=-1.0).then_inc(K.gates_a.sem, 1)
            act.wait_ge(K.gates_a.sem, a0 + 1)
            nc.scalar.activation(G[:, 2, :], G[:, 7, :], ACT.Ln, bias=1.0).then_inc(K.gates_a.sem, 1)
    K.turned.total += 1
    K.gates_v.total += 1
    K.gates_a.total += 2


def normed_heads(K):
    nc = K.nc
    groups = [(QA, N_Q, 0), (KSL, N_KV, 1), (KWN, N_KV, 2), (QF, FOX, 3), (KF, FOX, 4)]
    total = sum(h for _, h, _ in groups)
    with nc.Block(no_gpsimd_drain=True) as block:
        sq0, st0, rs0 = K.square_ready.total, K.stat_ready.total, K.rstd_ready.total

        @block.scalar
        def _(act):
            for t in range(TT):
                nc.scalar.activation(K.squares[:, t, :], K.uq[:, t, :], ACT.Square).then_inc(K.square_ready.sem, 1)

        @block.vector
        def _(dve):
            ch = Chain(dve, K.dve_step)

            def heads(buf, t, c, h):
                return buf[:, t, c:c + h * HD].rearrange("p (h d) -> p h d", d=HD)
            for t in range(TT):
                dve.wait_ge(K.square_ready.sem, sq0 + t + 1)
                at = 0
                for c, h, _ in groups:
                    ch.do(nc.vector.tensor_reduce(K.head_ms[:, t, 0, at:at + h], heads(K.squares, t, c, h), AX.X,
                                                  ALU.add))
                    at += h
                nc.vector.tensor_scalar(K.head_ms[:, t, 1, :], K.head_ms[:, t, 0, :], 1.0 / HD, RMS_EPS, ALU.mult,
                                        ALU.add).then_inc(K.stat_ready.sem, 1)
            for t in range(TT):
                rotate(K, ch, heads(K.uq, t, KC, N_KV), 1, t)
                dve.wait_ge(K.rstd_ready.sem, rs0 + t + 1)
                at = 0
                for c, h, g in groups:
                    x = heads(K.uq, t, c, h)
                    ch.do(nc.vector.tensor_tensor(x, x, K.head_ms[:, t, 2, at:at + h].unsqueeze(2).broadcast_to(
                        [P, h, HD]), ALU.mult))
                    ch.do(nc.vector.tensor_tensor(x, x, K.head_gain[:, g, :].unsqueeze(1).broadcast_to([P, h, HD]),
                                                  ALU.mult))
                    at += h
                    if g < 3:
                        rotate(K, ch, x, 1, t)
                write_twice(K, K.twice[:, t, :, :, :], K.uq[:, t, KC:QF])

        @block.gpsimd
        def _(pool):
            for t in range(TT):
                pool.wait_ge(K.stat_ready.sem, st0 + t + 1)
                nc.gpsimd.tensor_tensor(K.head_ms[:, t, 2, :], K.head_ms[:, t, 1, :], K.minus_half[:, 0:total],
                                        ALU.pow).then_inc(K.rstd_ready.sem, 1)
            pool.wait_ge(K.rstd_ready.sem, rs0 + TT)

    K.square_ready.total += TT
    K.stat_ready.total += TT
    K.rstd_ready.total += TT


def compress(K):
    nc = K.nc
    first = K.next_load
    nb = N_KV * N_CMP
    JJ = CMP_BLOCK // 2
    with nc.Block(no_gpsimd_drain=True) as block:
        turned, took = K.turned.total, K.act_took.total

        @block.tensor
        def _(pe):
            for i, c in enumerate((KC, VC)):
                for h in range(N_KV):
                    for t in range(TT):
                        head = K.twice[:, t, (c - KC) // HD + h, :, :].rearrange("p a d -> p (a d)")
                        tr = nc.tensor.transpose(K.psum[:, i, (h * TT + t) * P:(h * TT + t + 1) * P], head,
                                                 K.ident[:, :])
                tr.then_inc(K.turned.sem, 1)

        @block.scalar
        def _(act):
            for i in range(2):
                act.wait_ge(K.turned.sem, turned + i + 1)
                ps = K.psum[:, i, :].rearrange("p (h n) -> p h n", n=SEQ)
                nc.scalar.activation(K.kc2[0:HD, i, :, :], ps[0:HD, :, :], ACT.Copy)
                nc.scalar.activation(K.kc2[HD:P, i, :, 0:SEQ - 1], ps[HD:P, :, 1:SEQ],
                                     ACT.Copy).then_inc(K.act_took.sem, 1)

        @block.vector
        def _(dve):
            ch = Chain(dve, K.dve_step)
            for which, pos in ((0, K.col_of["pos_k"]), (1, K.col_of["pos_v"])):
                dve.wait_ge(K.act_took.sem, took + which + 1)
                for h in range(N_KV):
                    tok = K.kc2[:, which, h, :].rearrange("p (n s) -> p s n", s=CMP_STRIDE)
                    for half in range(2):
                        js = slice(half * JJ // 2, (half + 1) * JJ // 2)
                        last = nc.vector.tensor_tensor(
                            K.block_sum[:, which, js, h * N_CMP:(h + 1) * N_CMP],
                            tok[:, 0:CMP_STRIDE:2, half:half + N_CMP],
                            K.cols[:, pos + half * JJ // 2:pos + (half + 1) * JJ // 2].unsqueeze(2).broadcast_to(
                                [P, JJ // 2, N_CMP]), ALU.add)
                ch.do(last)
                ch.do(nc.vector.tensor_copy(K.blocks[0][:, which, :, :], K.block_sum[:, which, :, :]))
                nc.vector.tensor_tensor(K.blocks[1][:, which, :, :], K.block_sum[:, which, :, :],
                                        K.blocks[0][:, which, :, :].bitcast(F32), ALU.subtract)
    K.turned.total += 2
    K.act_took.total += 2

    with nc.Block(no_gpsimd_drain=True) as block:
        a0, t0, v0 = K.act_took.total, K.turned.total, K.dve_took.total
        st0, rs0 = K.stat_ready.total, K.rstd_ready.total

        @block.sync
        def _(sp):
            refill(K, sp, first, 5)

        @block.tensor
        def _(pe):
            for which in range(2):
                for half in range(2):
                    n = first + 2 * which + half
                    weights_here(K, pe, n)
                    w1 = weight_parts(K, n)[0]
                    for j in range(JJ // 2):
                        jj = half * JJ // 2 + j
                        mm = product(K, K.psum[0:nb, which, 0:CMP_HID], [x[:, which, jj, :] for x in K.blocks],
                                     [part[:, j, :] for part in w1], jj == 0, jj == JJ - 1)
                    mm.then_inc(K.load_used, 1)
            for which in range(2):
                pe.wait_ge(K.act_took.sem, a0 + which + 1)
                for k in range(2):
                    tr = nc.tensor.transpose(K.psum[:, 2 + which, k * P:k * P + nb],
                                             K.cmp_hid[0:nb, which, k * P:(k + 1) * P], K.ident[0:nb, 0:nb])
                tr.then_inc(K.turned.sem, 1)
            weights_here(K, pe, first + 4)
            for which in range(2):
                pe.wait_ge(K.dve_took.sem, v0 + which + 1)
                w2 = weight_parts(K, first + 4)[which]
                for h in range(N_KV):
                    for k in range(2):
                        mm = product(K, K.psum[0:N_CMP, 4 + which, h * HD:(h + 1) * HD],
                                     [x[:, which, k, h * N_CMP:(h + 1) * N_CMP] for x in K.cmp_hidT],
                                     [part[:, k, :] for part in w2], k == 0, k == 1)
            mm.then_inc(K.load_used, 1)
            pe.wait_ge(K.dve_took.sem, v0 + 3)
            for h in range(N_KV):
                tr = nc.tensor.transpose(K.psum[:, 6, h * P:h * P + N_CMP],
                                         K.cmp_k2[:, h, :, :].rearrange("p a d -> p (a d)"),
                                         K.ident[0:N_CMP, 0:N_CMP])
            tr.then_inc(K.turned.sem, 1)

        @block.scalar
        def _(act):
            for which in range(2):
                for n in range(2):
                    split_ahead(K, act, "act", first + 2 * which + n)
                act.wait_ge(K.load_used, first + 2 * which + 2)
                nc.scalar.activation(K.cmp_hid[0:nb, which, :], K.psum[0:nb, which, 0:CMP_HID],
                                     ACT.Silu).then_inc(K.act_took.sem, 1)
            split_ahead(K, act, "act", first + 4)
            act.wait_ge(K.load_used, first + 5)
            nc.scalar.activation(K.cmp_v[:, :, :], K.psum[0:N_CMP, 5, 0:N_KV * HD].rearrange(
                "p (h d) -> p h d", d=HD), ACT.Copy)

        @block.vector
        def _(dve):
            ch = Chain(dve, K.dve_step)
            for n in range(4):
                split_ahead(K, dve, "dve", first + n)
            for which in range(2):
                dve.wait_ge(K.turned.sem, t0 + which + 1)
                ps = K.psum[:, 2 + which, 0:2 * P].rearrange("p (k n) -> p k n", k=2)[:, :, 0:nb]
                ch.do(nc.vector.tensor_copy(K.cmp_hidT[0][:, which, :, :], ps))
                nc.vector.tensor_tensor(K.cmp_hidT[1][:, which, :, :], ps, K.cmp_hidT[0][:, which, :, :].bitcast(F32),
                                        ALU.subtract).then_inc(K.dve_took.sem, 1)
            split_ahead(K, dve, "dve", first + 4)
            dve.wait_ge(K.load_used, first + 5)
            k = K.cmp_k
            ch.do(nc.vector.tensor_copy(k[:, :, :], K.psum[0:N_CMP, 4, 0:N_KV * HD].rearrange(
                "p (h d) -> p h d", d=HD)))
            ch.do(nc.vector.tensor_tensor(K.cmp_sq[:, :, :], k[:, :, :], k[:, :, :], ALU.mult))
            ch.do(nc.vector.tensor_reduce(K.stat[0:N_CMP, 0, 0:N_KV], K.cmp_sq[:, :, :], AX.X, ALU.add))
            nc.vector.tensor_scalar(K.stat[0:N_CMP, 0, 2:4], K.stat[0:N_CMP, 0, 0:N_KV], 1.0 / HD, RMS_EPS, ALU.mult,
                                    ALU.add).then_inc(K.stat_ready.sem, 1)
            dve.wait_ge(K.rstd_ready.sem, rs0 + 1)
            ch.do(nc.vector.tensor_tensor(k[:, :, :], k[:, :, :], K.stat[0:N_CMP, 0, 4:6].unsqueeze(2).broadcast_to(
                [N_CMP, N_KV, HD]), ALU.mult))
            ch.do(nc.vector.tensor_tensor(k[:, :, :], k[:, :, :], K.head_gain[0:N_CMP, 5, :].unsqueeze(1).broadcast_to(
                [N_CMP, N_KV, HD]), ALU.mult))
            write_twice(K, K.cmp_k2[:, :, :, :], k[:, :, :].rearrange("p h d -> p (h d)")).then_inc(K.dve_took.sem, 1)
            dve.wait_ge(K.turned.sem, t0 + 3)
            nc.vector.tensor_copy(K.cmp_kT[:, :, :], K.psum[:, 6, 0:2 * P].rearrange(
                "p (h n) -> p h n", h=2)[:, :, 0:N_CMP])

        @block.gpsimd
        def _(pool):
            pool.wait_ge(K.stat_ready.sem, st0 + 1)
            nc.gpsimd.tensor_tensor(K.stat[0:N_CMP, 0, 4:6], K.stat[0:N_CMP, 0, 2:4], K.minus_half[0:N_CMP, 0:2],
                                    ALU.pow).then_inc(K.rstd_ready.sem, 1)
            pool.wait_ge(K.rstd_ready.sem, rs0 + 1)

    K.act_took.total += 2
    K.turned.total += 3
    K.dve_took.total += 3
    K.stat_ready.total += 1
    K.rstd_ready.total += 1
    K.next_load += 5


def stationary(xT):
    return lambda k, t: [x[:, k, t * P:(t + 1) * P] for x in xT]


def embed(K, p, gate_bias_row, normed_row):
    nc = K.nc
    with nc.Block(no_gpsimd_drain=True) as block:

        @block.sync
        def _(sp):
            K.p_loads += 1
            sp.dma_start(K.p[:, :, :], p.rearrange("(t p) d -> p t d", p=P)).then_inc(K.p_loaded, 16)
            sp.wait_ge(K.p_loaded, 16 * K.p_loads)
    turn_parts(K, [([K.p[:, t, k * P:(k + 1) * P] for t in range(TT)], [x[:, k, :] for x in K.pT], None)
                   for k in range(PLE // P)])
    gate = K.scratch

    def take_gate(item, t, ps):
        s = slice(item * BANK, (item + 1) * BANK)
        if gate_bias_row is None:
            return nc.scalar.activation(gate[:, t, s], ps, ACT.Sigmoid)
        return nc.vector.tensor_tensor(gate[:, t, s], ps, K.rows[:, gate_bias_row, s], ALU.add)

    if gate_bias_row is not None:
        with nc.Block(no_gpsimd_drain=True) as block:
            @block.vector
            def _(dve):
                row_here(K, dve, gate_bias_row)
    project(K, [(stationary(K.xT), KT, [(0, BANK)])] * 2, lambda n, t: "act" if gate_bias_row is None else "dve", take_gate)
    if gate_bias_row is not None:
        with nc.Block(no_gpsimd_drain=True) as block:
            @block.scalar
            def _(act):
                for t in range(TT):
                    nc.scalar.activation(gate[:, t, :], gate[:, t, :], ACT.Sigmoid)
    proj = (stationary(K.pT), PLE // P, [(h * BANK, (h + 1) * BANK) for h in range(2)])

    def take_proj(item, t, ps):
        s = slice(item * BANK, (item + 1) * BANK)
        if normed_row is None:
            return nc.vector.tensor_tensor(K.z[:, t, s], ps, gate[:, t, s], ALU.mult)
        return nc.scalar.activation(K.z[:, t, s], ps, ACT.Copy)
    project(K, [proj], lambda n, t: "dve" if normed_row is None else "act", take_proj)
    if normed_row is not None:
        keep = K.scratch
        K.scratch = K.hid_flat
        root_norm(K, K.z, [(0, D)], K.z)
        K.scratch = keep
    with nc.Block(no_gpsimd_drain=True) as block:

        @block.vector
        def _(dve):
            ch = Chain(dve, K.dve_step)
            if normed_row is not None:
                row_here(K, dve, normed_row)
            for t in range(TT):
                if normed_row is not None:
                    ch.do(nc.vector.tensor_tensor(K.z[:, t, :], K.z[:, t, :], K.rows[:, normed_row, :], ALU.mult))
                    ch.do(nc.vector.tensor_tensor(K.z[:, t, :], K.z[:, t, :], gate[:, t, :], ALU.mult))
                nc.vector.tensor_tensor(K.x[:, t, :], K.x[:, t, :], K.z[:, t, :], ALU.add)


def build(nc, a, out, stop=99):
    K = Kit()
    K.nc = nc
    with ExitStack() as ctx:
        def sb(name, shape, dt=F32):
            return ctx.enter_context(nc.sbuf_tensor(name, shape, dt))

        def sem(name):
            return ctx.enter_context(nc.semaphore(name))

        K.ring = sb("ring", [P, SLOTS, SLOT])
        K.wh = sb("wh", [P, PARTS, SLOT], F32R)
        K.wl = sb("wl", [P, PARTS, SLOT], F32R)
        K.x = sb("x", [P, TT, D])
        K.xT = [sb("xT_high", [P, KT, SEQ], F32R), sb("xT_low", [P, KT, SEQ], F32R)]
        K.hidT = [sb("hidT_high", [P, 2, 4, SEQ], F32R), sb("hidT_low", [P, 2, 4, SEQ], F32R)]
        K.z = sb("z", [P, TT, D])
        K.rows = sb("rows", [P, ROWS, D])
        K.psum = ctx.enter_context(nc.psum_tensor("psum", [P, NBANK, BANK], F32))
        K.ident = sb("ident", [P, P])
        K.sel = sb("sel", [P, FOX, P])
        K.fox_bias = sb("fox_bias", [P, SEQ])
        K.ones = sb("ones", [P, SEQ])
        K.minus_half = sb("minus_half", [P, 32])
        K.causal = sb("causal", [P, SEQ])
        K.window = sb("window", [P, SEQ])
        K.causal_t = sb("causal_t", [P, 3 * P])
        K.cmp_mask = sb("cmp_mask", [P, TT, N_CMP])
        K.cmp_keep = sb("cmp_keep", [P, TT, N_CMP])
        K.inv_freq = sb("inv_freq", [P, HALF])
        K.cols = sb("cols", [P, 80])
        K.positions = sb("positions", [P, TT], I32)
        K.index = sb("index", [P, TT], I32)
        K.pos_f = sb("pos_f", [P, 2 * TT])
        K.angle = sb("angle", [P, 5, 2 * TT * HALF])
        K.cos_sin = sb("cos_sin", [P, 2, 2 * TT * HALF])
        K.rot = sb("rot", [P, 4, A_Q_HEADS, HALF])
        K.gate_bias = sb("gate_bias", [P, 3])
        K.sinks = sb("sinks", [P, A_Q_HEADS])
        K.head_gain = sb("head_gain", [P, 6, HD])
        K.stat = sb("stat", [P, TT, 6])
        K.bn = sb("bn", [P, TT, 2, 6])
        K.bn8 = sb("bn8", [P, TT * M_HEADS, 6])
        K.mean_var = sb("mean_var", [P, TT * M_HEADS, 2])
        K.mstat = sb("mstat", [P, 5, TT * M_HEADS])
        K.u_col = sb("u_col", [P, TT * M_HEADS])
        K.exp_m = sb("exp_m", [P, TT * M_HEADS])
        K.neg_max = sb("neg_max", [P, 64])
        K.sums = sb("sums", [P, 64])
        K.recip = sb("recip", [P, 8])
        K.head_ms = sb("head_ms", [P, TT, 3, 28])
        arena = sb("arena", [P, ARENA])

        def cut(at, rows, *shape):
            n = int(np.prod(shape))
            assert at + n <= ARENA, (at, n)
            view = arena[0:rows, at:at + n]
            names = "abcd"[:len(shape)]
            return view.rearrange(f"p ({' '.join(names)}) -> p {' '.join(names)}",
                                  **dict(zip(names, shape))) if len(shape) > 1 else view

        K.hid = cut(0, P, 2, TT, 512)
        K.hid_flat = cut(0, P, TT, D)
        K.rel = cut(2048, P, TT, 512)
        K.scratch = cut(3072, P, TT, D)
        K.p = cut(5120, P, TT, PLE)
        flat = [h[:, :, :, :].rearrange("p b j n -> p (b j n)") for h in K.hidT]
        K.pT = [f[:, 0:PLE // P * SEQ].rearrange("p (k n) -> p k n", n=SEQ) for f in flat]
        K.qk = cut(0, P, TT, D)
        K.h_raw = cut(0, P, TT, M_HEADS, M_DV + 1)
        K.o = cut(2056, P, TT, D + 8)
        K.qkT = cut(4120, P, 2 * M_HEADS, SEQ)
        K.v_ext = cut(6168, P, TT, M_HEADS, M_DV + 1)
        K.decayed = cut(8224, P, 2, 3 * P)
        z_flat = K.z[:, :, :].rearrange("p t d -> p (t d)")
        K.exponent = z_flat[:, 0:6 * P].rearrange("p (b n) -> p b n", b=2)
        K.decay = z_flat[:, 6 * P:12 * P].rearrange("p (b n) -> p b n", b=2)
        K.gates = K.rows[0:FOX, 2:4, :].rearrange("p r n -> p (r n)").rearrange("p (g n) -> p g n", g=8)
        SK = SEQ + 8
        QA_W = (A_Q_HEADS + A_KV_HEADS) * HD
        K.uq = cut(0, P, TT, QW)
        K.uq1 = cut(0, P, TT, QA_W)
        K.s_sb = cut(0, P, 3, 2, SK)
        K.probs = cut(1584, P, 3, 2, SK)
        K.probsT = cut(3168, P, 2, 512)
        K.uv = cut(4192, P, TT, VW)
        K.uv1 = cut(4192, P, TT, A_KV_HEADS * HD)
        K.attT = cut(5792, P, 16, SEQ)
        K.squares = cut(5792, P, TT, QW)
        K.group_tmp = K.rows[:, 3, 0:512]
        K.kc2 = K.z[:, :, :].rearrange("p t (h n) -> p t h n", n=SEQ)[:, :, 0:N_KV, :]
        nb = N_KV * N_CMP
        K.block_sum = K.rows[:, 2, 0:32 * nb].rearrange("p (w j n) -> p w j n", w=2, j=16)
        K.blocks = [f[:, 0:32 * nb].rearrange("p (w j n) -> p w j n", w=2, j=16) for f in flat]
        K.cmp_hidT = [f[:, 32 * nb:36 * nb].rearrange("p (w k n) -> p w k n", w=2, k=2) for f in flat]
        K.cmp_hid = cut(0, P, 2, CMP_HID)
        K.cmp_k = cut(512, N_CMP, N_KV, HD)
        K.cmp_sq = cut(640, N_CMP, N_KV, HD)
        K.cmp_k2 = cut(768, N_CMP, N_KV, 2, HD)
        K.twice = K.rows[:, 0:2, :].rearrange("p r n -> p (r n)").rearrange("p (t h a d) -> p t h a d", t=TT, a=2, d=HD)
        K.cmp_v = sb("cmp_v", [N_CMP, N_KV, HD])
        K.cmp_kT = sb("cmp_kT", [P, N_KV, N_CMP])

        K.turned = Signal(sem("turned"))
        K.act_took = Signal(sem("act_took"))
        K.dve_took = Signal(sem("dve_took"))
        K.filled = Signal(sem("filled"))
        K.hidden_ready = Signal(sem("hidden_ready"))
        K.high_turned = Signal(sem("high_turned"))
        K.low_turned = Signal(sem("low_turned"))
        K.act_turned = Signal(sem("act_turned"))
        K.dve_turned = Signal(sem("dve_turned"))
        K.stat_ready = Signal(sem("stat_ready"))
        K.rstd_ready = Signal(sem("rstd_ready"))
        K.hat_ready = Signal(sem("hat_ready"))
        K.square_ready = Signal(sem("square_ready"))
        K.dve_step = Signal(sem("dve_step"))
        K.angle_ready = Signal(sem("angle_ready"))
        K.gates_v = Signal(sem("gates_v"))
        K.gates_a = Signal(sem("gates_a"))
        K.scores_ready = Signal(sem("scores_ready"))
        K.masked_scores = Signal(sem("masked_scores"))
        K.probs_ready = Signal(sem("probs_ready"))
        K.probs_kept = Signal(sem("probs_kept"))
        K.weights_ready = Signal(sem("weights_ready"))
        K.values_ready = Signal(sem("values_ready"))
        K.group_out = Signal(sem("group_out"))
        K.slot_loaded = [sem(f"slot_loaded{i}") for i in range(SLOTS)]
        K.row_loaded = [sem(f"row_loaded{i}") for i in range(ROWS)]
        K.row_loads = [0] * ROWS
        K.high_ready = sem("high_ready")
        K.low_ready = sem("low_ready")
        K.load_used = sem("load_used")
        K.input_loaded = sem("input_loaded")
        K.small_loaded = sem("small_loaded")
        K.zeroed = sem("zeroed")
        K.masked = sem("masked")
        K.p_loaded = sem("p_loaded")
        K.stored = sem("stored")
        K.masked_total, K.p_loads, K.next_load = 0, 0, 0
        K.loads = plan_weights(a)

        def done(level):
            if stop <= level:
                store(K, out)
                return True
            return False

        setup(K, a)
        rows_stage(K, {0: a["mix_ln_g"][0], 1: a["mix_ln_b"][0]})
        full = (stationary(K.xT), KT, [(0, BANK)])

        def take_mlstm(item, t, ps):
            if item in (2, 3):
                dst = K.v_ext[:, t, 2 * (item - 2):2 * (item - 1), 0:M_DV]
                ps = ps.rearrange("p (h d) -> p h d", d=M_DV)
            elif item < 2:
                dst = K.qk[:, t, item * BANK:(item + 1) * BANK]
            else:
                dst = K.o[:, t, (item - 4) * BANK:(item - 4) * BANK + ps.shape[1]]
            if item in (4, 5):
                return nc.scalar.activation(dst, ps, ACT.Sigmoid)
            return nc.scalar.activation(dst, ps, ACT.Copy) if t == 0 else nc.vector.tensor_copy(dst, ps)
        project(K, [full] * 6 + [(stationary(K.xT), KT, [(0, 8)])],
                lambda n, t: "act" if t == 0 or n in (4, 5) else "dve", take_mlstm)
        turn(K, [([K.qk[:, t, k * P:(k + 1) * P] for t in range(TT)], K.qkT[:, k, :], None) for k in range(8)])
        gate_columns(K)
        mlstm(K)
        mlstm_norm(K)
        rows_stage(K, {2: a["mlp_ln_g"][0], 3: a["mlp_ln_b"][0]})
        turn_model(K, K.z, K.col_of["head_g"])
        if done(0):
            return
        model_product(K)
        residual_norm(K, 0, 1)
        if done(1):
            return
        rows_stage(K, {0: a["ple_b_gate"][0]})
        turn_model(K, K.x)
        feed_forward(K, D_FF // 512, 512, False)
        residual_norm(K, 2, 3)
        if done(2):
            return
        turn_model(K, K.x)
        embed(K, a["p"][0, 0], 0, None)
        if done(3):
            return
        turn_model(K, K.x)
        rows_stage(K, {0: a["b_b_q"][0], 1: a["kv_b"], 2: a["b_b_o"][0], 3: a["mix_ln_g"][1]})

        def take_qkv(item, t, ps):
            if item > 0:
                cols = slice((item - 1) * BANK, item * BANK)
                return nc.vector.tensor_tensor(K.uq1[:, t, cols], ps, K.rows[:, 0, cols], ALU.add)
            w = A_KV_HEADS * HD
            nc.vector.tensor_tensor(K.uq1[:, t, D:D + w], ps[:, 0:w], K.rows[:, 1, 0:w], ALU.add)
            return nc.vector.tensor_tensor(K.uv1[:, t, :], ps[:, w:2 * w], K.rows[:, 1, w:2 * w], ALU.add)
        with nc.Block(no_gpsimd_drain=True) as block:
            @block.vector
            def _(dve):
                row_here(K, dve, 0)
                row_here(K, dve, 1)
        project(K, [full] * 3, lambda n, t: "dve", take_qkv)
        with nc.Block(no_gpsimd_drain=True) as block:
            @block.vector
            def _(dve):
                ch = Chain(dve, K.dve_step)
                for t in range(TT):
                    for h0, h in ((0, A_Q_HEADS), (A_Q_HEADS, A_KV_HEADS)):
                        rotate(K, ch, K.uq1[:, t, h0 * HD:(h0 + h) * HD].rearrange("p (h d) -> p h d", d=HD), 0, t)
                    write_twice(K, K.twice[:, t, 0:A_KV_HEADS, :, :], K.uq1[:, t, D:D + A_KV_HEADS * HD])
        turn(K, two_heads(K, K.uq1, 0, A_Q_HEADS, 0) + twice_heads(K, 0, A_KV_HEADS, A_Q_HEADS // 2))
        units, groups = [], []
        for t in range(TT):
            size = (t + 1) * P
            for g in range(A_Q_HEADS // 8):
                for pair in range(4):
                    h = 8 * g + 2 * pair
                    kv = h // (A_Q_HEADS // A_KV_HEADS)
                    vals = [K.uv1[:, s, kv * HD:(kv + 1) * HD] for s in range(t + 1)]
                    units.append(dict(q=halves(K, h // 2, t * P, (t + 1) * P),
                                      k=halves(K, A_Q_HEADS // 2 + kv, 0, size), size=size, bias=None, keep=None,
                                      mask=K.causal[:, P:SEQ] if t == 0 else K.window[:, :], sink=h, v=[vals] * 2))
                groups.append(divided(K, K.z[:, t, g * 512:(g + 1) * 512]))
        rows_stage(K, {1: a["mix_ln_b"][1]})
        attend(K, units, groups)
        turn_model(K, K.z)
        model_product(K)
        residual_norm(K, 3, 1, bias=2)
        if done(4):
            return
        turn_model(K, K.x)
        rows_stage(K, {0: a["mlp_ln_g"][1], 1: a["mlp_ln_b"][1], 2: a["ple_b_gate"][1]})
        feed_forward(K, D_FF // 512, 512, False)
        residual_norm(K, 0, 1)
        if done(5):
            return
        turn_model(K, K.x)
        embed(K, a["p"][1, 0], 2, None)
        if done(6):
            return
        root_norm(K, K.x, [(0, D)], K.z)
        turn_model(K, K.z, K.col_of["ffn1"])
        feed_forward(K, D_FF_2 // 256, 256, True)
        half_step(K)
        if done(7):
            return
        root_norm(K, K.x, [(0, D)], K.z)
        turn_model(K, K.z, K.col_of["mix"])

        def take_in2(item, t, ps):
            for buf, c0, c1, at in IN2_CHUNKS[item][2]:
                dst = (K.uq if buf == "q" else K.uv)[:, t, c0:c1]
                src = ps[:, at:at + c1 - c0]
                last = nc.scalar.activation(dst, src, ACT.Copy) if t == 0 else nc.vector.tensor_copy(dst, src)
            return last
        project(K, [(stationary(K.xT), KT, [(0, n1 - n0)]) for n0, n1, _ in IN2_CHUNKS],
                lambda n, t: "act" if t == 0 else "dve", take_in2)
        fox_gates(K)
        normed_heads(K)
        aQ, aKS, aKW, aQF, aKF = 0, 4, 6, 8, 12
        turn(K, two_heads(K, K.uq, QA, N_Q, aQ) + twice_heads(K, 4, N_KV, aKS)
             + twice_heads(K, 6, N_KV, aKW) + two_heads(K, K.uq, QF, FOX, aQF)
             + two_heads(K, K.uq, KF, FOX, aKF))
        compress(K)
        with nc.Block(no_gpsimd_drain=True) as block:
            @block.scalar
            def _(act):
                for t in range(TT):
                    nc.scalar.activation(K.uv[:, t, GA:VF], K.uv[:, t, GA:VF], ACT.Sigmoid)
        units, groups = [], []
        for t in range(TT):
            q0, q1 = t * P, (t + 1) * P
            size = (t + 1) * P
            causal = K.causal[:, P:SEQ] if t == 0 else K.causal[:, :]
            values = lambda c: [K.uv[:, s, c:c + HD] for s in range(t + 1)]
            for kind in ("cmp", "slc", "win", "fox"):
                for pair in range(4):
                    h = 2 * pair
                    kv = h // (N_Q // N_KV)
                    u = dict(q=halves(K, (aQF if kind == "fox" else aQ) + pair, q0, q1), size=size, mask=causal,
                             bias=None, keep=None, sink=None)
                    if kind == "fox":
                        u.update(k=halves(K, aKF + pair, 0, size),
                                 bias=[(K.sel[:, h + i, :], K.fox_bias[:, 0:size]) for i in range(2)],
                                 v=[values(VF + (h + i) * HD) for i in range(2)])
                    elif kind == "cmp":
                        u.update(k=[K.cmp_kT[i * HD:(i + 1) * HD, kv, :] for i in range(2)], size=N_CMP,
                                 keep=K.cmp_keep[:, t, :], mask=K.cmp_mask[:, t, :], v=[[K.cmp_v[:, kv, :]]] * 2)
                    else:
                        ak, vc = (aKS, VSL) if kind == "slc" else (aKW, VWN)
                        u.update(k=halves(K, ak + kv, 0, size), v=[values(vc + kv * HD)] * 2)
                    units.append(u)
            gate = K.uv[:, t, GA:VF].rearrange("p (h c) -> p h c", c=3)
            for c in range(3):
                groups.append(divided(K, K.z[:, t, 0:512], gate=gate[:, :, c], add=c > 0))
            groups.append(divided(K, K.z[:, t, 512:1024]))
        attend(K, units, groups)
        root_norm(K, K.z, [(0, 512), (512, 1024)], K.z)
        turn_model(K, K.z, K.col_of["out_nsa"])
        model_product(K)
        with nc.Block(no_gpsimd_drain=True) as block:
            @block.vector
            def _(dve):
                for t in range(TT):
                    for h in range(2):
                        s = slice(h * BANK, (h + 1) * BANK)
                        nc.vector.tensor_tensor(K.x[:, t, s], K.psum[:, 2 * t + h, :], K.x[:, t, s], ALU.add)
        if done(8):
            return
        root_norm(K, K.x, [(0, D)], K.z)
        turn_model(K, K.z, K.col_of["ffn2"])
        rows_stage(K, {0: a["ple_norm_2"][0]})
        feed_forward(K, D_FF_2 // 256, 256, True)
        half_step(K)
        if done(9):
            return
        root_norm(K, K.x, [(0, D)], K.z)
        turn_model(K, K.z, K.col_of["ple"])
        embed(K, a["p_2"][0, 0], None, 0)
        store(K, out)


ARENA = 9888
ROWS = 4


def two_heads(K, src, col, heads, at):
    return [([src[:, t, col + j * P:col + (j + 1) * P] for t in range(TT)], K.attT[:, at + j, :], None)
            for j in range(heads // 2)]


def write_twice(K, dst, src):
    r, n = dst.shape[0], dst.shape[1]
    return K.nc.vector.tensor_copy(dst, src.rearrange("p (h d) -> p h d", d=HD).unsqueeze(2).broadcast_to([r, n, 2, HD]))


def twice_heads(K, first, heads, at):
    return [([K.twice[:, t, first + j, :, :].rearrange("p a d -> p (a d)") for t in range(TT)], K.attT[:, at + j, :],
             None) for j in range(heads)]


def halves(K, tile, lo, hi):
    return [K.attT[i * HD:(i + 1) * HD, tile, lo:hi] for i in range(2)]


def divided(K, dst, gate=None, add=False):
    nc = K.nc
    d = dst.rearrange("p (h d) -> p h d", d=HD)

    def run(ch, outputs, sums):
        ch.do(nc.vector.reciprocal(K.recip[:, :], sums))
        if gate is not None:
            ch.do(nc.vector.tensor_tensor(K.recip[:, :], K.recip[:, :], gate, ALU.mult))
        r = K.recip[:, :].unsqueeze(2).broadcast_to([P, 8, HD])
        if not add:
            return nc.vector.tensor_tensor(d, outputs, r, ALU.mult)
        tmp = K.group_tmp[:, :].rearrange("p (h d) -> p h d", d=HD)
        ch.do(nc.vector.tensor_tensor(tmp, outputs, r, ALU.mult))
        return nc.vector.tensor_tensor(d, d, tmp, ALU.add)
    return run


def model_product(K):
    nc = K.nc
    first = K.next_load
    with nc.Block(no_gpsimd_drain=True) as block:

        @block.sync
        def _(sp):
            refill(K, sp, first, 4)

        @block.tensor
        def _(pe):
            for h in range(2):
                for half in range(2):
                    n = first + 2 * h + half
                    weights_here(K, pe, n)
                    w = weight_parts(K, n)[0]
                    for t in range(TT):
                        for k in range(KT // 2):
                            kk = half * KT // 2 + k
                            mm = product(K, K.psum[:, 2 * t + h, :], stationary(K.xT)(kk, t),
                                         [part[:, k, :] for part in w], kk == 0, kk == KT - 1)
                    mm.then_inc(K.load_used, 1)

        @block.scalar
        def _(act):
            for n in range(first, first + 4):
                split_ahead(K, act, "act", n)

        @block.vector
        def _(dve):
            for n in range(first, first + 4):
                split_ahead(K, dve, "dve", n)
    K.next_load += 4


def store(K, out):
    with K.nc.Block(no_gpsimd_drain=True) as block:

        @block.sync
        def _(sp):
            sp.dma_start(out[0].rearrange("(t p) d -> p t d", p=P), K.x[:, :, :]).then_inc(K.stored, 16)
            sp.wait_ge(K.stored, 16)


STOP = 99


def kernel(**inputs):
    import concourse.bacc as bacc
    from concourse.bass_utils import run_bass_kernel_spmd

    nc = bacc.Bacc("TRN2", target_bir_lowering=False, num_devices=1)
    arrays, aps = {}, {}
    for name, value in inputs.items():
        v = np.ascontiguousarray(value)
        arrays[f"in_{name}"] = v
        aps[name] = nc.dram_tensor(f"in_{name}", v.shape, mybir.dt.from_np(v.dtype), kind="ExternalInput").ap()
    out = nc.dram_tensor("out", (1, SEQ, D), F32, kind="ExternalOutput").ap()
    build(nc, aps, out, STOP)
    return run_bass_kernel_spmd(nc, [arrays], core_ids=[0]).results[0]["out"]
```

```python
import math
from contextlib import ExitStack

import numpy as np

import concourse.bass as bass
from concourse import mybir

F32 = mybir.dt.float32
F32R = mybir.dt.float32r
I32 = mybir.dt.int32
ALU = mybir.AluOpType
ACT = mybir.ActivationFunctionType
AX = mybir.AxisListType

P = 128
SEQ = 256
TT = SEQ // P
D = 1024
KT = D // P
BANK = 512
NBANK = 8
DEPTH = 2
ALPHA = (2 * DEPTH) ** 0.25
LN_EPS = 1e-5
RMS_EPS = 1e-6
NEG = -1e30

M_HEADS, M_DK, M_DV, GATE_CAP = 4, 128, 256, 15.0
HD = 64
A_Q_HEADS, A_KV_HEADS = 16, 4
ROT, THETA = HD // 4, 500000.0
HALF = ROT // 2
PLE = 256
D_FF, D_FF_2 = 4096, 2816
N_Q, N_KV, FOX = 8, 2, 8
QA, KC, VC, KSL, KWN, QF, KF, QW = 0, 512, 640, 768, 896, 1024, 1536, 2048
VSL, VWN, GA, VF, FL, VW = 0, 128, 256, 280, 792, 800
IN2_CHUNKS = [
    (0, 512, [("q", QA, KC, 0)]),
    (512, 1024, [("q", KC, KWN, 0), ("v", VSL, VWN, 384)]),
    (1024, 1304, [("q", KWN, QF, 0), ("v", VWN, VF, 128)]),
    (1304, 1816, [("q", QF, KF, 0)]),
    (1816, 2328, [("q", KF, QW, 0)]),
    (2328, 2840, [("v", VF, FL, 0)]),
    (2840, 2848, [("v", FL, VW, 0)]),
]
CMP_BLOCK, CMP_STRIDE, CMP_HID = 32, 16, 256
N_CMP = (SEQ - CMP_BLOCK) // CMP_STRIDE + 1

SLOT = 2048
SLOTS = 4
PARTS = 3
AHEAD = PARTS - 1


class Signal:

    def __init__(self, sem):
        self.sem, self.total = sem, 0


class Chain:

    def __init__(self, eng, steps):
        self.eng, self.steps = eng, steps

    def do(self, ins):
        self.steps.total += 1
        ins.then_inc(self.steps.sem, 1)
        self.eng.wait_ge(self.steps.sem, self.steps.total)


def shares(owners):
    seen, out = {}, []
    for o in owners:
        seen[o] = seen.get(o, 0) + 1
        out.append(seen[o])
    return out


class Kit:
    pass


def rows_of(w):
    return w.rearrange("(k p) n -> p k n", p=P)


def plan_weights(a):
    loads = []

    def load(*pieces):
        assert sum(p.shape[1] * p.shape[2] for p in pieces) <= SLOT
        loads.append(list(pieces))

    def cols(w, n0, n1):
        v = rows_of(w)[:, :, n0:n1]
        n = loads_of(v.shape[1], n1 - n0)
        for i in range(n):
            load(v[:, i * v.shape[1] // n:(i + 1) * v.shape[1] // n, :])

    def mlp(up, down, hid, width):
        def piece_up(c):
            for i in range(2):
                load(*[rows_of(w)[:, i * KT // 2:(i + 1) * KT // 2, c * width:(c + 1) * width] for w in up])

        def piece_down(c):
            cols(down[c * width:(c + 1) * width, :], 0, D)
        n = hid // width
        piece_up(0)
        for c in range(n):
            if c + 1 < n:
                piece_up(c + 1)
            piece_down(c)

    def ple(gate, proj):
        cols(proj, 0, D)
        for c in range(2):
            cols(gate, c * BANK, (c + 1) * BANK)

    for n0 in range(0, 3072, BANK):
        cols(a["a_w_in"][0], n0, n0 + BANK)
    cols(a["a_w_in"][0], 3072, 3080)
    for c in range(2):
        cols(a["a_w_out"][0], c * BANK, (c + 1) * BANK)
    mlp([a["mlp_w_up"][0]], a["mlp_w_down"][0], D_FF, 512)
    ple(a["ple_w_gate"][0], a["ple_w_proj"][0])
    cols(a["kv_w"], 0, BANK)
    for c in range(2):
        cols(a["b_w_q"][0], c * BANK, (c + 1) * BANK)
    for c in range(2):
        cols(a["b_w_o"][0], c * BANK, (c + 1) * BANK)
    mlp([a["mlp_w_up"][1]], a["mlp_w_down"][1], D_FF, 512)
    ple(a["ple_w_gate"][1], a["ple_w_proj"][1])
    mlp([a["ffn1_wg_2"][0], a["ffn1_wu_2"][0]], a["ffn1_wd_2"][0], D_FF_2, 256)
    for n0, n1, _ in IN2_CHUNKS:
        cols(a["w_in_2"][0], n0, n1)
    cols(a["cmp_k_w1_2"][0], 0, CMP_HID)
    cols(a["cmp_v_w1_2"][0], 0, CMP_HID)
    load(rows_of(a["cmp_k_w2_2"][0]), rows_of(a["cmp_v_w2_2"][0]))
    for c in range(2):
        cols(a["w_out_2"][0], c * BANK, (c + 1) * BANK)
    mlp([a["ffn2_wg_2"][0], a["ffn2_wu_2"][0]], a["ffn2_wd_2"][0], D_FF_2, 256)
    ple(a["ple_w_gate_2"][0], a["ple_w_proj_2"][0])
    return loads


def loads_of(k, n):
    return 1 if k * n <= SLOT else 2


def pieces_in(K, n, slot):
    out, at = [], 0
    for src in K.loads[n]:
        k, w = src.shape[1], src.shape[2]
        out.append(slot[:, at:at + k * w].rearrange("p (k n) -> p k n", k=k))
        at += k * w
    return out


def weight_parts(K, n):
    return list(zip(pieces_in(K, n, K.wh[:, n % PARTS, :]), pieces_in(K, n, K.wl[:, n % PARTS, :])))


def load_weights(K, sp, n):
    if n < len(K.loads):
        for dst, src in zip(pieces_in(K, n, K.ring[:, n % SLOTS, :]), K.loads[n]):
            sp.dma_start(dst, src).then_inc(K.slot_loaded[n % SLOTS], 16)


def load_size(K, n):
    return sum(p.shape[1] * p.shape[2] for p in K.loads[n])


def split_high(K, act, n):
    if n < len(K.loads):
        act.wait_ge(K.slot_loaded[n % SLOTS], 16 * sum(len(K.loads[m]) for m in range(n % SLOTS, n + 1, SLOTS)))
        if n >= PARTS:
            act.wait_ge(K.load_used, n - PARTS + 1)
        w = load_size(K, n)
        K.nc.scalar.activation(K.wh[:, n % PARTS, 0:w], K.ring[:, n % SLOTS, 0:w], ACT.Copy).then_inc(K.high_ready, 1)


def split_low(K, dve, n):
    if n < len(K.loads):
        dve.wait_ge(K.high_ready, n + 1)
        w = load_size(K, n)
        K.nc.vector.tensor_tensor(K.wl[:, n % PARTS, 0:w], K.ring[:, n % SLOTS, 0:w],
                                  K.wh[:, n % PARTS, 0:w].bitcast(F32), ALU.subtract).then_inc(K.low_ready, 1)


def split_ahead(K, eng, name, n):
    (split_high if name == "act" else split_low)(K, eng, n + AHEAD)


def weights_here(K, pe, n):
    pe.wait_ge(K.low_ready, n + 1)


def product(K, out, x, w, start, stop):
    nc = K.nc
    nc.tensor.matmul(out, x[0], w[0], start=start, stop=False)
    nc.tensor.matmul(out, x[0], w[1], start=False, stop=False)
    return nc.tensor.matmul(out, x[1], w[0], start=False, stop=stop)


def refill(K, sp, first, count):
    for n in range(first + AHEAD, first + AHEAD + count):
        if n < len(K.loads):
            sp.wait_ge(K.low_ready, n + 1)
            load_weights(K, sp, n + SLOTS)


def tile_order(h):
    order = [(half, t) for half in range(2) for t in range(TT)]
    return order if h == 0 else sorted(order, key=lambda item: item[1])


def up_half(K, where, gated, n, half, t):
    g = 2 if gated else 1
    out = K.psum[:, where, :].rearrange("p (g n) -> p g n", g=g)
    w = [part[:, n % PARTS, :].rearrange("p (g k n) -> p k g n", g=g, k=KT // 2) for part in (K.wh, K.wl)]
    for k in range(KT // 2):
        kk = half * KT // 2 + k
        mm = product(K, out, [x[:, kk, t * P:(t + 1) * P] for x in K.xT], [part[:, k, :, :] for part in w],
                     kk == 0, kk == KT - 1)
    return mm


def turn(K, items, along=None):
    nc = K.nc
    with nc.Block(no_gpsimd_drain=True) as block:
        turned, taken = K.turned.total, {"act": K.act_took.total, "dve": K.dve_took.total}
        who = ["act" if i % 2 == 0 else "dve" for i in range(len(items))]
        nth = shares(who)

        @block.tensor
        def _(pe):
            for i, (srcs, dst, scale) in enumerate(items):
                if i >= NBANK:
                    j = i - NBANK
                    pe.wait_ge((K.act_took if who[j] == "act" else K.dve_took).sem, taken[who[j]] + nth[j])
                for t, src in enumerate(srcs):
                    last = nc.tensor.transpose(K.psum[0:dst.shape[0], i % NBANK, t * src.shape[0]:(t + 1) * src.shape[0]],
                                               src, K.ident[0:src.shape[0], 0:src.shape[0]])
                last.then_inc(K.turned.sem, 1)

        def copy(eng, i):
            srcs, dst, scale = items[i]
            ps = K.psum[0:dst.shape[0], i % NBANK, 0:len(srcs) * srcs[0].shape[0]]
            eng.wait_ge(K.turned.sem, turned + i + 1)
            if who[i] == "act":
                if scale is None:
                    nc.scalar.activation(dst, ps, ACT.Copy).then_inc(K.act_took.sem, 1)
                else:
                    nc.scalar.activation(dst, ps, ACT.Copy, scale=scale).then_inc(K.act_took.sem, 1)
            elif scale is None:
                nc.vector.tensor_copy(dst, ps).then_inc(K.dve_took.sem, 1)
            else:
                nc.vector.tensor_scalar(dst, ps, scale, None, ALU.mult).then_inc(K.dve_took.sem, 1)

        @block.scalar
        def _(act):
            for i in range(0, len(items), 2):
                copy(act, i)
                if along:
                    along["act"](act, i)

        @block.vector
        def _(dve):
            for i in range(1, len(items), 2):
                copy(dve, i)
                if along:
                    along["dve"](dve, i)

    K.turned.total += len(items)
    K.act_took.total += who.count("act")
    K.dve_took.total += who.count("dve")


def turn_parts(K, items):
    nc = K.nc
    with nc.Block(no_gpsimd_drain=True) as block:
        turned, high0, low0 = K.turned.total, K.high_turned.total, K.low_turned.total

        @block.tensor
        def _(pe):
            for i, (srcs, dst, scale) in enumerate(items):
                if i >= NBANK:
                    pe.wait_ge(K.low_turned.sem, low0 + i - NBANK + 1)
                for t, src in enumerate(srcs):
                    p, w = src.shape
                    last = nc.tensor.transpose(K.psum[0:w, i % NBANK, t * p:(t + 1) * p], src, K.ident[0:p, 0:p])
                last.then_inc(K.turned.sem, 1)

        def bank_of(i):
            srcs = items[i][0]
            return K.psum[0:srcs[0].shape[1], i % NBANK, 0:len(srcs) * srcs[0].shape[0]]

        @block.scalar
        def _(act):
            for i, (srcs, dst, scale) in enumerate(items):
                act.wait_ge(K.turned.sem, turned + i + 1)
                nc.scalar.activation(dst[0], bank_of(i), ACT.Copy,
                                     scale=1.0 if scale is None else scale).then_inc(K.high_turned.sem, 1)

        @block.vector
        def _(dve):
            for i, (srcs, dst, scale) in enumerate(items):
                dve.wait_ge(K.high_turned.sem, high0 + i + 1)
                nc.vector.scalar_tensor_tensor(dst[1], bank_of(i), 1.0 if scale is None else scale,
                                               dst[0].bitcast(F32), ALU.mult,
                                               ALU.subtract).then_inc(K.low_turned.sem, 1)

    K.turned.total += len(items)
    K.high_turned.total += len(items)
    K.low_turned.total += len(items)


def turn_model(K, src, scale_col=None):
    turn_parts(K, [([src[:, t, k * P:(k + 1) * P] for t in range(TT)], (K.xT[0][:, k, :], K.xT[1][:, k, :]),
                    None if scale_col is None else K.cols[:, scale_col + k:scale_col + k + 1]) for k in range(KT)])


def project(K, groups, who, take, rows={}, needed=(), along=None, prime=()):
    nc = K.nc
    first = K.next_load
    items, group_loads, n = [], [], first
    for g, (stat, kt, spans) in enumerate(groups):
        m = loads_of(kt, spans[-1][1])
        group_loads.append(range(n, n + m))
        n += m
        items += [(g, span, t) for span in spans for t in range(TT)]
    count = n - first
    owners = [who(i // TT, t) for i, (_, _, t) in enumerate(items)]
    nth = shares(owners)
    closes = [i + 1 == len(items) or items[i + 1][0] != items[i][0] for i in range(len(items))]
    filled0, took = K.filled.total, {"act": K.act_took.total, "dve": K.dve_took.total}
    led, K.led = K.led, False
    with nc.Block(no_gpsimd_drain=True) as block:

        @block.sync
        def _(sp):
            load_rows(K, sp, rows)
            if prime:
                refill(K, sp, first - AHEAD, AHEAD)
            refill(K, sp, first, count)

        @block.tensor
        def _(pe):
            for g, (stat, kt, spans) in enumerate(groups):
                mine = [i for i, it in enumerate(items) if it[0] == g]
                ks = kt // len(group_loads[g])
                for half, n in enumerate(group_loads[g]):
                    weights_here(K, pe, n)
                    w = weight_parts(K, n)[0]
                    for i in mine:
                        _, (lo, hi), t = items[i]
                        if led and i == 0:
                            continue
                        if half == 0 and i >= NBANK:
                            j = i - NBANK
                            pe.wait_ge((K.act_took if owners[j] == "act" else K.dve_took).sem,
                                       took[owners[j]] + nth[j])
                        for k in range(ks):
                            kk = half * ks + k
                            mm = product(K, K.psum[:, i % NBANK, 0:hi - lo], stat(kk, t),
                                         [part[:, k, lo:hi] for part in w], kk == 0, kk == kt - 1)
                        if i == mine[-1]:
                            mm.then_inc(K.load_used, 1)
                        elif half == len(group_loads[g]) - 1:
                            mm.then_inc(K.filled.sem, 1)

        def engine(eng, name):
            for n in prime:
                (split_high if name == "act" else split_low)(K, eng, n)
            for g in range(len(groups)):
                if name == "dve" and g < len(needed):
                    row_here(K, eng, needed[g])
                for n in group_loads[g]:
                    split_ahead(K, eng, name, n)
                for i, (gi, (lo, hi), t) in enumerate(items):
                    if gi == g and owners[i] == name:
                        if closes[i]:
                            eng.wait_ge(K.load_used, group_loads[g][-1] + 1)
                        else:
                            eng.wait_ge(K.filled.sem, filled0 + sum(not c for c in closes[:i + 1]))
                        take(i // TT, t, K.psum[:, i % NBANK, 0:hi - lo]).then_inc(
                            (K.act_took if name == "act" else K.dve_took).sem, 1)
                if along and name in along:
                    along[name](eng, g)

        @block.scalar
        def _(act):
            engine(act, "act")

        @block.vector
        def _(dve):
            engine(dve, "dve")

        @block.gpsimd
        def _(pool):
            for g in range(len(groups)):
                if along and "pool" in along:
                    along["pool"](pool, g)

    K.filled.total += sum(not c for c in closes)
    K.act_took.total += owners.count("act")
    K.dve_took.total += owners.count("dve")
    K.next_load += count


def feed_forward(K, count, width, gated, tail, embedding=False, rows={}):
    nc = K.nc
    jt = width // P
    npair = jt // 2
    nd = loads_of(jt, D)
    first = K.next_load
    up_load = lambda c: first + (0 if c == 0 else 2 + (c - 1) * (2 + nd))
    down_load = lambda c: first + 2 + c * (2 + nd) + (2 if c + 1 < count else 0)
    total = count * (2 + nd)
    fill0, act0, hid0 = K.filled.total, K.act_took.total, K.hidden_ready.total
    turned0, high0, low0 = K.turned.total, K.high_turned.total, K.low_turned.total
    hid, rel, hidT = K.hid, K.rel, K.hidT
    K.filled.total += count
    K.act_took.total += TT * count
    K.hidden_ready.total += TT * count
    K.turned.total += npair * count
    K.high_turned.total += npair * count
    K.low_turned.total += npair * count
    K.next_load += total
    emb_load, emb_fill0, emb_took0 = K.next_load, K.filled.total, K.act_took.total
    if embedding:
        K.filled.total += 2 * TT - 1
        K.act_took.total += 2 * TT
        K.next_load += 1
    emb_bank = [0, 1, 6, 7]
    sums0, led = K.sums_ready.total, K.led
    K.sums_ready.total += 1

    def sums(eng, t, h):
        if t == 0:
            eng.wait_ge(K.sums_ready.sem, sums0 + 1)
        else:
            eng.wait_ge(K.load_used, first + total)
    follow = tail(sums)
    bank_of = lambda c, q: 6 + (npair * c + q) % 2

    def up_ready(eng, c, t):
        if t == 0:
            eng.wait_ge(K.filled.sem, fill0 + c + 1)
        else:
            eng.wait_ge(K.load_used, up_load(c) + 2)

    def steps():
        yield from [("split", up_load(0)), ("hidden", 0, 0), ("split", up_load(0) + 1), ("hidden", 0, 1)]
        for c in range(count):
            if c + 1 < count:
                yield from [("split", up_load(c + 1)), ("hidden", c + 1, 0)]
            yield ("parts", c)
            if c + 1 < count:
                yield from [("split", up_load(c + 1) + 1), ("hidden", c + 1, 1)]
            for i in range(nd):
                if down_load(c) + i + 1 < first + total:
                    yield ("split", down_load(c) + i)

    with nc.Block(no_gpsimd_drain=True) as block:

        @block.sync
        def _(sp):
            load_rows(K, sp, rows)
            refill(K, sp, first, total + embedding)

        @block.tensor
        def _(pe):
            def up(c, t):
                if c >= 1:
                    if gated:
                        pe.wait_ge(K.hidden_ready.sem, hid0 + TT * (c - 1) + t + 1)
                    else:
                        pe.wait_ge(K.act_took.sem, act0 + TT * (c - 1) + t + 1)
                if led and c == 0 and t == 0:
                    return
                for half in range(2):
                    n = up_load(c) + half
                    weights_here(K, pe, n)
                    mm = up_half(K, 4 + t, gated, n, half, t)
                    if t == 1:
                        mm.then_inc(K.load_used, 1)
                    elif half == 1:
                        mm.then_inc(K.filled.sem, 1)

            def turn_hidden(c):
                pe.wait_ge(K.hidden_ready.sem, hid0 + TT * (c + 1))
                for q in range(npair):
                    i = npair * c + q
                    if i >= 2:
                        pe.wait_ge(K.low_turned.sem, low0 + i - 1)
                    for j in range(2):
                        for t in range(TT):
                            tr = nc.tensor.transpose(K.psum[:, bank_of(c, q), (2 * j + t) * P:(2 * j + t + 1) * P],
                                                     hid[:, c % 2, t, (2 * q + j) * P:(2 * q + j + 1) * P],
                                                     K.ident[:, :])
                    tr.then_inc(K.turned.sem, 1)

            def down_tile(c, t):
                for j in range(jt):
                    n = down_load(c) + j * nd // jt
                    if t == 0 and j % (jt // nd) == 0:
                        weights_here(K, pe, n)
                    if t == 0 and j % 2 == 0:
                        pe.wait_ge(K.low_turned.sem, low0 + npair * c + j // 2 + 1)
                    w = weight_parts(K, n)[0]
                    for h in range(2):
                        mm = product(K, K.psum[:, 2 * t + h, :],
                                     [x[:, c % 2, j, t * P:(t + 1) * P] for x in hidT],
                                     [part[:, j % (jt // nd), h * BANK:(h + 1) * BANK] for part in w],
                                     False, c == count - 1 and j == jt - 1)
                    if t == 1 and (j + 1) % (jt // nd) == 0:
                        mm.then_inc(K.load_used, 1)
                if t == 0 and c == count - 1:
                    mm.then_inc(K.sums_ready.sem, 1)

            def embedding_product(t):
                if not embedding:
                    return
                n = emb_load
                weights_here(K, pe, n)
                w = weight_parts(K, n)[0]
                if t == 0:
                    follow.sums_read(pe)
                for h in range(2):
                    i = 2 * t + h
                    for k in range(PLE // P):
                        mm = product(K, K.psum[:, emb_bank[i], :], stationary(K.pT)(k, t),
                                     [part[:, k, h * BANK:(h + 1) * BANK] for part in w], k == 0, k == PLE // P - 1)
                    mm.then_inc(K.load_used if i == 2 * TT - 1 else K.filled.sem, 1)
                if t == TT - 1:
                    pe.wait_ge(K.act_took.sem, emb_took0 + 2 * TT)

            def down(c):
                for j in range(jt):
                    n = down_load(c) + j * nd // jt
                    if j % (jt // nd) == 0:
                        weights_here(K, pe, n)
                    if j % 2 == 0:
                        pe.wait_ge(K.low_turned.sem, low0 + npair * c + j // 2 + 1)
                    w = weight_parts(K, n)[0]
                    for t in range(TT):
                        for h in range(2):
                            mm = product(K, K.psum[:, 2 * t + h, :],
                                         [x[:, c % 2, j, t * P:(t + 1) * P] for x in hidT],
                                         [part[:, j % (jt // nd), h * BANK:(h + 1) * BANK] for part in w],
                                         c == 0 and j == 0, False)
                    if (j + 1) % (jt // nd) == 0:
                        mm.then_inc(K.load_used, 1)

            for t in range(TT):
                up(0, t)
            for c in range(count):
                if c + 1 < count:
                    up(c + 1, 0)
                turn_hidden(c)
                if c + 1 < count:
                    up(c + 1, 1)
                if gated and c == count - 2:
                    down_tile(c, 0)
                elif c + 1 < count:
                    down(c)
                else:
                    down_tile(c, 0)
                    if gated:
                        down_tile(c - 1, 1)
                    down_tile(c, 1)
            follow.pe(pe, [lambda pe: embedding_product(0), lambda pe: embedding_product(1)])

        @block.scalar
        def _(act):
            for step, *args in steps():
                if step == "split":
                    split_ahead(K, act, "act", *args)
                elif step == "hidden":
                    c, t = args
                    up_ready(act, c, t)
                    if c >= 1:
                        act.wait_ge(K.hidden_ready.sem, hid0 + TT * (c - 1) + t + 1)
                    nc.scalar.activation(rel[:, t, 0:width], K.psum[:, 4 + t, 0:width],
                                         ACT.Silu if gated else ACT.Relu,
                                         scale=K.rstd[:, t:t + 1] if gated else 1.0).then_inc(K.act_took.sem, 1)
                else:
                    c, = args
                    for q in range(npair):
                        act.wait_ge(K.turned.sem, turned0 + npair * c + q + 1)
                        if c >= 2:
                            act.wait_ge(K.load_used, down_load(c - 2) + nd)
                        nc.scalar.activation(hidT[0][:, c % 2, 2 * q:2 * q + 2, :],
                                             K.psum[:, bank_of(c, q), :].rearrange("p (j n) -> p j n", j=2),
                                             ACT.Copy).then_inc(K.high_turned.sem, 1)
            def copies(act, t):
                for i in range(2 * t, 2 * t + 2 if embedding else 0):
                    if i == 2 * TT - 1:
                        act.wait_ge(K.load_used, emb_load + 1)
                    else:
                        act.wait_ge(K.filled.sem, emb_fill0 + i + 1)
                    h = i % 2
                    nc.scalar.activation(K.e[:, t, h * BANK:(h + 1) * BANK], K.psum[:, emb_bank[i], :],
                                         ACT.Copy).then_inc(K.act_took.sem, 1)

            def with_first(act):
                for n in range(first + total - 1, first + total + embedding):
                    split_ahead(K, act, "act", n)
                copies(act, 0)
            follow.act(act, [with_first, lambda act: copies(act, 1)])

        @block.vector
        def _(dve):
            for step, *args in steps():
                if step == "split":
                    split_ahead(K, dve, "dve", *args)
                elif step == "hidden":
                    c, t = args
                    dve.wait_ge(K.act_took.sem, act0 + TT * c + t + 1)
                    if c >= 2:
                        dve.wait_ge(K.turned.sem, turned0 + npair * (c - 1))
                    if gated:
                        nc.vector.scalar_tensor_tensor(hid[:, c % 2, t, 0:width], K.psum[:, 4 + t, width:2 * width],
                                                       K.rstd[:, t:t + 1], rel[:, t, 0:width], ALU.mult,
                                                       ALU.mult).then_inc(K.hidden_ready.sem, 1)
                    else:
                        nc.vector.tensor_tensor(hid[:, c % 2, t, 0:width], rel[:, t, 0:width], rel[:, t, 0:width],
                                                ALU.mult).then_inc(K.hidden_ready.sem, 1)
                else:
                    c, = args
                    for q in range(npair):
                        dve.wait_ge(K.high_turned.sem, high0 + npair * c + q + 1)
                        at = (slice(None), c % 2, slice(2 * q, 2 * q + 2), slice(None))
                        nc.vector.tensor_tensor(hidT[1][at],
                                                K.psum[:, bank_of(c, q), :].rearrange("p (j n) -> p j n", j=2),
                                                hidT[0][at].bitcast(F32), ALU.subtract).then_inc(K.low_turned.sem, 1)
            follow.dve(dve, [lambda dve: split_ahead(K, dve, "dve", first + total - 1),
                             lambda dve: split_ahead(K, dve, "dve", emb_load) if embedding else None])

        @block.gpsimd
        def _(pool):
            follow.pool(pool)


class Tail:

    def __init__(self, K, kind, ready, gain=None, shift=None, bias=None, step=None, column=None, lead=None):
        self.K, self.kind, self.ready, self.lead = K, kind, ready, lead
        self.gain, self.shift, self.bias, self.step, self.column = gain, shift, bias, step, column
        self.scaled = column is not None
        self.stat0, self.rstd0 = K.stat_ready.total, K.rstd_ready.total
        self.rows0, self.square0 = K.rows_ready.total, K.square_ready.total
        self.turned0, self.high0, self.low0 = K.turned.total, K.high_turned.total, K.low_turned.total
        self.lead_load = K.next_load
        if kind == "layer":
            K.stat_ready.total += TT
            K.rows_ready.total += 2 * TT
        if kind == "root":
            K.rows_ready.total += 2 * TT if step is not None else 0
            K.square_ready.total += 2 * TT
        if kind != "plain":
            K.rstd_ready.total += TT
        K.turned.total += 2 * TT
        K.high_turned.total += 2 * TT
        K.low_turned.total += 2 * TT
        K.led = lead is not None


    def update(self, dve, ch, t):
        K, nc = self.K, self.K.nc
        for h in range(2):
            s = slice(h * BANK, (h + 1) * BANK)
            if self.kind == "layer":
                self.ready(dve, t, h)
                m = nc.vector.scalar_tensor_tensor(K.z[:, t, s], K.x[:, t, s], ALPHA, K.psum[:, 2 * t + h, :],
                                                   ALU.mult, ALU.add)
                if h == 1:
                    ch.do(m)
            elif self.step is not None:
                self.ready(dve, t, h)
                nc.vector.scalar_tensor_tensor(K.x[:, t, s], K.psum[:, 2 * t + h, :], self.step, K.x[:, t, s],
                                               ALU.mult, ALU.add).then_inc(K.rows_ready.sem, 1)

    def norm(self, dve, ch, t):
        if self.kind != "layer":
            return
        K, nc = self.K, self.K.nc
        z = K.z[:, t, :]
        if self.bias is not None:
            row_here(K, dve, self.bias)
            ch.do(nc.vector.tensor_tensor(z, z, K.rows[:, self.bias, :], ALU.add))
        for h in range(2):
            m = nc.vector.bn_stats(K.bn[:, t, h, :], z[:, h * BANK:(h + 1) * BANK])
        ch.do(m)
        ch.do(nc.vector.bn_aggr(K.stat[:, t, 0:2], K.bn[:, t, :, :]))
        nc.vector.tensor_scalar(K.stat[:, t, 1:2], K.stat[:, t, 1:2], LN_EPS, None,
                                ALU.add).then_inc(K.stat_ready.sem, 1)
        if t == 0:
            row_here(K, dve, self.gain)
        for h in range(2):
            s = slice(h * BANK, (h + 1) * BANK)
            m = nc.vector.scalar_tensor_tensor(K.z[:, t, s], K.z[:, t, s], K.stat[:, t, 0:1],
                                               K.rows[:, self.gain, s], ALU.subtract, ALU.mult)
        ch.do(m)
        dve.wait_ge(K.rstd_ready.sem, self.rstd0 + t + 1)
        if t == 0:
            row_here(K, dve, self.shift)
        for h in range(2):
            s = slice(h * BANK, (h + 1) * BANK)
            nc.vector.scalar_tensor_tensor(K.x[:, t, s], K.z[:, t, s], K.rstd[:, t:t + 1],
                                           K.rows[:, self.shift, s], ALU.mult, ALU.add).then_inc(K.rows_ready.sem, 1)

    def low(self, dve, t):
        K, nc = self.K, self.K.nc
        for h in range(2):
            dve.wait_ge(K.high_turned.sem, self.high0 + 2 * t + h + 1)
            for first, n in self.tiles(h):
                dst = [x[:, first:first + n, t * P:(t + 1) * P] for x in K.xT]
                ps = self.bank(t, h, first, n)
                m = nc.vector.scalar_tensor_tensor(dst[1], ps, self.scale(first), dst[0].bitcast(F32), ALU.mult,
                                                   ALU.subtract)
            m.then_inc(K.low_turned.sem, 1)


    def square(self, act, t):
        K, nc = self.K, self.K.nc
        if self.kind == "root":
            for h in range(2):
                s = slice(h * BANK, (h + 1) * BANK)
                self.rows(act, t, h)
                nc.scalar.activation(K.hid_flat[:, t, s], K.x[:, t, s], ACT.Square,
                                     accum_out=K.stat[:, t, h:h + 1]).then_inc(K.square_ready.sem, 1)

    def high(self, act, t):
        K, nc = self.K, self.K.nc
        for h in range(2):
            act.wait_ge(K.turned.sem, self.turned0 + 2 * t + h + 1)
            for first, n in self.tiles(h):
                m = nc.scalar.activation(K.xT[0][:, first:first + n, t * P:(t + 1) * P],
                                         self.bank(t, h, first, n), ACT.Copy, scale=self.scale(first))
            m.then_inc(K.high_turned.sem, 1)


    def pool(self, pool):
        K, nc = self.K, self.K.nc
        if self.kind == "plain":
            return
        for t in range(TT):
            if self.kind == "layer":
                pool.wait_ge(K.stat_ready.sem, self.stat0 + t + 1)
                src = K.stat[:, t, 1:2]
            else:
                src = K.stat[:, t, 2:3]
                ch = Chain(pool, K.pool_step)
                pool.wait_ge(K.square_ready.sem, self.square0 + 2 * t + 2)
                ch.do(nc.gpsimd.tensor_tensor(src, K.stat[:, t, 0:1], K.stat[:, t, 1:2], ALU.add))
                ch.do(nc.gpsimd.tensor_scalar(src, src, 1.0 / D, RMS_EPS, ALU.mult, ALU.add))
            nc.gpsimd.tensor_tensor(K.rstd[:, t:t + 1], src, K.minus_half[:, 0:1],
                                    ALU.pow).then_inc(K.rstd_ready.sem, 1)
        pool.wait_ge(K.rstd_ready.sem, self.rstd0 + TT)


    def rows(self, eng, t, h):
        if self.kind == "layer" or self.step is not None:
            eng.wait_ge(self.K.rows_ready.sem, self.rows0 + 2 * t + h + 1)
        else:
            self.ready(eng, t, h)

    def sums_read(self, eng):
        if self.kind == "layer":
            eng.wait_ge(self.K.stat_ready.sem, self.stat0 + 1)
        else:
            self.rows(eng, 0, 1)

    def turn(self, pe, t, halves=(0, 1)):
        K, nc = self.K, self.K.nc
        for h in halves:
            self.rows(pe, t, h)
            for k in range(KT // 2):
                kk = h * KT // 2 + k
                tr = nc.tensor.transpose(K.psum[:, 4 + 2 * t + h, k * P:(k + 1) * P], K.x[:, t, kk * P:(kk + 1) * P],
                                         K.ident[:, :])
            tr.then_inc(K.turned.sem, 1)

    def run_lead(self, pe, half):
        K = self.K
        if self.lead is not None:
            where, gated = self.lead
            pe.wait_ge(K.low_turned.sem, self.low0 + 2)
            weights_here(K, pe, self.lead_load + half)
            mm = up_half(K, where, gated, self.lead_load + half, half, 0)
            if half == 1:
                mm.then_inc(K.filled.sem, 1)


    def dve(self, dve, more=()):
        ch = Chain(dve, self.K.dve_step)
        self.update(dve, ch, 0)
        self.norm(dve, ch, 0)
        for step in more[0:1]:
            step(dve)
        self.update(dve, ch, 1)
        self.low(dve, 0)
        for step in more[1:2]:
            step(dve)
        self.norm(dve, ch, 1)
        self.low(dve, 1)

    def act(self, act, more=()):
        self.square(act, 0)
        for step in more[0:1]:
            step(act)
        self.high(act, 0)
        for step in more[1:2]:
            step(act)
        self.square(act, 1)
        self.high(act, 1)

    def pe(self, pe, more=()):
        for step in more[0:1]:
            step(pe)
        self.turn(pe, 0)
        for step in more[1:2]:
            step(pe)
        early = self.kind != "layer" and self.step is None
        if early:
            self.turn(pe, 1, [0])
        self.run_lead(pe, 0)
        self.turn(pe, 1, [1] if early else [0, 1])
        self.run_lead(pe, 1)


    def tiles(self, h):
        n = KT // 2
        return [(h * n + k, 1) for k in range(n)] if self.scaled else [(h * n, n)]

    def bank(self, t, h, first, n):
        at = first - h * KT // 2
        return self.K.psum[:, 4 + 2 * t + h, at * P:(at + n) * P].rearrange("p (k n) -> p k n", k=n)

    def scale(self, first):
        return self.K.cols[:, self.column + first:self.column + first + 1] if self.scaled else 1.0


def root_norm(K, src, widths, dst):
    nc = K.nc
    n = len(widths)
    with nc.Block(no_gpsimd_drain=True) as block:
        sq0, stat0, rstd0 = K.square_ready.total, K.stat_ready.total, K.rstd_ready.total

        @block.scalar
        def _(act):
            for t in range(TT):
                for i, (lo, hi) in enumerate(widths):
                    nc.scalar.activation(K.scratch[:, t, lo:hi], src[:, t, lo:hi], ACT.Square,
                                         accum_out=K.stat[:, t, i:i + 1]).then_inc(K.square_ready.sem, 1)

        @block.vector
        def _(dve):
            for t in range(TT):
                dve.wait_ge(K.square_ready.sem, sq0 + n * (t + 1))
                for i, (lo, hi) in enumerate(widths):
                    last = nc.vector.tensor_scalar(K.stat[:, t, 2 + i:3 + i], K.stat[:, t, i:i + 1], 1.0 / (hi - lo),
                                                   RMS_EPS, ALU.mult, ALU.add)
                last.then_inc(K.stat_ready.sem, 1)
            for t in range(TT):
                dve.wait_ge(K.rstd_ready.sem, rstd0 + t + 1)
                for i, (lo, hi) in enumerate(widths):
                    nc.vector.tensor_scalar(dst[:, t, lo:hi], src[:, t, lo:hi], K.stat[:, t, 4 + i:5 + i], None,
                                            ALU.mult)

        @block.gpsimd
        def _(pool):
            for t in range(TT):
                pool.wait_ge(K.stat_ready.sem, stat0 + t + 1)
                nc.gpsimd.tensor_tensor(K.stat[:, t, 4:4 + n], K.stat[:, t, 2:2 + n], K.minus_half[:, 0:n],
                                        ALU.pow).then_inc(K.rstd_ready.sem, 1)
            pool.wait_ge(K.rstd_ready.sem, rstd0 + TT)

    K.square_ready.total += n * TT
    K.stat_ready.total += TT
    K.rstd_ready.total += TT


def row_here(K, eng, r):
    eng.wait_ge(K.row_loaded[r], 16 * K.row_loads[r])


def load_rows(K, sp, which):
    for r, vec in which.items():
        w = vec.shape[0]
        sp.dma_start(K.rows[:, r, 0:w], vec.partition_broadcast(P)).then_inc(K.row_loaded[r], 16)
        K.row_loads[r] += 1


def setup(K, a):
    nc = K.nc
    lists = [("head_g", a["a_head_norm_g"][0]), ("ffn1", a["ffn1_norm_2"][0]), ("mix", a["mix_norm_2"][0]),
             ("out_nsa", a["out_norm_nsa_2"][0]), ("out_fox", a["out_norm_fox_2"][0]), ("ffn2", a["ffn2_norm_2"][0]),
             ("ple", a["ple_gate_norm_2"][0]), ("pos_k", a["cmp_pos_k_2"][0].rearrange("j d -> (j d)")),
             ("pos_v", a["cmp_pos_v_2"][0].rearrange("j d -> (j d)"))]
    K.col_of, n = {}, 0
    for name, vec in lists:
        K.col_of[name] = n
        n += vec.shape[0] // P
    K.n_cols = n
    with nc.Block(no_gpsimd_drain=True) as block:

        @block.sync
        def _(sp):
            load_weights(K, sp, 0)
            sp.dma_start(K.x[:, :, :], a["x"][0].rearrange("(t p) d -> p t d", p=P)).then_inc(K.input_loaded, 16)
            for n in range(1, SLOTS):
                load_weights(K, sp, n)
            for name, vec in lists:
                c, m = K.col_of[name], vec.shape[0] // P
                sp.dma_start(K.z[c:c + m, 0, 0:P], vec.rearrange("(k p) -> k p", p=P)).then_inc(K.small_loaded, 16)
            sp.dma_start(K.positions[:, :], a["positions"][0].rearrange("(t p) -> p t", p=P),
                          allow_slow_non_contiguous=True).then_inc(K.small_loaded, 16)
            sp.dma_start(K.gate_bias[0:M_HEADS, 0:1], a["a_b_igate"][0].unsqueeze(1)).then_inc(K.small_loaded, 16)
            sp.dma_start(K.gate_bias[0:M_HEADS, 1:2], a["a_b_fgate"][0].unsqueeze(1)).then_inc(K.small_loaded, 16)
            sp.dma_start(K.gate_bias[0:FOX, 2:3], a["b_forget_2"][0].unsqueeze(1)).then_inc(K.small_loaded, 16)
            sp.dma_start(K.sinks[:, :], a["b_sinks"][0].partition_broadcast(P)).then_inc(K.small_loaded, 16)
            for i, name in enumerate(["q_norm_nsa_2", "k_norm_slc_2", "k_norm_win_2", "q_norm_fox_2", "k_norm_fox_2",
                                      "k_norm_cmp_2"]):
                sp.dma_start(K.head_gain[:, i, :], a[name][0].partition_broadcast(P)).then_inc(K.small_loaded, 16)

        @block.scalar
        def _(act):
            split_high(K, act, 0)

        @block.vector
        def _(dve):
            for ap, value in [(K.ident[:, :], 0.0), (K.sel[:, :, :], 0.0), (K.ones[:, :], 1.0), (K.fox_bias[:, :], 0.0),
                              (K.minus_half[:, :], -0.5), (K.causal[:, :], 0.0), (K.window[:, :], 0.0),
                              (K.causal_t[:, :], 0.0), (K.cmp_mask[:, :, :], 0.0), (K.cmp_keep[:, :, :], 1.0),
                              (K.v_ext[:, :, :, :], 1.0)]:
                last = nc.vector.memset(ap, value)
            for i in range(HALF):
                last = nc.vector.memset(K.inv_freq[:, i:i + 1], float(np.float32(THETA) ** np.float32(-i * 2.0 / ROT)))
            last.then_inc(K.zeroed, 1)
            split_low(K, dve, 0)

        @block.gpsimd
        def _(pool):
            pool.wait_ge(K.zeroed, 1)

            def select(out, src, pattern, base, mult, fill, op=ALU.is_ge):
                K.masked_total += 1
                nc.gpsimd.affine_select(out=out, in_=src, compare_op=op, fill=fill, base=base, pattern=pattern,
                                        channel_multiplier=mult).then_inc(K.masked, 1)
                pool.wait_ge(K.masked, K.masked_total)

            select(K.ident[:, :], K.ident[:, :], [[-1, P]], 0, 1, 1.0, ALU.not_equal)
            select(K.sel[:, :, :], K.sel[:, :, :], [[-1, FOX], [0, P]], 0, 1, 1.0, ALU.not_equal)
            select(K.causal[:, :], K.causal[:, :], [[-1, SEQ]], P, 1, NEG)
            select(K.window[:, :], K.causal[:, :], [[1, SEQ]], 0, -1, NEG, ALU.is_gt)
            select(K.causal_t[:, 0:P], K.causal_t[:, 0:P], [[1, P]], 0, -1, NEG)
            select(K.causal_t[:, 2 * P:3 * P], K.causal_t[:, 2 * P:3 * P], [[1, P]], 0, -1, NEG)
            for t in range(TT):
                pat = [[-CMP_STRIDE, N_CMP]]
                select(K.cmp_mask[:, t, :], K.cmp_mask[:, t, :], pat, t * P - CMP_BLOCK + 1, 1, NEG)
                select(K.cmp_keep[:, t, :], K.cmp_keep[:, t, :], pat, t * P - CMP_BLOCK + 1, 1, 0.0)
            nc.gpsimd.iota(K.index[:, :], [[P, TT]], base=0, channel_multiplier=1).then_inc(K.masked, 1)
            K.masked_total += 1
            pool.wait_ge(K.masked, K.masked_total)

        @block.tensor
        def _(pe):
            pe.wait_ge(K.input_loaded, 16)

    K.small_loads = len(lists) + 11
    turn_model(K, K.x)


def rotary_tables(K):
    nc = K.nc
    ready0 = K.angle_ready.total
    K.angle_ready.total += 1

    def dve(eng, g):
        if g == 1:
            eng.wait_ge(K.small_loaded, 16 * K.small_loads)
            ch = Chain(eng, K.dve_step)
            A = K.angle
            ch.do(nc.vector.tensor_copy(K.pos_f[:, 0:TT], K.positions[:, :]))
            ch.do(nc.vector.tensor_copy(K.pos_f[:, TT:2 * TT], K.index[:, :]))
            for i in range(2 * TT):
                ch.do(nc.vector.tensor_scalar(A[:, 0, i * HALF:(i + 1) * HALF], K.inv_freq[:, :],
                                              K.pos_f[:, i:i + 1], None, ALU.mult))
            for which, shift in ((1, 0.25), (2, 0.0)):
                ch.do(nc.vector.tensor_scalar(A[:, 3, :], A[:, 0, :], 1.0 / (2 * math.pi), shift, ALU.mult, ALU.add))
                ch.do(nc.vector.tensor_scalar(A[:, 3, :], A[:, 3, :], ROUND, None, ALU.add))
                ch.do(nc.vector.tensor_scalar(A[:, 3, :], A[:, 3, :], ROUND, None, ALU.subtract))
                ch.do(nc.vector.scalar_tensor_tensor(A[:, which, :], A[:, 3, :], -TWO_PI[0], A[:, 0, :],
                                                     ALU.mult, ALU.add))
                ch.do(nc.vector.scalar_tensor_tensor(A[:, which, :], A[:, 3, :], -TWO_PI[1], A[:, which, :],
                                                     ALU.mult, ALU.add))
                ch.do(nc.vector.scalar_tensor_tensor(A[:, which, :], A[:, 3, :], -TWO_PI[2], A[:, which, :],
                                                     ALU.mult, ALU.add))
                if which == 1:
                    ch.do(nc.vector.tensor_scalar(A[:, which, :], A[:, which, :], math.pi / 2, None, ALU.add))
                ch.do(nc.vector.tensor_scalar(A[:, which, :], A[:, which, :], PI_BELOW, -PI_BELOW, ALU.min, ALU.max))
            nc.vector.tensor_copy(A[:, 4, :], A[:, 1, :]).then_inc(K.angle_ready.sem, 1)

    def act(eng, g):
        if g == 2:
            eng.wait_ge(K.angle_ready.sem, ready0 + 1)
            nc.scalar.activation(K.cos_sin[:, 0, :], K.angle[:, 1, :], ACT.Sin)
            nc.scalar.activation(K.cos_sin[:, 1, :], K.angle[:, 2, :], ACT.Sin)

    return {"dve": dve, "act": act}


ROUND = 1.5 * 2.0 ** 23
TWO_PI = [6.28125, float(np.float32(2 * math.pi - 6.28125)),
          float(2 * math.pi - 6.28125 - float(np.float32(2 * math.pi - 6.28125)))]
PI_BELOW = 3.1415925


def rotate(K, ch, heads, table, t):
    nc = K.nc
    n = heads.shape[1]
    at = (table * TT + t) * HALF
    cos, sin = [K.cos_sin[:, i, at:at + HALF].unsqueeze(1).broadcast_to([P, n, HALF]) for i in range(2)]
    a, b = heads[:, :, 0:HALF], heads[:, :, HALF:ROT]
    w = [K.rot[:, i, 0:n, :] for i in range(4)]
    nc.vector.tensor_tensor(w[0], a, cos, ALU.mult)
    nc.vector.tensor_tensor(w[1], b, sin, ALU.mult)
    nc.vector.tensor_tensor(w[2], b, cos, ALU.mult)
    ch.do(nc.vector.tensor_tensor(w[3], a, sin, ALU.mult))
    nc.vector.tensor_tensor(a, w[0], w[1], ALU.subtract)
    ch.do(nc.vector.tensor_tensor(b, w[2], w[3], ALU.add))


def gate_columns(K):
    nc = K.nc
    H = M_HEADS
    with nc.Block(no_gpsimd_drain=True) as block:
        turned, step0, act0 = K.turned.total, K.gates_v.total, K.gates_a.total

        @block.tensor
        def _(pe):
            for i in range(2):
                for t in range(TT):
                    tr = nc.tensor.transpose(K.psum[0:H, 0, (i * TT + t) * P:(i * TT + t + 1) * P],
                                             K.o[:, t, D + i * H:D + (i + 1) * H], K.ident[:, :])
            tr.then_inc(K.turned.sem, 1)
            pe.wait_ge(K.gates_v.sem, step0 + 3)
            for i, r in enumerate((1, 3)):
                for t in range(TT):
                    at = (i * TT + t) * H
                    tr = nc.tensor.transpose(K.psum[:, 1, at:at + H], K.gates[0:H, r, t * P:(t + 1) * P],
                                             K.ident[0:H, 0:H])
            tr.then_inc(K.turned.sem, 1)

        @block.vector
        def _(dve):
            ch = Chain(dve, K.dve_step)
            G = K.gates
            nc.vector.tensor_scalar(K.gate_bias[0:H, 0:2], K.gate_bias[0:H, 0:2], 1.0 / GATE_CAP, None,
                                    ALU.mult).then_inc(K.gates_v.sem, 1)
            dve.wait_ge(K.gates_a.sem, act0 + 3)
            ch.do(nc.vector.tensor_tensor_scan(G[0:H, 5, :], K.ones[0:H, :], G[0:H, 6, :], 0.0, ALU.mult,
                                               ALU.subtract))
            ch.do(nc.vector.scalar_tensor_tensor(G[0:H, 1, :], G[0:H, 0, 0:SEQ], GATE_CAP, G[0:H, 5, :], ALU.mult,
                                                 ALU.subtract))
            ch.do(nc.vector.tensor_tensor_scan(G[0:H, 4, :], G[0:H, 1, :], G[0:H, 1, :], 0.0, ALU.max, ALU.max))
            nc.vector.tensor_scalar(G[0:H, 2, :], G[0:H, 4, :], -1.0, None, ALU.mult).then_inc(K.gates_v.sem, 1)
            nc.vector.scalar_tensor_tensor(G[0:H, 3, :], G[0:H, 4, :], -1.0, G[0:H, 5, :], ALU.mult,
                                           ALU.subtract).then_inc(K.gates_v.sem, 1)
            dve.wait_ge(K.turned.sem, turned + 2)
            nc.vector.tensor_copy(K.u_col[:, :], K.psum[:, 1, 0:TT * H]).then_inc(K.gates_v.sem, 1)

        @block.scalar
        def _(act):
            G = K.gates
            act.wait_ge(K.turned.sem, turned + 1)
            act.wait_ge(K.gates_v.sem, step0 + 1)
            nc.scalar.activation(G[0:H, 0, :], K.psum[0:H, 0, 0:SEQ], ACT.Tanh, bias=K.gate_bias[0:H, 0:1],
                                 scale=1.0 / GATE_CAP)
            nc.scalar.activation(G[0:H, 7, :], K.psum[0:H, 0, SEQ:2 * SEQ], ACT.Tanh, bias=K.gate_bias[0:H, 1:2],
                                 scale=1.0 / GATE_CAP).then_inc(K.gates_a.sem, 1)
            act.wait_ge(K.gates_a.sem, act0 + 1)
            nc.scalar.activation(G[0:H, 7, :], G[0:H, 7, :], ACT.Exp, scale=-GATE_CAP).then_inc(K.gates_a.sem, 1)
            act.wait_ge(K.gates_a.sem, act0 + 2)
            nc.scalar.activation(G[0:H, 6, :], G[0:H, 7, :], ACT.Ln, bias=1.0).then_inc(K.gates_a.sem, 1)
            act.wait_ge(K.gates_v.sem, step0 + 4)
            nc.scalar.activation(K.exp_m[:, :], K.psum[:, 1, TT * H:2 * TT * H], ACT.Exp)

    K.turned.total += 2
    K.gates_v.total += 4
    K.gates_a.total += 3


def mlstm(K):
    nc = K.nc
    H, W = M_HEADS, 3 * P
    pieces = ((0, 0, SEQ, 0), (1, P, SEQ, SEQ))
    with nc.Block(no_gpsimd_drain=True) as block:
        scores0, arg0, expd0, weight0 = K.scores_ready.total, K.masked_scores.total, K.probs_ready.total, \
            K.weights_ready.total
        out0, took0 = K.values_ready.total, K.act_took.total

        @block.tensor
        def _(pe):
            def scores(h):
                if h >= 2:
                    pe.wait_ge(K.weights_ready.sem, weight0 + h - 1)
                for s, q0, q1, at in pieces:
                    nc.tensor.matmul(K.psum[:, h % 2, at:at + q1 - q0], K.qkT[:, H + h, s * P:(s + 1) * P],
                                     K.qkT[:, h, q0:q1], start=True, stop=True)
                    mm = nc.tensor.matmul(K.psum[:, 2 + h % 2, at:at + q1 - q0], K.sel[0:H, h, :],
                                          K.gates[0:H, 2, q0:q1], start=True, stop=True)
                mm.then_inc(K.scores_ready.sem, 1)

            def values(h):
                pe.wait_ge(K.weights_ready.sem, weight0 + h + 1)
                if h >= 2:
                    pe.wait_ge(K.act_took.sem, took0 + TT * (h - 1))
                w = K.decayed[:, h % 2, :]
                b = 4 + 2 * (h % 2)
                nc.tensor.matmul(K.psum[:, b, 0:M_DV + 1], w[:, 0:P], K.v_ext[:, 0, h, :], start=True, stop=True)
                nc.tensor.matmul(K.psum[:, b + 1, 0:M_DV + 1], w[:, P:2 * P], K.v_ext[:, 0, h, :],
                                 start=True, stop=False)
                nc.tensor.matmul(K.psum[:, b + 1, 0:M_DV + 1], w[:, 2 * P:3 * P], K.v_ext[:, 1, h, :],
                                 start=False, stop=True).then_inc(K.values_ready.sem, 1)

            scores(0)
            for h in range(H):
                if h + 1 < H:
                    scores(h + 1)
                values(h)

        @block.vector
        def _(dve):
            def exponent(h):
                dve.wait_ge(K.scores_ready.sem, scores0 + h + 1)
                if h >= 2:
                    dve.wait_ge(K.probs_ready.sem, expd0 + h - 1)
                nc.vector.scalar_tensor_tensor(K.exponent[:, h % 2, 0:SEQ], K.psum[:, 2 + h % 2, 0:SEQ],
                                               K.u_col[:, h:h + 1], K.causal_t[:, 0:SEQ], ALU.add, ALU.add)
                nc.vector.scalar_tensor_tensor(K.exponent[:, h % 2, SEQ:W], K.psum[:, 2 + h % 2, SEQ:W],
                                               K.u_col[:, H + h:H + h + 1], K.causal_t[:, SEQ:W], ALU.add,
                                               ALU.add).then_inc(K.masked_scores.sem, 1)

            def weigh(h):
                dve.wait_ge(K.probs_ready.sem, expd0 + h + 1)
                if h >= 2:
                    dve.wait_ge(K.values_ready.sem, out0 + h - 1)
                nc.vector.scalar_tensor_tensor(K.decayed[:, h % 2, :], K.psum[:, h % 2, 0:W], M_DK ** -0.5,
                                               K.decay[:, h % 2, :], ALU.mult,
                                               ALU.mult).then_inc(K.weights_ready.sem, 1)

            ch = Chain(dve, K.dve_step)

            def gate(h):
                dve.wait_ge(K.act_took.sem, took0 + TT * (h + 1))
                for t in range(TT):
                    m = nc.vector.bn_stats(K.bn8[:, t * H + h, :], K.h_raw[:, t, h, 0:M_DV])
                ch.do(m)
                for t in range(TT):
                    m = nc.vector.bn_aggr(K.mean_var[:, t * H + h, :], K.bn8[:, t * H + h, :])
                ch.do(m)
                for t in range(TT):
                    nc.vector.scalar_tensor_tensor(K.h_raw[:, t, h, 0:M_DV], K.h_raw[:, t, h, 0:M_DV],
                                                   K.mean_var[:, t * H + h, 0:1],
                                                   K.o[:, t, h * M_DV:(h + 1) * M_DV], ALU.subtract, ALU.mult)

            exponent(0)
            for h in range(H):
                if h + 1 < H:
                    exponent(h + 1)
                weigh(h)
                if h >= 1:
                    gate(h - 1)
            gate(H - 1)

        @block.scalar
        def _(act):
            def decay(h):
                act.wait_ge(K.masked_scores.sem, arg0 + h + 1)
                if h >= 2:
                    act.wait_ge(K.weights_ready.sem, weight0 + h - 1)
                nc.scalar.activation(K.decay[:, h % 2, :], K.exponent[:, h % 2, :],
                                     ACT.Exp).then_inc(K.probs_ready.sem, 1)

            def copy_out(h):
                act.wait_ge(K.values_ready.sem, out0 + h + 1)
                for t in range(TT):
                    nc.scalar.activation(K.h_raw[:, t, h, :], K.psum[:, 4 + 2 * (h % 2) + t, 0:M_DV + 1],
                                         ACT.Copy).then_inc(K.act_took.sem, 1)

            decay(0)
            for h in range(H):
                if h + 1 < H:
                    decay(h + 1)
                copy_out(h)

    K.scores_ready.total += H
    K.masked_scores.total += H
    K.probs_ready.total += H
    K.weights_ready.total += H
    K.values_ready.total += H
    K.act_took.total += TT * H


def mlstm_norm(K):
    nc = K.nc
    H, n = M_HEADS, TT * M_HEADS
    with nc.Block(no_gpsimd_drain=True) as block:
        stat0, rstd0 = K.stat_ready.total, K.rstd_ready.total
        S = K.mstat

        @block.vector
        def _(dve):
            ch = Chain(dve, K.dve_step)
            var = K.mean_var[:, :, 1]
            for t in range(TT):
                den = K.h_raw[:, t, :, M_DV]
                ch.do(nc.vector.scalar_tensor_tensor(S[:, 0, t * H:(t + 1) * H], den, -1.0, den, ALU.mult, ALU.max))
            ch.do(nc.vector.tensor_tensor(S[:, 0, :], S[:, 0, :], K.exp_m[:, :], ALU.max))
            ch.do(nc.vector.reciprocal(S[:, 1, :], S[:, 0, :]))
            ch.do(nc.vector.tensor_tensor(S[:, 2, :], S[:, 1, :], S[:, 1, :], ALU.mult))
            ch.do(nc.vector.tensor_tensor(S[:, 2, :], S[:, 2, :], var, ALU.mult))
            nc.vector.tensor_scalar(S[:, 2, :], S[:, 2, :], LN_EPS, None, ALU.add).then_inc(K.stat_ready.sem, 1)
            dve.wait_ge(K.rstd_ready.sem, rstd0 + 1)
            ch.do(nc.vector.tensor_tensor(S[:, 4, :], S[:, 3, :], S[:, 1, :], ALU.mult))
            nc.vector.tensor_copy(S[:, 2, :], S[:, 4, :]).then_inc(K.stat_ready.sem, 1)
            for h in range(H):
                i = H + h
                nc.vector.tensor_scalar(K.z[:, 1, h * M_DV:(h + 1) * M_DV], K.h_raw[:, 1, h, 0:M_DV],
                                        S[:, 4, i:i + 1], None, ALU.mult)

        @block.scalar
        def _(act):
            act.wait_ge(K.stat_ready.sem, stat0 + 2)
            for h in range(H):
                nc.scalar.activation(K.z[:, 0, h * M_DV:(h + 1) * M_DV], K.h_raw[:, 0, h, 0:M_DV], ACT.Copy,
                                     scale=S[:, 2, h:h + 1])

        @block.gpsimd
        def _(pool):
            pool.wait_ge(K.stat_ready.sem, stat0 + 1)
            nc.gpsimd.tensor_tensor(S[:, 3, :], S[:, 2, :], K.minus_half[:, 0:n], ALU.pow).then_inc(K.rstd_ready.sem, 1)
            pool.wait_ge(K.rstd_ready.sem, rstd0 + 1)

    K.stat_ready.total += 2
    K.rstd_ready.total += 1


def attend(K, units, groups, rows={}):
    nc = K.nc
    n = len(units)
    with nc.Block(no_gpsimd_drain=True) as block:
        sc0, ms0, pr0, kp0 = K.scores_ready.total, K.masked_scores.total, K.probs_ready.total, K.probs_kept.total
        rd0 = K.scores_read.total
        tu0, ac0, vc0 = K.turned.total, K.act_turned.total, K.dve_turned.total
        va0, og0 = K.values_ready.total, K.group_out.total
        kept = lambda i: sum(1 for u in units[:i] if u["keep"] is not None)
        columns = lambda u: u["size"] + (u["sink"] is not None)
        tiles = lambda u: [(s, min(P, u["size"] - s)) for s in range(0, u["size"], P)]

        def copied(eng, i):
            if i % 2 == 0:
                eng.wait_ge(K.act_turned.sem, ac0 + i // 2 + 1)
            else:
                eng.wait_ge(K.dve_turned.sem, vc0 + i // 2 + 1)

        @block.sync
        def _(sp):
            load_rows(K, sp, rows)

        @block.tensor
        def _(pe):
            def scores(i):
                u = units[i]
                if i >= 2:
                    pe.wait_ge(K.scores_read.sem, rd0 + i - 1)
                out = [K.psum[:, 2 * (i % 2) + a, 0:u["size"]] for a in range(2)]
                if u["bias"] is not None:
                    for a in range(2):
                        nc.tensor.matmul(out[a], *u["bias"][a], start=True, stop=False)
                for a in range(2):
                    mm = nc.tensor.matmul(out[a], u["q"][a], u["k"][a], start=u["bias"] is None, stop=True)
                mm.then_inc(K.scores_ready.sem, 1)

            def turn_probs(i):
                u = units[i]
                pe.wait_ge(K.probs_ready.sem, pr0 + i + 1)
                if u["keep"] is not None:
                    pe.wait_ge(K.probs_kept.sem, kp0 + kept(i) + 1)
                if i >= 2:
                    copied(pe, i - 2)
                for a in range(2):
                    for j, (s, w) in enumerate(tiles(u)):
                        tr = nc.tensor.transpose(K.psum[0:w, 4 + i % 2, (2 * a + j) * P:(2 * a + j + 1) * P],
                                                 K.probs[:, i % 3, a, s:s + w], K.ident[:, :])
                tr.then_inc(K.turned.sem, 1)

            def values(i):
                u = units[i]
                copied(pe, i)
                g = i // 4
                if i % 4 == 0 and g >= 2:
                    pe.wait_ge(K.group_out.sem, og0 + g - 1)
                for a in range(2):
                    for j, (s, w) in enumerate(tiles(u)):
                        at = (2 * (i % 4) + a) * HD
                        mm = nc.tensor.matmul(K.psum[:, 6 + g % 2, at:at + HD],
                                              K.probsT[0:w, i % 2, (2 * a + j) * P:(2 * a + j + 1) * P],
                                              u["v"][a][j], start=(j == 0), stop=(j == len(tiles(u)) - 1))
                mm.then_inc(K.values_ready.sem, 1)

            for i in range(n + 3):
                if i < n:
                    scores(i)
                if 0 <= i - 2 < n:
                    turn_probs(i - 2)
                if 0 <= i - 3 < n:
                    values(i - 3)

        def copy(eng, i):
            u = units[i]
            eng.wait_ge(K.turned.sem, tu0 + i + 1)
            if i >= 2:
                eng.wait_ge(K.values_ready.sem, va0 + i - 1)
            w = min(P, u["size"])
            if u["size"] > P:
                src, dst = K.psum[:, 4 + i % 2, :], K.probsT[:, i % 2, :]
            else:
                src, dst = [z.rearrange("p (a j q) -> p a j q", a=2, j=2)[:, :, 0, :]
                            for z in (K.psum[0:w, 4 + i % 2, :], K.probsT[0:w, i % 2, :])]
            if i % 2 == 0:
                nc.scalar.activation(dst, src, ACT.Copy).then_inc(K.act_turned.sem, 1)
            else:
                nc.vector.tensor_copy(dst, src).then_inc(K.dve_turned.sem, 1)

        @block.scalar
        def _(act):
            for i in range(n + 2):
                if i < n:
                    u = units[i]
                    act.wait_ge(K.masked_scores.sem, ms0 + i + 1)
                    if i >= 3:
                        act.wait_ge(K.turned.sem, tu0 + i - 2)
                    for a in range(2):
                        at = slice(0, columns(u))
                        e = nc.scalar.activation(K.probs[:, i % 3, a, at], K.s_sb[:, i % 3, a, at], ACT.Exp,
                                                 bias=K.neg_max[:, 2 * i + a:2 * i + a + 1],
                                                 accum_out=K.sums[:, 2 * i + a:2 * i + a + 1])
                    e.then_inc(K.probs_ready.sem, 1)
                if 0 <= i - 2 < n and i % 2 == 0:
                    copy(act, i - 2)

        @block.vector
        def _(dve):
            ch = Chain(dve, K.dve_step)
            for i in range(n + 5):
                if i < n:
                    u = units[i]
                    w = u["size"]
                    dve.wait_ge(K.scores_ready.sem, sc0 + i + 1)
                    if i >= 3:
                        dve.wait_ge(K.probs_ready.sem, pr0 + i - 2)
                    s_sb = K.s_sb[:, i % 3, :, :]
                    if u["sink"] is not None:
                        nc.vector.tensor_copy(s_sb[:, :, w:w + 1],
                                              K.sinks[:, u["sink"]:u["sink"] + 2].unsqueeze(2))
                    ps = K.psum[:, 2 * (i % 2):2 * (i % 2) + 2, 0:w]
                    nc.vector.scalar_tensor_tensor(s_sb[:, :, 0:w], ps, HD ** -0.5,
                                                   u["mask"].unsqueeze(1).broadcast_to([P, 2, w]), ALU.mult,
                                                   ALU.add).then_inc(K.scores_read.sem, 1)
                    dve.wait_ge(K.scores_read.sem, rd0 + i + 1)
                    nc.vector.tensor_reduce(K.neg_max[:, 2 * i:2 * i + 2], s_sb[:, :, 0:columns(u)], AX.X, ALU.max,
                                            negate=True).then_inc(K.masked_scores.sem, 1)
                if 0 <= i - 1 < n and units[i - 1]["keep"] is not None:
                    dve.wait_ge(K.probs_ready.sem, pr0 + i)
                    w = units[i - 1]["size"]
                    p = K.probs[:, (i - 1) % 3, :, 0:w]
                    nc.vector.tensor_tensor(p, p, units[i - 1]["keep"].unsqueeze(1).broadcast_to([P, 2, w]),
                                            ALU.mult).then_inc(K.probs_kept.sem, 1)
                if 0 <= i - 2 < n and i % 2 == 1:
                    copy(dve, i - 2)
                if 0 <= i - 4 < n and (i - 4) % 4 == 3:
                    g = (i - 4) // 4
                    dve.wait_ge(K.values_ready.sem, va0 + i - 3)
                    at = slice(8 * g, 8 * g + 8)
                    groups[g](ch, K.psum[:, 6 + g % 2, :].rearrange("p (h d) -> p h d", d=HD),
                              K.sums[:, at]).then_inc(K.group_out.sem, 1)

    K.scores_ready.total += n
    K.masked_scores.total += n
    K.scores_read.total += n
    K.probs_ready.total += n
    K.probs_kept.total += kept(n)
    K.turned.total += n
    K.act_turned.total += (n + 1) // 2
    K.dve_turned.total += n // 2
    K.values_ready.total += n
    K.group_out.total += n // 4


def fox_gates(K):
    nc = K.nc
    G = K.gates
    v0, a0, took0 = K.gates_v.total, K.gates_a.total, K.act_took.total
    K.gates_v.total += 1
    K.gates_a.total += 2

    def dve(eng, i):
        ch = Chain(eng, K.dve_step)
        if i == 1:
            eng.wait_ge(K.act_took.sem, took0 + 1)
            ch.do(nc.vector.tensor_scalar(G[:, 0, :], G[:, 6, :], K.gate_bias[0:FOX, 2:3], None, ALU.add))
            nc.vector.scalar_tensor_tensor(G[:, 1, :], G[:, 0, :], -1.0, G[:, 0, :], ALU.mult,
                                           ALU.max).then_inc(K.gates_v.sem, 1)
            ch.do(nc.vector.tensor_scalar(G[:, 3, :], G[:, 0, :], 0.0, None, ALU.min))
        if i == 13:
            eng.wait_ge(K.gates_a.sem, a0 + 2)
            ch.do(nc.vector.tensor_tensor(G[:, 4, :], G[:, 3, :], G[:, 2, :], ALU.subtract))
            ch.do(nc.vector.tensor_tensor_scan(G[:, 5, :], K.ones[0:FOX, :], G[:, 4, :], 0.0, ALU.mult, ALU.add))
            nc.vector.tensor_scalar(K.fox_bias[0:FOX, :], G[:, 5, :], -HD ** 0.5, None, ALU.mult)

    def act(eng, i):
        if i == 4:
            eng.wait_ge(K.gates_v.sem, v0 + 1)
            nc.scalar.activation(G[:, 7, :], G[:, 1, :], ACT.Exp, scale=-1.0).then_inc(K.gates_a.sem, 1)
        if i == 6:
            eng.wait_ge(K.gates_a.sem, a0 + 1)
            nc.scalar.activation(G[:, 2, :], G[:, 7, :], ACT.Ln, bias=1.0).then_inc(K.gates_a.sem, 1)

    return {"dve": dve, "act": act}


def normed_heads(K):
    nc = K.nc
    chunks = [(QA, N_Q, 0), (KSL, N_KV, 1), (KWN, N_KV, 2), (QF, FOX, 3), (KF, FOX, 4)]
    at = [sum(h for _, h, _ in chunks[:g]) for g in range(len(chunks))]
    sq0, st0, rs0 = K.square_ready.total, K.stat_ready.total, K.rstd_ready.total
    act0, dve0 = K.act_took.total, K.dve_took.total
    K.square_ready.total += TT * len(chunks)
    K.stat_ready.total += TT * len(chunks)
    K.rstd_ready.total += TT * len(chunks)

    def heads(buf, t, c, h):
        return buf[:, t, c:c + h * HD].rearrange("p (h d) -> p h d", d=HD)

    def act(eng, g):
        if g == 3:
            for t in range(TT):
                nc.scalar.activation(K.uv[:, t, GA:VF], K.uv[:, t, GA:VF], ACT.Sigmoid)
        if g < len(chunks):
            c, h, _ = chunks[g]
            eng.wait_ge(K.act_took.sem, act0 + g + 1)
            for t in range(TT):
                if t == 1:
                    eng.wait_ge(K.dve_took.sem, dve0 + g + 1)
                nc.scalar.activation(K.squares[:, t, c:c + h * HD], K.uq[:, t, c:c + h * HD],
                                     ACT.Square).then_inc(K.square_ready.sem, 1)

    def norm(eng, ch, g):
        c, h, gain = chunks[g]
        for t in range(TT):
            x = heads(K.uq, t, c, h)
            eng.wait_ge(K.rstd_ready.sem, rs0 + TT * g + t + 1)
            ch.do(nc.vector.tensor_tensor(x, x, K.head_ms[:, t, 2, at[g]:at[g] + h].unsqueeze(2).broadcast_to(
                [P, h, HD]), ALU.mult))
            if gain < 3:
                rotate(K, ch, x, 1, t)
            if g == 2:
                write_twice(K, K.twice[:, t, :, :, :], K.uq[:, t, KC:QF])

    def dve(eng, g):
        ch = Chain(eng, K.dve_step)
        if 1 <= g <= len(chunks):
            norm(eng, ch, g - 1)
        if g < len(chunks):
            c, h, gain = chunks[g]
            for t in range(TT):
                eng.wait_ge(K.square_ready.sem, sq0 + TT * g + t + 1)
                ch.do(nc.vector.tensor_reduce(K.head_ms[:, t, 0, at[g]:at[g] + h], heads(K.squares, t, c, h), AX.X,
                                              ALU.add))
                nc.vector.tensor_scalar(K.head_ms[:, t, 1, at[g]:at[g] + h], K.head_ms[:, t, 0, at[g]:at[g] + h],
                                        1.0 / HD, RMS_EPS, ALU.mult, ALU.add).then_inc(K.stat_ready.sem, 1)
            for t in range(TT):
                if g == 1:
                    rotate(K, ch, heads(K.uq, t, KC, N_KV), 1, t)
                x = heads(K.uq, t, c, h)
                ch.do(nc.vector.tensor_tensor(x, x, K.head_gain[:, gain, :].unsqueeze(1).broadcast_to([P, h, HD]),
                                              ALU.mult))

    def pool(eng, g):
        if g < len(chunks):
            h = chunks[g][1]
            for t in range(TT):
                eng.wait_ge(K.stat_ready.sem, st0 + TT * g + t + 1)
                nc.gpsimd.tensor_tensor(K.head_ms[:, t, 2, at[g]:at[g] + h], K.head_ms[:, t, 1, at[g]:at[g] + h],
                                        K.minus_half[:, 0:h], ALU.pow).then_inc(K.rstd_ready.sem, 1)
        if g == len(chunks):
            eng.wait_ge(K.rstd_ready.sem, rs0 + TT * len(chunks))

    return {"act": act, "dve": dve, "pool": pool}


def compress(K):
    nc = K.nc
    first = K.next_load
    nb = N_KV * N_CMP
    JJ = CMP_BLOCK // 2
    with nc.Block(no_gpsimd_drain=True) as block:
        turned, took = K.turned.total, K.act_took.total

        @block.tensor
        def _(pe):
            for i, c in enumerate((KC, VC)):
                for h in range(N_KV):
                    for t in range(TT):
                        head = K.twice[:, t, (c - KC) // HD + h, :, :].rearrange("p a d -> p (a d)")
                        tr = nc.tensor.transpose(K.psum[:, i, (h * TT + t) * P:(h * TT + t + 1) * P], head,
                                                 K.ident[:, :])
                tr.then_inc(K.turned.sem, 1)

        @block.scalar
        def _(act):
            for i in range(2):
                act.wait_ge(K.turned.sem, turned + i + 1)
                ps = K.psum[:, i, :].rearrange("p (h n) -> p h n", n=SEQ)
                nc.scalar.activation(K.kc2[0:HD, i, :, :], ps[0:HD, :, :], ACT.Copy)
                nc.scalar.activation(K.kc2[HD:P, i, :, 0:SEQ - 1], ps[HD:P, :, 1:SEQ],
                                     ACT.Copy).then_inc(K.act_took.sem, 1)

        @block.vector
        def _(dve):
            ch = Chain(dve, K.dve_step)
            for which, pos in ((0, K.col_of["pos_k"]), (1, K.col_of["pos_v"])):
                dve.wait_ge(K.act_took.sem, took + which + 1)
                for h in range(N_KV):
                    tok = K.kc2[:, which, h, :].rearrange("p (n s) -> p s n", s=CMP_STRIDE)
                    for half in range(2):
                        js = slice(half * JJ // 2, (half + 1) * JJ // 2)
                        last = nc.vector.tensor_tensor(
                            K.block_sum[:, which, js, h * N_CMP:(h + 1) * N_CMP],
                            tok[:, 0:CMP_STRIDE:2, half:half + N_CMP],
                            K.cols[:, pos + half * JJ // 2:pos + (half + 1) * JJ // 2].unsqueeze(2).broadcast_to(
                                [P, JJ // 2, N_CMP]), ALU.add)
                ch.do(last)
                ch.do(nc.vector.tensor_copy(K.blocks[0][:, which, :, :], K.block_sum[:, which, :, :]))
                nc.vector.tensor_tensor(K.blocks[1][:, which, :, :], K.block_sum[:, which, :, :],
                                        K.blocks[0][:, which, :, :].bitcast(F32), ALU.subtract)
    K.turned.total += 2
    K.act_took.total += 2

    with nc.Block(no_gpsimd_drain=True) as block:
        a0, t0, v0 = K.act_took.total, K.turned.total, K.dve_took.total
        st0, rs0 = K.stat_ready.total, K.rstd_ready.total

        @block.sync
        def _(sp):
            refill(K, sp, first, 5)

        @block.tensor
        def _(pe):
            for which in range(2):
                for half in range(2):
                    n = first + 2 * which + half
                    weights_here(K, pe, n)
                    w1 = weight_parts(K, n)[0]
                    for j in range(JJ // 2):
                        jj = half * JJ // 2 + j
                        mm = product(K, K.psum[0:nb, which, 0:CMP_HID], [x[:, which, jj, :] for x in K.blocks],
                                     [part[:, j, :] for part in w1], jj == 0, jj == JJ - 1)
                    mm.then_inc(K.load_used, 1)
            for which in range(2):
                pe.wait_ge(K.act_took.sem, a0 + which + 1)
                for k in range(2):
                    tr = nc.tensor.transpose(K.psum[:, 2 + which, k * P:k * P + nb],
                                             K.cmp_hid[0:nb, which, k * P:(k + 1) * P], K.ident[0:nb, 0:nb])
                tr.then_inc(K.turned.sem, 1)
            weights_here(K, pe, first + 4)
            for which in range(2):
                pe.wait_ge(K.dve_took.sem, v0 + which + 1)
                w2 = weight_parts(K, first + 4)[which]
                for h in range(N_KV):
                    for k in range(2):
                        mm = product(K, K.psum[0:N_CMP, 4 + which, h * HD:(h + 1) * HD],
                                     [x[:, which, k, h * N_CMP:(h + 1) * N_CMP] for x in K.cmp_hidT],
                                     [part[:, k, :] for part in w2], k == 0, k == 1)
            mm.then_inc(K.load_used, 1)
            pe.wait_ge(K.dve_took.sem, v0 + 3)
            for h in range(N_KV):
                tr = nc.tensor.transpose(K.psum[:, 6, h * P:h * P + N_CMP],
                                         K.cmp_k2[:, h, :, :].rearrange("p a d -> p (a d)"),
                                         K.ident[0:N_CMP, 0:N_CMP])
            tr.then_inc(K.turned.sem, 1)

        @block.scalar
        def _(act):
            for which in range(2):
                for n in range(2):
                    split_ahead(K, act, "act", first + 2 * which + n)
                act.wait_ge(K.load_used, first + 2 * which + 2)
                nc.scalar.activation(K.cmp_hid[0:nb, which, :], K.psum[0:nb, which, 0:CMP_HID],
                                     ACT.Silu).then_inc(K.act_took.sem, 1)
            split_ahead(K, act, "act", first + 4)
            act.wait_ge(K.load_used, first + 5)
            nc.scalar.activation(K.cmp_v[:, :, :], K.psum[0:N_CMP, 5, 0:N_KV * HD].rearrange(
                "p (h d) -> p h d", d=HD), ACT.Copy)

        @block.vector
        def _(dve):
            ch = Chain(dve, K.dve_step)
            for n in range(4):
                split_ahead(K, dve, "dve", first + n)
            for which in range(2):
                dve.wait_ge(K.turned.sem, t0 + which + 1)
                ps = K.psum[:, 2 + which, 0:2 * P].rearrange("p (k n) -> p k n", k=2)[:, :, 0:nb]
                ch.do(nc.vector.tensor_copy(K.cmp_hidT[0][:, which, :, :], ps))
                nc.vector.tensor_tensor(K.cmp_hidT[1][:, which, :, :], ps, K.cmp_hidT[0][:, which, :, :].bitcast(F32),
                                        ALU.subtract).then_inc(K.dve_took.sem, 1)
            split_ahead(K, dve, "dve", first + 4)
            dve.wait_ge(K.load_used, first + 5)
            k = K.cmp_k
            ch.do(nc.vector.tensor_copy(k[:, :, :], K.psum[0:N_CMP, 4, 0:N_KV * HD].rearrange(
                "p (h d) -> p h d", d=HD)))
            ch.do(nc.vector.tensor_tensor(K.cmp_sq[:, :, :], k[:, :, :], k[:, :, :], ALU.mult))
            ch.do(nc.vector.tensor_reduce(K.stat[0:N_CMP, 0, 0:N_KV], K.cmp_sq[:, :, :], AX.X, ALU.add))
            nc.vector.tensor_scalar(K.stat[0:N_CMP, 0, 2:4], K.stat[0:N_CMP, 0, 0:N_KV], 1.0 / HD, RMS_EPS, ALU.mult,
                                    ALU.add).then_inc(K.stat_ready.sem, 1)
            dve.wait_ge(K.rstd_ready.sem, rs0 + 1)
            ch.do(nc.vector.tensor_tensor(k[:, :, :], k[:, :, :], K.stat[0:N_CMP, 0, 4:6].unsqueeze(2).broadcast_to(
                [N_CMP, N_KV, HD]), ALU.mult))
            ch.do(nc.vector.tensor_tensor(k[:, :, :], k[:, :, :], K.head_gain[0:N_CMP, 5, :].unsqueeze(1).broadcast_to(
                [N_CMP, N_KV, HD]), ALU.mult))
            write_twice(K, K.cmp_k2[:, :, :, :], k[:, :, :].rearrange("p h d -> p (h d)")).then_inc(K.dve_took.sem, 1)
            dve.wait_ge(K.turned.sem, t0 + 3)
            nc.vector.tensor_copy(K.cmp_kT[:, :, :], K.psum[:, 6, 0:2 * P].rearrange(
                "p (h n) -> p h n", h=2)[:, :, 0:N_CMP])

        @block.gpsimd
        def _(pool):
            pool.wait_ge(K.stat_ready.sem, st0 + 1)
            nc.gpsimd.tensor_tensor(K.stat[0:N_CMP, 0, 4:6], K.stat[0:N_CMP, 0, 2:4], K.minus_half[0:N_CMP, 0:2],
                                    ALU.pow).then_inc(K.rstd_ready.sem, 1)
            pool.wait_ge(K.rstd_ready.sem, rs0 + 1)

    K.act_took.total += 2
    K.turned.total += 3
    K.dve_took.total += 3
    K.stat_ready.total += 1
    K.rstd_ready.total += 1
    K.next_load += 5


def stationary(xT):
    return lambda k, t: [x[:, k, t * P:(t + 1) * P] for x in xT]


def embed(K, tail, gate_bias=None, gain=None, rows={}):
    nc = K.nc
    first = K.next_load
    K.next_load += 4
    n = 2 * TT
    led = K.led
    fill0, logit0, gate0, x0 = K.filled.total, K.logits_ready.total, K.gate_ready.total, K.updated.total
    sq0, st0, rs0 = K.square_ready.total, K.stat_ready.total, K.rstd_ready.total
    K.filled.total += 2
    K.logits_ready.total += n if gate_bias is not None else 0
    K.gate_ready.total += n
    K.updated.total += n
    if gain is not None:
        K.square_ready.total += TT
        K.stat_ready.total += TT
        K.rstd_ready.total += TT

    def updated(eng, t, h):
        eng.wait_ge(K.updated.sem, x0 + TT * h + t + 1)
    follow = tail(updated) if tail else None

    def gate_product(eng, h, t):
        if t == 0:
            eng.wait_ge(K.filled.sem, fill0 + h + 1)
        else:
            eng.wait_ge(K.load_used, first + 2 * h + 2)

    with nc.Block(no_gpsimd_drain=True) as block:

        @block.sync
        def _(sp):
            load_rows(K, sp, rows)
            refill(K, sp, first, 4)

        @block.tensor
        def _(pe):
            for h in range(2):
                for half, t in tile_order(h):
                    if led and h == 0 and t == 0:
                        continue
                    m = first + 2 * h + half
                    weights_here(K, pe, m)
                    w = weight_parts(K, m)[0]
                    for k in range(KT // 2):
                        kk = half * KT // 2 + k
                        mm = product(K, K.psum[:, 2 * t + h, :], stationary(K.xT)(kk, t),
                                     [part[:, k, :] for part in w], kk == 0, kk == KT - 1)
                    if t == 1:
                        mm.then_inc(K.load_used, 1)
                    elif half == 1:
                        mm.then_inc(K.filled.sem, 1)
            if follow:
                follow.pe(pe)

        @block.scalar
        def _(act):
            if gain is not None:
                for t in range(TT):
                    nc.scalar.activation(K.hid_flat[:, t, :], K.e[:, t, :], ACT.Square,
                                         accum_out=K.stat[:, t, 4:5]).then_inc(K.square_ready.sem, 1)
            for h in range(2):
                for n in range(first + 2 * h, first + 2 * h + 2 - h):
                    split_ahead(K, act, "act", n)
                for t in range(TT):
                    s = slice(h * BANK, (h + 1) * BANK)
                    if gate_bias is None:
                        gate_product(act, h, t)
                        src = K.psum[:, 2 * t + h, :]
                    else:
                        act.wait_ge(K.logits_ready.sem, logit0 + TT * h + t + 1)
                        src = K.z[:, t, s]
                    nc.scalar.activation(K.z[:, t, s], src, ACT.Sigmoid,
                                         scale=K.rstd[:, t:t + 1] if gate_bias is None else 1.0).then_inc(
                                             K.gate_ready.sem, 1)
            if follow:
                follow.act(act, [lambda act: None, lambda act: split_ahead(K, act, "act", first + 3)])

        @block.vector
        def _(dve):
            ch = Chain(dve, K.dve_step)
            if gain is not None:
                for t in range(TT):
                    dve.wait_ge(K.square_ready.sem, sq0 + t + 1)
                    nc.vector.tensor_scalar(K.stat[:, t, 4:5], K.stat[:, t, 4:5], 1.0 / D, RMS_EPS, ALU.mult,
                                            ALU.add).then_inc(K.stat_ready.sem, 1)
            for h in range(2):
                for n in range(first + 2 * h, first + 2 * h + 2 - h):
                    split_ahead(K, dve, "dve", n)
                if gain is not None and h == 0:
                    row_here(K, dve, gain)
                    for t in range(TT):
                        dve.wait_ge(K.rstd_ready.sem, rs0 + t + 1)
                        ch.do(nc.vector.scalar_tensor_tensor(K.e[:, t, :], K.e[:, t, :], K.stat[:, t, 5:6],
                                                             K.rows[:, gain, :], ALU.mult, ALU.mult))
                s = slice(h * BANK, (h + 1) * BANK)
                if gate_bias is not None:
                    row_here(K, dve, gate_bias)
                    for t in range(TT):
                        gate_product(dve, h, t)
                        nc.vector.tensor_tensor(K.z[:, t, s], K.psum[:, 2 * t + h, :], K.rows[:, gate_bias, s],
                                                ALU.add).then_inc(K.logits_ready.sem, 1)
                for t in range(TT):
                    dve.wait_ge(K.gate_ready.sem, gate0 + TT * h + t + 1)
                    ch.do(nc.vector.tensor_tensor(K.z[:, t, s], K.z[:, t, s], K.e[:, t, s], ALU.mult))
                    nc.vector.tensor_tensor(K.x[:, t, s], K.x[:, t, s], K.z[:, t, s],
                                            ALU.add).then_inc(K.updated.sem, 1)
            if follow:
                follow.dve(dve, [lambda dve: None, lambda dve: split_ahead(K, dve, "dve", first + 3)])

        @block.gpsimd
        def _(pool):
            if gain is not None:
                for t in range(TT):
                    pool.wait_ge(K.stat_ready.sem, st0 + t + 1)
                    nc.gpsimd.tensor_tensor(K.stat[:, t, 5:6], K.stat[:, t, 4:5], K.minus_half[:, 0:1],
                                            ALU.pow).then_inc(K.rstd_ready.sem, 1)
                pool.wait_ge(K.rstd_ready.sem, rs0 + TT)
            if follow:
                follow.pool(pool)


def build(nc, a, out):
    K = Kit()
    K.nc = nc
    with ExitStack() as ctx:
        def sb(name, shape, dt=F32):
            return ctx.enter_context(nc.sbuf_tensor(name, shape, dt))

        def sem(name):
            return ctx.enter_context(nc.semaphore(name))

        K.ring = sb("ring", [P, SLOTS, SLOT])
        K.wh = sb("wh", [P, PARTS, SLOT], F32R)
        K.wl = sb("wl", [P, PARTS, SLOT], F32R)
        K.x = sb("x", [P, TT, D])
        K.xT = [sb("xT_high", [P, KT, SEQ], F32R), sb("xT_low", [P, KT, SEQ], F32R)]
        K.hidT = [sb("hidT_high", [P, 2, 4, SEQ], F32R), sb("hidT_low", [P, 2, 4, SEQ], F32R)]
        K.z = sb("z", [P, TT, D])
        K.rows = sb("rows", [P, ROWS, D])
        K.psum = ctx.enter_context(nc.psum_tensor("psum", [P, NBANK, BANK], F32))
        K.ident = sb("ident", [P, P])
        K.sel = sb("sel", [P, FOX, P])
        K.fox_bias = sb("fox_bias", [P, SEQ])
        K.ones = sb("ones", [P, SEQ])
        K.minus_half = sb("minus_half", [P, 32])
        K.causal = sb("causal", [P, SEQ])
        K.window = sb("window", [P, SEQ])
        K.causal_t = sb("causal_t", [P, 3 * P])
        K.cmp_mask = sb("cmp_mask", [P, TT, N_CMP])
        K.cmp_keep = sb("cmp_keep", [P, TT, N_CMP])
        K.inv_freq = sb("inv_freq", [P, HALF])
        K.cols = sb("cols", [P, 80])
        K.positions = sb("positions", [P, TT], I32)
        K.index = sb("index", [P, TT], I32)
        K.pos_f = sb("pos_f", [P, 2 * TT])
        K.angle = sb("angle", [P, 5, 2 * TT * HALF])
        K.cos_sin = sb("cos_sin", [P, 2, 2 * TT * HALF])
        K.rot = sb("rot", [P, 4, A_Q_HEADS, HALF])
        K.gate_bias = sb("gate_bias", [P, 3])
        K.sinks = sb("sinks", [P, A_Q_HEADS])
        K.head_gain = sb("head_gain", [P, 6, HD])
        K.stat = sb("stat", [P, TT, 6])
        K.rstd = sb("rstd", [P, TT])
        K.bn = sb("bn", [P, TT, 2, 6])
        K.bn8 = sb("bn8", [P, TT * M_HEADS, 6])
        K.mean_var = sb("mean_var", [P, TT * M_HEADS, 2])
        K.mstat = sb("mstat", [P, 5, TT * M_HEADS])
        K.u_col = sb("u_col", [P, TT * M_HEADS])
        K.exp_m = sb("exp_m", [P, TT * M_HEADS])
        K.neg_max = sb("neg_max", [P, 64])
        K.sums = sb("sums", [P, 64])
        K.recip = sb("recip", [P, 8])
        K.head_ms = sb("head_ms", [P, TT, 3, 28])
        arena = sb("arena", [P, ARENA])

        def cut(at, rows, *shape):
            n = int(np.prod(shape))
            assert at + n <= ARENA, (at, n)
            view = arena[0:rows, at:at + n]
            names = "abcd"[:len(shape)]
            return view.rearrange(f"p ({' '.join(names)}) -> p {' '.join(names)}",
                                  **dict(zip(names, shape))) if len(shape) > 1 else view

        K.hid = cut(0, P, 2, TT, 512)
        K.hid_flat = cut(0, P, TT, D)
        K.rel = cut(2048, P, TT, 512)
        K.scratch = cut(3072, P, TT, D)
        K.e = K.scratch
        K.p = cut(5120, P, TT, PLE)
        flat = [h[:, :, :, :].rearrange("p b j n -> p (b j n)") for h in K.hidT]
        K.pT = [sb("pT_high", [P, PLE // P, SEQ], F32R), sb("pT_low", [P, PLE // P, SEQ], F32R)]
        K.qk = cut(0, P, TT, D)
        K.h_raw = cut(0, P, TT, M_HEADS, M_DV + 1)
        K.o = cut(2056, P, TT, D + 8)
        K.qkT = cut(4120, P, 2 * M_HEADS, SEQ)
        K.v_ext = cut(6168, P, TT, M_HEADS, M_DV + 1)
        K.decayed = cut(8224, P, 2, 3 * P)
        z_flat = K.z[:, :, :].rearrange("p t d -> p (t d)")
        K.exponent = z_flat[:, 0:6 * P].rearrange("p (b n) -> p b n", b=2)
        K.decay = z_flat[:, 6 * P:12 * P].rearrange("p (b n) -> p b n", b=2)
        K.gates = K.rows[0:FOX, 2:4, :].rearrange("p r n -> p (r n)").rearrange("p (g n) -> p g n", g=8)
        SK = SEQ + 8
        QA_W = (A_Q_HEADS + A_KV_HEADS) * HD
        K.uq = cut(0, P, TT, QW)
        K.uq1 = cut(0, P, TT, QA_W)
        K.s_sb = cut(0, P, 3, 2, SK)
        K.probs = cut(1584, P, 3, 2, SK)
        K.probsT = cut(3168, P, 2, 512)
        K.uv = cut(4192, P, TT, VW)
        K.uv1 = cut(4192, P, TT, A_KV_HEADS * HD)
        K.attT = cut(5792, P, 16, SEQ)
        K.squares = cut(5792, P, TT, QW)
        K.group_tmp = K.rows[:, 3, 0:512]
        K.kc2 = K.z[:, :, :].rearrange("p t (h n) -> p t h n", n=SEQ)[:, :, 0:N_KV, :]
        nb = N_KV * N_CMP
        K.block_sum = K.rows[:, 2, 0:32 * nb].rearrange("p (w j n) -> p w j n", w=2, j=16)
        K.blocks = [f[:, 0:32 * nb].rearrange("p (w j n) -> p w j n", w=2, j=16) for f in flat]
        K.cmp_hidT = [f[:, 32 * nb:36 * nb].rearrange("p (w k n) -> p w k n", w=2, k=2) for f in flat]
        K.cmp_hid = cut(0, P, 2, CMP_HID)
        K.cmp_k = cut(512, N_CMP, N_KV, HD)
        K.cmp_sq = cut(640, N_CMP, N_KV, HD)
        K.cmp_k2 = cut(768, N_CMP, N_KV, 2, HD)
        K.twice = K.rows[:, 0:2, :].rearrange("p r n -> p (r n)").rearrange("p (t h a d) -> p t h a d", t=TT, a=2, d=HD)
        K.cmp_v = sb("cmp_v", [N_CMP, N_KV, HD])
        K.cmp_kT = sb("cmp_kT", [P, N_KV, N_CMP])

        K.turned = Signal(sem("turned"))
        K.act_took = Signal(sem("act_took"))
        K.dve_took = Signal(sem("dve_took"))
        K.filled = Signal(sem("filled"))
        K.hidden_ready = Signal(sem("hidden_ready"))
        K.sums_ready = Signal(sem("sums_ready"))
        K.rows_ready = Signal(sem("rows_ready"))
        K.logits_ready = Signal(sem("logits_ready"))
        K.gate_ready = Signal(sem("gate_ready"))
        K.updated = Signal(sem("updated"))
        K.high_turned = Signal(sem("high_turned"))
        K.low_turned = Signal(sem("low_turned"))
        K.act_turned = Signal(sem("act_turned"))
        K.dve_turned = Signal(sem("dve_turned"))
        K.stat_ready = Signal(sem("stat_ready"))
        K.rstd_ready = Signal(sem("rstd_ready"))
        K.square_ready = Signal(sem("square_ready"))
        K.input_turned = Signal(sem("input_turned"))
        K.input_high = Signal(sem("input_high"))
        K.input_low = Signal(sem("input_low"))
        K.dve_step = Signal(sem("dve_step"))
        K.pool_step = Signal(sem("pool_step"))
        K.angle_ready = Signal(sem("angle_ready"))
        K.gates_v = Signal(sem("gates_v"))
        K.gates_a = Signal(sem("gates_a"))
        K.scores_ready = Signal(sem("scores_ready"))
        K.scores_read = Signal(sem("scores_read"))
        K.masked_scores = Signal(sem("masked_scores"))
        K.probs_ready = Signal(sem("probs_ready"))
        K.probs_kept = Signal(sem("probs_kept"))
        K.weights_ready = Signal(sem("weights_ready"))
        K.values_ready = Signal(sem("values_ready"))
        K.group_out = Signal(sem("group_out"))
        K.slot_loaded = [sem(f"slot_loaded{i}") for i in range(SLOTS)]
        K.row_loaded = [sem(f"row_loaded{i}") for i in range(ROWS)]
        K.row_loads = [0] * ROWS
        K.high_ready = sem("high_ready")
        K.low_ready = sem("low_ready")
        K.load_used = sem("load_used")
        K.input_loaded = sem("input_loaded")
        K.small_loaded = sem("small_loaded")
        K.zeroed = sem("zeroed")
        K.masked = sem("masked")
        K.p_loaded = sem("p_loaded")
        K.stored = sem("stored")
        K.masked_total, K.p_loads, K.next_load, K.led = 0, 0, 0, False
        K.loads = plan_weights(a)

        setup(K, a)
        full = (stationary(K.xT), KT, [(0, BANK)])

        def take_mlstm(item, t, ps):
            if item in (2, 3):
                dst = K.v_ext[:, t, 2 * (item - 2):2 * (item - 1), 0:M_DV]
                ps = ps.rearrange("p (h d) -> p h d", d=M_DV)
            elif item < 2:
                dst = K.qk[:, t, item * BANK:(item + 1) * BANK]
            else:
                dst = K.o[:, t, (item - 4) * BANK:(item - 4) * BANK + ps.shape[1]]
            if item in (4, 5):
                return nc.scalar.activation(dst, ps, ACT.Sigmoid)
            return nc.scalar.activation(dst, ps, ACT.Copy) if t == 0 else nc.vector.tensor_copy(dst, ps)
        project(K, [full] * 6 + [(stationary(K.xT), KT, [(0, 8)])],
                lambda n, t: "act" if t == 0 or n in (4, 5) else "dve", take_mlstm,
                {0: a["mix_ln_g"][0], 1: a["mix_ln_b"][0]}, along=rotary_tables(K), prime=[1])
        turn(K, [([K.qk[:, t, k * P:(k + 1) * P] for t in range(TT)], K.qkT[:, k, :], None) for k in range(8)]
             + [([K.z[0:K.n_cols, 0, 0:P]], K.cols[:, 0:K.n_cols], None)])
        gate_columns(K)
        mlstm(K)
        mlstm_norm(K)
        turn_model(K, K.z, K.col_of["head_g"])
        to_ffn, to_gated, to_rest = (4, False), (4, True), (0, False)
        layer = lambda gain, shift, bias=None, lead=None: lambda ready: Tail(
            K, "layer", ready, gain, shift, bias, lead=lead)
        root = lambda col, step=None, lead=None: lambda ready: Tail(
            K, "root", ready, step=step, column=K.col_of[col], lead=lead)
        plain = lambda ready: Tail(K, "plain", ready, lead=to_rest)
        model_product(K, layer(0, 1, lead=to_ffn), a["p"][0, 0], {2: a["mlp_ln_g"][0], 3: a["mlp_ln_b"][0]})
        feed_forward(K, D_FF // 512, 512, False, layer(2, 3, lead=to_rest), True, {0: a["ple_b_gate"][0]})
        embed(K, plain, gate_bias=0, rows={1: a["kv_b"], 2: a["b_b_o"][0], 3: a["mix_ln_g"][1]})

        def take_qkv(item, t, ps):
            if item > 0:
                cols = slice((item - 1) * BANK, item * BANK)
                return nc.vector.tensor_tensor(K.uq1[:, t, cols], ps, K.rows[:, 0, cols], ALU.add)
            w = A_KV_HEADS * HD
            nc.vector.tensor_tensor(K.uq1[:, t, D:D + w], ps[:, 0:w], K.rows[:, 1, 0:w], ALU.add)
            return nc.vector.tensor_tensor(K.uv1[:, t, :], ps[:, w:2 * w], K.rows[:, 1, w:2 * w], ALU.add)
        qkv0 = K.dve_took.total

        def rotate_chunk(dve, g):
            ch = Chain(dve, K.dve_step)
            dve.wait_ge(K.dve_took.sem, qkv0 + TT * (g + 1))
            c, h = (D, A_KV_HEADS) if g == 0 else ((g - 1) * BANK, BANK // HD)
            for t in range(TT):
                rotate(K, ch, K.uq1[:, t, c:c + h * HD].rearrange("p (h d) -> p h d", d=HD), 0, t)
            if g == 2:
                for t in range(TT):
                    write_twice(K, K.twice[:, t, 0:A_KV_HEADS, :, :], K.uq1[:, t, D:D + A_KV_HEADS * HD])
        project(K, [full] * 3, lambda n, t: "dve", take_qkv, {0: a["b_b_q"][0]}, [1, 0], {"dve": rotate_chunk})
        turn(K, two_heads(K, K.uq1, 0, A_Q_HEADS, 0) + twice_heads(K, 0, A_KV_HEADS, A_Q_HEADS // 2))
        units, groups = [], []
        for g in range(A_Q_HEADS // 8):
            for t in range(TT):
                size = (t + 1) * P
                for pair in range(4):
                    h = 8 * g + 2 * pair
                    kv = h // (A_Q_HEADS // A_KV_HEADS)
                    vals = [K.uv1[:, s, kv * HD:(kv + 1) * HD] for s in range(t + 1)]
                    units.append(dict(q=halves(K, h // 2, t * P, (t + 1) * P),
                                      k=halves(K, A_Q_HEADS // 2 + kv, 0, size), size=size, bias=None, keep=None,
                                      mask=K.causal[:, P:SEQ] if t == 0 else K.window[:, :], sink=h, v=[vals] * 2))
                groups.append(divided(K, K.z[:, t, g * 512:(g + 1) * 512]))
        attend(K, units, groups, {1: a["mix_ln_b"][1]})
        turn_model(K, K.z)
        model_product(K, layer(3, 1, 2, to_ffn), a["p"][1, 0], {0: a["mlp_ln_g"][1]})
        feed_forward(K, D_FF // 512, 512, False, layer(0, 1, lead=to_rest), True, {1: a["mlp_ln_b"][1], 2: a["ple_b_gate"][1]})
        embed(K, root("ffn1", lead=to_gated), gate_bias=2)
        feed_forward(K, D_FF_2 // 256, 256, True, root("mix", 0.5, to_rest))

        def take_in2(item, t, ps):
            for buf, c0, c1, at in IN2_CHUNKS[item][2]:
                dst = (K.uq if buf == "q" else K.uv)[:, t, c0:c1]
                src = ps[:, at:at + c1 - c0]
                last = (nc.scalar.activation(dst, src, ACT.Copy, scale=K.rstd[:, t:t + 1]) if t == 0 else
                        nc.vector.tensor_scalar(dst, src, K.rstd[:, t:t + 1], None, ALU.mult))
            return last
        project(K, [(stationary(K.xT), KT, [(0, n1 - n0)]) for n0, n1, _ in IN2_CHUNKS],
                lambda n, t: "act" if t == 0 else "dve", take_in2, along=normed_heads(K))
        aQ, aKS, aKW, aQF, aKF = 0, 4, 6, 8, 12
        turn(K, [([K.uv[:, t, FL:FL + FOX] for t in range(TT)], K.gates[:, 6, :], None)]
             + two_heads(K, K.uq, QA, N_Q, aQ) + twice_heads(K, 4, N_KV, aKS)
             + twice_heads(K, 6, N_KV, aKW) + two_heads(K, K.uq, QF, FOX, aQF)
             + two_heads(K, K.uq, KF, FOX, aKF), fox_gates(K))
        compress(K)
        units, groups = [], []
        for c, kind in enumerate(("cmp", "slc", "win", "fox")):
            for t in range(TT):
                q0, q1 = t * P, (t + 1) * P
                size = (t + 1) * P
                causal = K.causal[:, P:SEQ] if t == 0 else K.causal[:, :]
                values = lambda at: [K.uv[:, s, at:at + HD] for s in range(t + 1)]
                for pair in range(4):
                    h = 2 * pair
                    kv = h // (N_Q // N_KV)
                    u = dict(q=halves(K, (aQF if kind == "fox" else aQ) + pair, q0, q1), size=size, mask=causal,
                             bias=None, keep=None, sink=None)
                    if kind == "fox":
                        u.update(k=halves(K, aKF + pair, 0, size),
                                 bias=[(K.sel[:, h + i, :], K.fox_bias[:, 0:size]) for i in range(2)],
                                 v=[values(VF + (h + i) * HD) for i in range(2)])
                    elif kind == "cmp":
                        u.update(k=[K.cmp_kT[i * HD:(i + 1) * HD, kv, :] for i in range(2)], size=N_CMP,
                                 keep=K.cmp_keep[:, t, :], mask=K.cmp_mask[:, t, :], v=[[K.cmp_v[:, kv, :]]] * 2)
                    else:
                        ak, vc = (aKS, VSL) if kind == "slc" else (aKW, VWN)
                        u.update(k=halves(K, ak + kv, 0, size), v=[values(vc + kv * HD)] * 2)
                    units.append(u)
                if kind == "fox":
                    groups.append(divided(K, K.z[:, t, 512:1024]))
                else:
                    gate = K.uv[:, t, GA:VF].rearrange("p (h c) -> p h c", c=3)
                    groups.append(divided(K, K.z[:, t, 0:512], gate=gate[:, :, c], add=c > 0))
        attend(K, units, groups)
        root_norm(K, K.z, [(0, 512), (512, 1024)], K.z)
        turn_model(K, K.z, K.col_of["out_nsa"])
        model_product(K, root("ffn2", 1.0, to_gated), a["p_2"][0, 0], {0: a["ple_norm_2"][0]})
        feed_forward(K, D_FF_2 // 256, 256, True, root("ple", 0.5, to_rest), True)
        embed(K, None, gain=0)
        store(K, out)


ARENA = 9888
ROWS = 4


def two_heads(K, src, col, heads, at):
    return [([src[:, t, col + j * P:col + (j + 1) * P] for t in range(TT)], K.attT[:, at + j, :], None)
            for j in range(heads // 2)]


def write_twice(K, dst, src):
    r, n = dst.shape[0], dst.shape[1]
    return K.nc.vector.tensor_copy(dst, src.rearrange("p (h d) -> p h d", d=HD).unsqueeze(2).broadcast_to([r, n, 2, HD]))


def twice_heads(K, first, heads, at):
    return [([K.twice[:, t, first + j, :, :].rearrange("p a d -> p (a d)") for t in range(TT)], K.attT[:, at + j, :],
             None) for j in range(heads)]


def halves(K, tile, lo, hi):
    return [K.attT[i * HD:(i + 1) * HD, tile, lo:hi] for i in range(2)]


def divided(K, dst, gate=None, add=False):
    nc = K.nc
    d = dst.rearrange("p (h d) -> p h d", d=HD)

    def run(ch, outputs, sums):
        ch.do(nc.vector.reciprocal(K.recip[:, :], sums))
        if gate is not None:
            ch.do(nc.vector.tensor_tensor(K.recip[:, :], K.recip[:, :], gate, ALU.mult))
        r = K.recip[:, :].unsqueeze(2).broadcast_to([P, 8, HD])
        if not add:
            return nc.vector.tensor_tensor(d, outputs, r, ALU.mult)
        tmp = K.group_tmp[:, :].rearrange("p (h d) -> p h d", d=HD)
        ch.do(nc.vector.tensor_tensor(tmp, outputs, r, ALU.mult))
        return nc.vector.tensor_tensor(d, d, tmp, ALU.add)
    return run


def model_product(K, tail, p=None, rows={}):
    nc = K.nc
    first = K.next_load
    K.next_load += 4
    sums0, turned0, high0, low0 = K.sums_ready.total, K.input_turned.total, K.input_high.total, K.input_low.total
    K.sums_ready.total += 1
    for signal in (K.input_turned, K.input_high, K.input_low):
        signal.total += PLE // P

    def sums(eng, t, h):
        if t == 0:
            eng.wait_ge(K.sums_ready.sem, sums0 + 1)
        else:
            eng.wait_ge(K.load_used, first + 4)
    follow = tail(sums)
    K.p_loads += 1
    with nc.Block(no_gpsimd_drain=True) as block:

        @block.sync
        def _(sp):
            sp.dma_start(K.p[:, :, :], p.rearrange("(t p) d -> p t d", p=P)).then_inc(K.p_loaded, 16)
            load_rows(K, sp, rows)
            refill(K, sp, first, 4)

        @block.tensor
        def _(pe):
            for h in range(2):
                for half, t in tile_order(h):
                    n = first + 2 * h + half
                    weights_here(K, pe, n)
                    w = weight_parts(K, n)[0]
                    for k in range(KT // 2):
                        kk = half * KT // 2 + k
                        mm = product(K, K.psum[:, 2 * t + h, :], stationary(K.xT)(kk, t),
                                     [part[:, k, :] for part in w], kk == 0, kk == KT - 1)
                    if t == 1:
                        mm.then_inc(K.load_used, 1)
                    elif h == 1 and half == 1:
                        mm.then_inc(K.sums_ready.sem, 1)
            def turn_input(pe):
                pe.wait_ge(K.p_loaded, 16 * K.p_loads)
                for k in range(PLE // P):
                    for t in range(TT):
                        tr = nc.tensor.transpose(K.psum[:, 6 + k, t * P:(t + 1) * P],
                                                 K.p[:, t, k * P:(k + 1) * P], K.ident[:, :])
                    tr.then_inc(K.input_turned.sem, 1)

            def input_taken(pe):
                pe.wait_ge(K.input_low.sem, low0 + PLE // P)
            follow.pe(pe, [turn_input, input_taken])

        @block.scalar
        def _(act):
            for n in range(first, first + 3):
                split_ahead(K, act, "act", n)

            def with_first(act):
                for k in range(PLE // P):
                    act.wait_ge(K.input_turned.sem, turned0 + k + 1)
                    nc.scalar.activation(K.pT[0][:, k, :], K.psum[:, 6 + k, 0:SEQ],
                                         ACT.Copy).then_inc(K.input_high.sem, 1)
            follow.act(act, [with_first, lambda act: split_ahead(K, act, "act", first + 3)])

        @block.vector
        def _(dve):
            for n in range(first, first + 3):
                split_ahead(K, dve, "dve", n)

            def with_first(dve):
                for k in range(PLE // P):
                    dve.wait_ge(K.input_high.sem, high0 + k + 1)
                    nc.vector.tensor_tensor(K.pT[1][:, k, :], K.psum[:, 6 + k, 0:SEQ],
                                            K.pT[0][:, k, :].bitcast(F32),
                                            ALU.subtract).then_inc(K.input_low.sem, 1)
            follow.dve(dve, [with_first, lambda dve: split_ahead(K, dve, "dve", first + 3)])

        @block.gpsimd
        def _(pool):
            follow.pool(pool)


def store(K, out):
    with K.nc.Block(no_gpsimd_drain=True) as block:

        @block.sync
        def _(sp):
            sp.dma_start(out[0].rearrange("(t p) d -> p t d", p=P), K.x[:, :, :]).then_inc(K.stored, 16)
            sp.wait_ge(K.stored, 16)



def kernel(**inputs):
    import concourse.bacc as bacc
    from concourse.bass_utils import run_bass_kernel_spmd

    nc = bacc.Bacc("TRN2", target_bir_lowering=False, num_devices=1)
    arrays, aps = {}, {}
    for name, value in inputs.items():
        v = np.ascontiguousarray(value)
        arrays[f"in_{name}"] = v
        aps[name] = nc.dram_tensor(f"in_{name}", v.shape, mybir.dt.from_np(v.dtype), kind="ExternalInput").ap()
    out = nc.dram_tensor("out", (1, SEQ, D), F32, kind="ExternalOutput").ap()
    build(nc, aps, out)
    return run_bass_kernel_spmd(nc, [arrays], core_ids=[0]).results[0]["out"]
```
